# Optimizing a Trainium2 kernel written in Bass

```python
import math
import jax, jax.numpy as jnp
from jax import lax
import numpy as np

D_MODEL = 1024
BATCH = 1
SEQ = 256
DEPTH = 2

EPS = 1e-6
MIX_WIDTH = 512
N_BRANCH = 4
RET_HEADS = 4
RET_DK = MIX_WIDTH // RET_HEADS
RET_DV = MIX_WIDTH // RET_HEADS
RET_CHUNK = 128
ROPE_BASE = 10000.0
CONV_CH = MIX_WIDTH
CONV_WIDTH = 31
GMLP_CH = MIX_WIDTH
GMLP_GROUPS = 4
GMLP_GROUP_CH = GMLP_CH // GMLP_GROUPS
GMLP_CHUNK = 128
SWA_HEADS = 8
SWA_KV_HEADS = 2
SWA_GROUP = SWA_HEADS // SWA_KV_HEADS
SWA_HEAD_DIM = MIX_WIDTH // SWA_HEADS
SWA_WINDOW = 128
SWA_BLOCK = 128
REL_BUCKETS = 32
REL_MAX_DIST = 128
D_FF = ((8 * D_MODEL + 3 * 256 - 1) // (3 * 256)) * 256
RET_COLS = 4 * MIX_WIDTH
CONV_COLS = 2 * CONV_CH
GMLP_COLS = 2 * GMLP_CH
SWA_COLS = (SWA_HEADS + 2 * SWA_KV_HEADS) * SWA_HEAD_DIM
GATE_COLS = N_BRANCH * D_MODEL
IN_COLS = RET_COLS + CONV_COLS + GMLP_COLS + SWA_COLS + GATE_COLS
IN_SPLITS = [RET_COLS, RET_COLS + CONV_COLS, RET_COLS + CONV_COLS + GMLP_COLS,
             RET_COLS + CONV_COLS + GMLP_COLS + SWA_COLS]


def rms_norm(x, g):
    xf = x.astype(jnp.float32)
    y = xf * lax.rsqrt(jnp.mean(xf * xf, axis=-1, keepdims=True) + EPS)
    return (y * g.astype(jnp.float32)).astype(x.dtype)

def layer_norm(x, g, b):
    xf = x.astype(jnp.float32)
    mu = jnp.mean(xf, axis=-1, keepdims=True)
    var = jnp.mean(jnp.square(xf - mu), axis=-1, keepdims=True)
    return (xf - mu) * lax.rsqrt(var + EPS) * g.astype(jnp.float32) + b.astype(jnp.float32)

def rotary(x, pos):
    half = x.shape[-1] // 2
    inv = ROPE_BASE ** (-jnp.arange(half, dtype=jnp.float32) / half)
    ang = pos.astype(jnp.float32)[:, None] * inv[None, :]
    cos = jnp.cos(ang)[None, :, None, :]
    sin = jnp.sin(ang)[None, :, None, :]
    x1, x2 = x[..., :half], x[..., half:]
    return jnp.concatenate([x1 * cos - x2 * sin, x1 * sin + x2 * cos], axis=-1)

def retention(za, gn_g):
    B, S, _ = za.shape
    C = RET_CHUNK
    N = S // C
    H = RET_HEADS
    qa, ka, va, ga = jnp.split(za, 4, axis=-1)
    pos = jnp.arange(S)
    q = rotary(qa.astype(jnp.float32).reshape(B, S, H, RET_DK), pos)
    k = rotary(ka.astype(jnp.float32).reshape(B, S, H, RET_DK), pos) * (RET_DK ** -0.5)
    v = va.astype(jnp.float32).reshape(B, S, H, RET_DV)
    gamma = 1.0 - 2.0 ** (-5.0 - jnp.arange(H, dtype=jnp.float32))
    log_g = jnp.log(gamma)
    idx = jnp.arange(C, dtype=jnp.float32)
    diff = idx[:, None] - idx[None, :]
    decay = jnp.where(diff >= 0, jnp.exp(log_g[:, None, None] * jnp.maximum(diff, 0.0)), 0.0)
    xi = jnp.exp(log_g[None, :] * (idx[:, None] + 1.0))
    zeta = jnp.exp(log_g[None, :] * (C - 1.0 - idx[:, None]))
    chunk_decay = jnp.exp(log_g * C)
    qc = q.reshape(B, N, C, H, RET_DK)
    kc = k.reshape(B, N, C, H, RET_DK)
    vc = v.reshape(B, N, C, H, RET_DV)
    scores = jnp.einsum('bnthd,bnshd->bnhts', qc, kc) * decay[None, None]
    y_inner = jnp.einsum('bnhts,bnshv->bnthv', scores, vc)
    kv = jnp.einsum('bnshd,bnshv->bnhdv', kc * zeta[None, None, :, :, None], vc)

    def step(state, kv_n):
        return chunk_decay[None, :, None, None] * state + kv_n, state

    state0 = jnp.zeros((B, H, RET_DK, RET_DV), jnp.float32)
    _, state_prev = lax.scan(step, state0, jnp.moveaxis(kv, 1, 0))
    state_prev = jnp.moveaxis(state_prev, 0, 1)
    y_cross = jnp.einsum('bnthd,bnhdv->bnthv', qc * xi[None, None, :, :, None], state_prev)
    y = (y_inner + y_cross).reshape(B, S, H, RET_DV)
    mu = jnp.mean(y, axis=-1, keepdims=True)
    var = jnp.mean(jnp.square(y - mu), axis=-1, keepdims=True)
    y = ((y - mu) * lax.rsqrt(var + EPS)).reshape(B, S, H * RET_DV) * gn_g.astype(jnp.float32)
    return jax.nn.silu(ga.astype(jnp.float32)) * y

def conformer_conv(zb, conv_w, conv_b, ln_g, ln_b):
    a, gate = jnp.split(zb, 2, axis=-1)
    u = (a * jax.nn.sigmoid(gate)).astype(conv_w.dtype)
    u = lax.conv_general_dilated(u, conv_w, window_strides=(1,), padding=[(CONV_WIDTH - 1, 0)],
                                 dimension_numbers=('NWC', 'WIO', 'NWC'),
                                 feature_group_count=CONV_CH)
    u = u + conv_b
    return jax.nn.silu(layer_norm(u, ln_g, ln_b))

def spatial_gating(zc, ln_g, ln_b, w_s, b_s):
    B, S, _ = zc.shape
    N = S // GMLP_CHUNK
    hc = jax.nn.gelu(zc.astype(jnp.float32))
    u, v = jnp.split(hc, 2, axis=-1)
    v = layer_norm(v, ln_g, ln_b).reshape(B, N, GMLP_CHUNK, GMLP_GROUPS, GMLP_GROUP_CH)
    mask = jnp.tril(jnp.ones((GMLP_CHUNK, GMLP_CHUNK), jnp.float32))
    ws = w_s.astype(jnp.float32) * mask[None]
    s = jnp.einsum('gts,bnsgc->bntgc', ws, v) + b_s.astype(jnp.float32).T[None, None, :, :, None]
    return u * s.reshape(B, S, GMLP_CH)

def t5_bucket(dist):
    max_exact = REL_BUCKETS // 2
    d = jnp.maximum(dist, 1).astype(jnp.float32)
    large = max_exact + (jnp.log(d / max_exact) / math.log(REL_MAX_DIST / max_exact)
                         * (REL_BUCKETS - max_exact)).astype(jnp.int32)
    large = jnp.minimum(large, REL_BUCKETS - 1)
    return jnp.where(dist < max_exact, dist, large)

def swa_attention(zd, q_g, k_g, sinks, rel_bias):
    B, S, _ = zd.shape
    Bk = SWA_BLOCK
    N = S // Bk
    d = SWA_HEAD_DIM
    qd, kd, vd = jnp.split(zd, [SWA_HEADS * d, (SWA_HEADS + SWA_KV_HEADS) * d], axis=-1)
    q = rms_norm(qd.reshape(B, S, SWA_HEADS, d), q_g).astype(jnp.float32)
    k = rms_norm(kd.reshape(B, S, SWA_KV_HEADS, d), k_g).astype(jnp.float32)
    v = vd.reshape(B, S, SWA_KV_HEADS, d).astype(jnp.float32)
    qb = q.reshape(B, N, Bk, SWA_KV_HEADS, SWA_GROUP, d)

    def band(t):
        tb = t.reshape(B, N, Bk, SWA_KV_HEADS, d)
        prev = jnp.pad(tb[:, :-1], ((0, 0), (1, 0), (0, 0), (0, 0), (0, 0)))
        return jnp.concatenate([prev, tb], axis=2)

    kb, vb = band(k), band(v)
    s = jnp.einsum('bnqhgd,bnkhd->bnhgqk', qb, kb) * (d ** -0.5)
    qi = jnp.arange(Bk)[:, None] + Bk
    kj = jnp.arange(2 * Bk)[None, :]
    dist = qi - kj
    in_win = (dist >= 0) & (dist < SWA_WINDOW)
    bias = rel_bias.astype(jnp.float32)[t5_bucket(jnp.maximum(dist, 0))]
    bias = bias.transpose(2, 0, 1).reshape(SWA_KV_HEADS, SWA_GROUP, Bk, 2 * Bk)
    valid = in_win[None] & ((jnp.arange(N)[:, None, None] > 0) | (kj[None] >= Bk))
    s = jnp.where(valid[None, :, None, None], s + bias[None, None], -jnp.inf)
    sink = sinks.astype(jnp.float32).reshape(SWA_KV_HEADS, SWA_GROUP)[None, None, :, :, None, None]
    m = jnp.maximum(jnp.max(s, axis=-1, keepdims=True), sink)
    p = jnp.exp(s - m)
    denom = jnp.sum(p, axis=-1, keepdims=True) + jnp.exp(sink - m)
    o = jnp.einsum('bnhgqk,bnkhd->bnqhgd', p / denom, vb)
    return o.reshape(B, S, SWA_HEADS * d)

def hybrid_layer(x, rel_bias, norm1_g, w_in, ret_gn_g, conv_w, conv_b, conv_ln_g, conv_ln_b,
                 gmlp_ln_g, gmlp_ln_b, gmlp_ws, gmlp_bs, swa_q_g, swa_k_g, swa_sinks,
                 w_branch, w_out, norm2_g, w_ffn_in, w_ffn_out):
    B, S, _ = x.shape
    h = rms_norm(x, norm1_g)
    z = h @ w_in
    za, zb, zc, zd, zg = jnp.split(z, IN_SPLITS, axis=-1)
    ya = retention(za, ret_gn_g)
    yb = conformer_conv(zb, conv_w, conv_b, conv_ln_g, conv_ln_b)
    yc = spatial_gating(zc, gmlp_ln_g, gmlp_ln_b, gmlp_ws, gmlp_bs)
    yd = swa_attention(zd, swa_q_g, swa_k_g, swa_sinks, rel_bias)
    ys = jnp.stack([ya, yb, yc, yd], axis=2).astype(w_branch.dtype)
    branches = jnp.einsum('bsnc,ncd->bsnd', ys, w_branch)
    gates = jax.nn.sigmoid(zg.reshape(B, S, N_BRANCH, D_MODEL))
    mix = jnp.sum(gates * branches, axis=2)
    x = x + (mix @ w_out).astype(x.dtype)
    h = rms_norm(x, norm2_g)
    gt, up = jnp.split(h @ w_ffn_in, 2, axis=-1)
    return x + ((jax.nn.silu(gt) * up) @ w_ffn_out).astype(x.dtype)

def first_inputs(seed: int = 0) -> dict:
    key = jax.random.key(seed)
    ks = jax.random.split(key, 24)
    f32 = jnp.float32
    nrm = lambda k, shape, s: jax.random.normal(k, shape, f32) * s
    L = DEPTH
    return {
        'x': nrm(ks[0], (BATCH, SEQ, D_MODEL), 1.0),
        'rel_bias': nrm(ks[1], (REL_BUCKETS, SWA_HEADS), 0.5),
        'norm1_g': 1.0 + nrm(ks[2], (L, D_MODEL), 0.02),
        'w_in': nrm(ks[3], (L, D_MODEL, IN_COLS), D_MODEL ** -0.5),
        'ret_gn_g': 1.0 + nrm(ks[4], (L, MIX_WIDTH), 0.02),
        'conv_w': nrm(ks[5], (L, CONV_WIDTH, 1, CONV_CH), CONV_WIDTH ** -0.5),
        'conv_b': nrm(ks[6], (L, CONV_CH), 0.02),
        'conv_ln_g': 1.0 + nrm(ks[7], (L, CONV_CH), 0.02),
        'conv_ln_b': nrm(ks[8], (L, CONV_CH), 0.02),
        'gmlp_ln_g': 1.0 + nrm(ks[9], (L, GMLP_CH), 0.02),
        'gmlp_ln_b': nrm(ks[10], (L, GMLP_CH), 0.02),
        'gmlp_ws': nrm(ks[11], (L, GMLP_GROUPS, GMLP_CHUNK, GMLP_CHUNK), 0.5 * GMLP_CHUNK ** -0.5),
        'gmlp_bs': 1.0 + nrm(ks[12], (L, GMLP_GROUPS, GMLP_CHUNK), 0.02),
        'swa_q_g': 1.0 + nrm(ks[13], (L, SWA_HEAD_DIM), 0.02),
        'swa_k_g': 1.0 + nrm(ks[14], (L, SWA_HEAD_DIM), 0.02),
        'swa_sinks': nrm(ks[15], (L, SWA_HEADS), 0.5),
        'w_branch': nrm(ks[16], (L, N_BRANCH, MIX_WIDTH, D_MODEL), MIX_WIDTH ** -0.5),
        'w_out': nrm(ks[17], (L, D_MODEL, D_MODEL), 0.5 * D_MODEL ** -0.5),
        'norm2_g': 1.0 + nrm(ks[18], (L, D_MODEL), 0.02),
        'w_ffn_in': nrm(ks[19], (L, D_MODEL, 2 * D_FF), D_MODEL ** -0.5),
        'w_ffn_out': nrm(ks[20], (L, D_FF, D_MODEL), 0.5 * D_FF ** -0.5),
    }

def first_block(x, rel_bias, norm1_g, w_in, ret_gn_g, conv_w, conv_b, conv_ln_g, conv_ln_b,
              gmlp_ln_g, gmlp_ln_b, gmlp_ws, gmlp_bs, swa_q_g, swa_k_g, swa_sinks,
              w_branch, w_out, norm2_g, w_ffn_in, w_ffn_out):
    for l in range(DEPTH):
        x = hybrid_layer(x, rel_bias, norm1_g[l], w_in[l], ret_gn_g[l], conv_w[l], conv_b[l],
                         conv_ln_g[l], conv_ln_b[l], gmlp_ln_g[l], gmlp_ln_b[l], gmlp_ws[l],
                         gmlp_bs[l], swa_q_g[l], swa_k_g[l], swa_sinks[l], w_branch[l],
                         w_out[l], norm2_g[l], w_ffn_in[l], w_ffn_out[l])
    return x


_first_inputs = first_inputs


def first_inputs(seed=0):
    import zlib

    import numpy as np

    out = dict(_first_inputs(seed))
    spreads = {}
    factors = {'norm1_g': 4.284,
     'ret_gn_g': 8.0,
     'conv_b': 5.477,
     'conv_ln_g': 8.0,
     'conv_ln_b': 8.0,
     'gmlp_ln_g': 8.0,
     'gmlp_ln_b': 8.0,
     'gmlp_bs': 8.0,
     'swa_q_g': 8.0,
     'swa_k_g': 8.0,
     'swa_sinks': 8.0,
     'norm2_g': 5.074}
    for name, (base, spread) in spreads.items():
        noise = np.random.default_rng([zlib.crc32(name.encode()), seed]).standard_normal(out[name].shape)
        drawn = base * np.exp(spread * noise) if base else spread * noise
        out[name] = __import__('jax').numpy.asarray(drawn.astype(out[name].dtype))
    for name, factor in factors.items():
        out[name] = (out[name] * factor).astype(out[name].dtype)
    return out


_narrow_inputs = first_inputs


def first_inputs(seed=0):

    out = dict(_narrow_inputs(seed))
    wider = {'rel_bias': 5.02,
     'conv_b': 3.74,
     'conv_ln_g': 9.51,
     'conv_ln_b': 9.82,
     'gmlp_ln_g': 6.58,
     'gmlp_ln_b': 6.82,
     'swa_sinks': 12.0}
    for name, times in wider.items():
        mean = out[name].mean()
        out[name] = (mean + times * (out[name] - mean)).astype(out[name].dtype)
    return out


N_A = DEPTH // 2
N_B = DEPTH - N_A
HEAD_DIM = 64
N_MIX_HEADS = 12
N_KV_GROUPS = 2
HEADS_PER_GROUP = N_MIX_HEADS // N_KV_GROUPS
N_MEM_HEADS = 4
N_MEM = 256
L_CMP = 32
CMP_STRIDE = 16
CMP_HIDDEN = 256
L_SEL = 64
TOP_N = 16
WINDOW = 512
Q_BLOCK = 128
D_FF_2 = 2816
CONV_WIDTH_2 = 3
ROPE_THETA = 10000.0
NEG = -1e30
FORCE_BONUS = 1e4

MIX_W = N_MIX_HEADS * HEAD_DIM
MEM_W = N_MEM_HEADS * HEAD_DIM
BRANCH_KV_W = 6 * N_KV_GROUPS * HEAD_DIM
GATE_W = 3 * N_MIX_HEADS
A_IN = MIX_W + BRANCH_KV_W + GATE_W + MEM_W
B_IN = MIX_W + MEM_W
SHARED_W = 2 * MIX_W + N_MIX_HEADS


def rms_norm_2(x, g):
    xf = x.astype(jnp.float32)
    y = xf * lax.rsqrt(jnp.mean(xf * xf, axis=-1, keepdims=True) + EPS)
    return (y * g.astype(jnp.float32)).astype(x.dtype)

def rope(x, pos):
    half = HEAD_DIM // 2
    inv = ROPE_THETA ** (-jnp.arange(half, dtype=jnp.float32) / half)
    ang = pos.astype(jnp.float32)[:, None] * inv[None, :]
    shape = (1, pos.shape[0]) + (1,) * (x.ndim - 3) + (half,)
    cos = jnp.cos(ang).reshape(shape)
    sin = jnp.sin(ang).reshape(shape)
    xf = x.astype(jnp.float32)
    x1, x2 = xf[..., :half], xf[..., half:]
    return jnp.concatenate([x1 * cos - x2 * sin, x2 * cos + x1 * sin], axis=-1).astype(x.dtype)

def masked_softmax(s, mask):
    s = jnp.where(mask, s, NEG)
    s = s - jnp.max(s, axis=-1, keepdims=True)
    e = jnp.exp(s) * mask
    return e / jnp.maximum(jnp.sum(e, axis=-1, keepdims=True), 1e-30)

def compress_blocks(u, pos_emb, w1, b1, w2, b2):
    B, S, G, dh = u.shape
    n_cmp = (S - L_CMP) // CMP_STRIDE + 1
    idx = jnp.arange(n_cmp)[:, None] * CMP_STRIDE + jnp.arange(L_CMP)[None, :]
    blocks = u[:, idx] + pos_emb[:, None, :]
    flat = blocks.transpose(0, 1, 3, 2, 4).reshape(B, n_cmp, G, L_CMP * dh)
    return jax.nn.gelu(flat @ w1 + b1) @ w2 + b2

def nsa_attention(q, kc, vc, k_slc, v_slc, k_win, v_win, gates):
    B, S, G, HG, dh = q.shape
    n_cmp = kc.shape[1]
    n_sel = S // L_SEL
    n_top = min(TOP_N, n_sel)
    n_qb = S // Q_BLOCK
    scale = HEAD_DIM ** -0.5
    cmp_start = jnp.arange(n_cmp) * CMP_STRIDE
    cmp_end = cmp_start + L_CMP - 1
    sel_start = jnp.arange(n_sel) * L_SEL
    overlap = ((cmp_start[:, None] < sel_start[None, :] + L_SEL)
               & (cmp_start[:, None] + L_CMP > sel_start[None, :])).astype(jnp.float32)
    kb = k_slc.reshape(B, n_sel, L_SEL, G, dh).transpose(0, 3, 1, 2, 4)
    vb = v_slc.reshape(B, n_sel, L_SEL, G, dh).transpose(0, 3, 1, 2, 4)
    kw_pad = jnp.pad(k_win, ((0, 0), (WINDOW, 0), (0, 0), (0, 0)))
    vw_pad = jnp.pad(v_win, ((0, 0), (WINDOW, 0), (0, 0), (0, 0)))
    bi = jnp.arange(B)[:, None, None, None]
    gi = jnp.arange(G)[None, :, None, None]
    j_sel = jnp.arange(n_sel)

    def block(args):
        c, qc, gc = args
        t = c * Q_BLOCK + jnp.arange(Q_BLOCK)
        s = jnp.einsum('btghd,bngd->bghtn', qc, kc).astype(jnp.float32) * scale
        p_cmp = masked_softmax(s, cmp_end[None, :] <= t[:, None])
        o_cmp = jnp.einsum('bghtn,bngd->btghd', p_cmp.astype(vc.dtype), vc)
        imp = jnp.einsum('bghtn,nj->bgtj', p_cmp, overlap)
        blk_t = t // L_SEL
        forced = (j_sel[None, :] == 0) | (j_sel[None, :] == blk_t[:, None]) | (j_sel[None, :] == blk_t[:, None] - 1)
        valid = j_sel[None, :] <= blk_t[:, None]
        score = jnp.where(valid, imp + FORCE_BONUS * forced.astype(jnp.float32), NEG)
        _, idx = lax.top_k(score, n_top)
        kg = kb[bi, gi, idx]
        vg = vb[bi, gi, idx]
        key_pos = idx[..., None] * L_SEL + jnp.arange(L_SEL)
        m_sel = (key_pos <= t[None, None, :, None, None]).reshape(B, G, 1, Q_BLOCK, n_top * L_SEL)
        s = jnp.einsum('btghd,bgtnld->bghtnl', qc, kg).astype(jnp.float32) * scale
        p = masked_softmax(s.reshape(B, G, HG, Q_BLOCK, n_top * L_SEL), m_sel)
        o_slc = jnp.einsum('bghtk,bgtkd->btghd', p.astype(vg.dtype),
                           vg.reshape(B, G, Q_BLOCK, n_top * L_SEL, dh))
        kw = lax.dynamic_slice_in_dim(kw_pad, c * Q_BLOCK, WINDOW + Q_BLOCK, axis=1)
        vw = lax.dynamic_slice_in_dim(vw_pad, c * Q_BLOCK, WINDOW + Q_BLOCK, axis=1)
        s_pos = c * Q_BLOCK - WINDOW + jnp.arange(WINDOW + Q_BLOCK)
        m_win = (s_pos[None, :] >= 0) & (s_pos[None, :] <= t[:, None]) & (t[:, None] - s_pos[None, :] < WINDOW)
        s = jnp.einsum('btghd,bsgd->bghts', qc, kw).astype(jnp.float32) * scale
        p = masked_softmax(s, m_win)
        o_win = jnp.einsum('bghts,bsgd->btghd', p.astype(vw.dtype), vw)
        g = gc.reshape(B, Q_BLOCK, G, HG, 3)
        return g[..., 0:1] * o_cmp + g[..., 1:2] * o_slc + g[..., 2:3] * o_win

    q_chunks = jnp.moveaxis(q.reshape(B, n_qb, Q_BLOCK, G, HG, dh), 1, 0)
    g_chunks = jnp.moveaxis(gates.reshape(B, n_qb, Q_BLOCK, N_MIX_HEADS, 3), 1, 0)
    out = lax.map(block, (jnp.arange(n_qb), q_chunks, g_chunks))
    return jnp.moveaxis(out, 0, 1).reshape(B, S, MIX_W)

def nsa_mixer(h, w_in, gate_b, cmp_pos, cmp_w1, cmp_b1, cmp_w2, cmp_b2, pos):
    B, S, _ = h.shape
    proj = h @ w_in
    q = proj[..., :MIX_W].reshape(B, S, N_MIX_HEADS, HEAD_DIM)
    kv = proj[..., MIX_W:MIX_W + BRANCH_KV_W].reshape(B, S, 6, N_KV_GROUPS, HEAD_DIM)
    gate_logit = proj[..., MIX_W + BRANCH_KV_W:MIX_W + BRANCH_KV_W + GATE_W]
    q_mem = proj[..., MIX_W + BRANCH_KV_W + GATE_W:].reshape(B, S, N_MEM_HEADS, HEAD_DIM)
    q = rope(q, pos).reshape(B, S, N_KV_GROUPS, HEADS_PER_GROUP, HEAD_DIM)
    k_cmp, v_cmp, k_slc, v_slc, k_win, v_win = (kv[:, :, i] for i in range(6))
    n_cmp = (S - L_CMP) // CMP_STRIDE + 1
    cmp_end = jnp.arange(n_cmp) * CMP_STRIDE + L_CMP - 1
    kc = rope(compress_blocks(k_cmp, cmp_pos[0], cmp_w1[0], cmp_b1[0], cmp_w2[0], cmp_b2[0]), cmp_end)
    vc = compress_blocks(v_cmp, cmp_pos[1], cmp_w1[1], cmp_b1[1], cmp_w2[1], cmp_b2[1])
    gates = jax.nn.sigmoid(gate_logit + gate_b).reshape(B, S, N_MIX_HEADS, 3)
    o = nsa_attention(q, kc, vc, rope(k_slc, pos), v_slc, rope(k_win, pos), v_win, gates)
    return o, q_mem

def forgetting_attention(q, k, v, dcum):
    B, S, H, dh = q.shape
    scale = HEAD_DIM ** -0.5
    outs = []
    for c in range(S // Q_BLOCK):
        lo, hi = c * Q_BLOCK, (c + 1) * Q_BLOCK
        t = lo + jnp.arange(Q_BLOCK)
        s = jnp.einsum('bthd,bshd->bhts', q[:, lo:hi], k[:, :hi]).astype(jnp.float32) * scale
        s = s + dcum[:, :, lo:hi, None] - dcum[:, :, None, :hi]
        p = masked_softmax(s, jnp.arange(hi)[None, :] <= t[:, None])
        outs.append(jnp.einsum('bhts,bshd->bthd', p.astype(v.dtype), v[:, :hi]))
    return jnp.concatenate(outs, axis=1).reshape(B, S, MIX_W)

def memory_attention(q_mem, mem, g_mem, w_mem_kv):
    B, M, _ = mem.shape
    kv = (rms_norm_2(mem, g_mem) @ w_mem_kv).reshape(B, M, 2, N_MEM_HEADS, HEAD_DIM)
    s = jnp.einsum('bthd,bmhd->bhtm', q_mem, kv[:, :, 0]).astype(jnp.float32) * HEAD_DIM ** -0.5
    p = jax.nn.softmax(s, axis=-1).astype(kv.dtype)
    o = jnp.einsum('bhtm,bmhd->bthd', p, kv[:, :, 1])
    return o.reshape(q_mem.shape[0], q_mem.shape[1], MEM_W)

def conv_ffn(h, w_up, conv_w, conv_b, w_down):
    u = h @ w_up
    C = u.shape[-1]
    u = lax.conv_general_dilated(u, conv_w[:, None, :], window_strides=(1,),
                                 padding=[(CONV_WIDTH_2 - 1, 0)],
                                 dimension_numbers=('NWC', 'WIO', 'NWC'),
                                 feature_group_count=C) + conv_b
    a, b = u[..., :D_FF_2], u[..., D_FF_2:]
    return (jax.nn.silu(a) * b) @ w_down

def second_inputs(seed: int = 0) -> dict:
    key = jax.random.key(seed)
    ks = jax.random.split(key, 24)
    f32 = jnp.float32
    nrm = lambda k, shape, scale: jax.random.normal(k, shape, f32) * scale
    return {
        "x": nrm(ks[0], (BATCH, SEQ, D_MODEL), 1.0),
        "mem": nrm(ks[1], (BATCH, N_MEM, D_MODEL), 1.0),
        "attn_norm": 1.0 + nrm(ks[2], (DEPTH, D_MODEL), 0.02),
        "ffn_norm": 1.0 + nrm(ks[3], (DEPTH, D_MODEL), 0.02),
        "mem_norm": 1.0 + nrm(ks[4], (DEPTH, D_MODEL), 0.02),
        "w_mem_kv": nrm(ks[5], (DEPTH, D_MODEL, 2 * MEM_W), D_MODEL ** -0.5),
        "w_o": nrm(ks[6], (DEPTH, MIX_W + MEM_W, D_MODEL), (MIX_W + MEM_W) ** -0.5),
        "w_up": nrm(ks[7], (DEPTH, D_MODEL, 2 * D_FF_2), D_MODEL ** -0.5),
        "conv_w": nrm(ks[8], (DEPTH, CONV_WIDTH_2, 2 * D_FF_2), CONV_WIDTH_2 ** -0.5),
        "conv_b": nrm(ks[9], (DEPTH, 2 * D_FF_2), 0.01),
        "w_down": nrm(ks[10], (DEPTH, D_FF_2, D_MODEL), D_FF_2 ** -0.5),
        "a_w_in": nrm(ks[11], (N_A, D_MODEL, A_IN), D_MODEL ** -0.5),
        "a_gate_b": nrm(ks[12], (N_A, GATE_W), 0.01),
        "a_cmp_pos": nrm(ks[13], (N_A, 2, L_CMP, HEAD_DIM), 0.1),
        "a_cmp_w1": nrm(ks[14], (N_A, 2, L_CMP * HEAD_DIM, CMP_HIDDEN), (L_CMP * HEAD_DIM) ** -0.5),
        "a_cmp_b1": nrm(ks[15], (N_A, 2, CMP_HIDDEN), 0.01),
        "a_cmp_w2": nrm(ks[16], (N_A, 2, CMP_HIDDEN, HEAD_DIM), CMP_HIDDEN ** -0.5),
        "a_cmp_b2": nrm(ks[17], (N_A, 2, HEAD_DIM), 0.01),
        "b_w_in": nrm(ks[18], (N_B, D_MODEL, B_IN), D_MODEL ** -0.5),
        "kv_norm": 1.0 + nrm(ks[19], (D_MODEL,), 0.02),
        "w_kv_shared": nrm(ks[20], (D_MODEL, SHARED_W), D_MODEL ** -0.5),
        "b_fgate": 3.0 + nrm(ks[21], (N_MIX_HEADS,), 0.1),
        "final_norm": 1.0 + nrm(ks[22], (D_MODEL,), 0.02),
    }

def second_block(x, mem, attn_norm, ffn_norm, mem_norm, w_mem_kv, w_o, w_up, conv_w, conv_b, w_down,
              a_w_in, a_gate_b, a_cmp_pos, a_cmp_w1, a_cmp_b1, a_cmp_w2, a_cmp_b2,
              b_w_in, kv_norm, w_kv_shared, b_fgate, final_norm):
    B, S, _ = x.shape
    pos = jnp.arange(S)
    k_sh = v_sh = dcum = None
    for l in range(DEPTH):
        h = rms_norm_2(x, attn_norm[l])
        if l < N_A:
            o_mix, q_mem = nsa_mixer(h, a_w_in[l], a_gate_b[l], a_cmp_pos[l], a_cmp_w1[l], a_cmp_b1[l],
                                     a_cmp_w2[l], a_cmp_b2[l], pos)
        else:
            if l == N_A:
                hs = rms_norm_2(x, kv_norm) @ w_kv_shared
                k_sh = hs[..., :MIX_W].reshape(B, S, N_MIX_HEADS, HEAD_DIM)
                v_sh = hs[..., MIX_W:2 * MIX_W].reshape(B, S, N_MIX_HEADS, HEAD_DIM)
                log_f = jax.nn.log_sigmoid(hs[..., 2 * MIX_W:].astype(jnp.float32) + b_fgate.astype(jnp.float32))
                dcum = jnp.cumsum(log_f, axis=1).transpose(0, 2, 1)
            proj = h @ b_w_in[l - N_A]
            q = proj[..., :MIX_W].reshape(B, S, N_MIX_HEADS, HEAD_DIM)
            q_mem = proj[..., MIX_W:].reshape(B, S, N_MEM_HEADS, HEAD_DIM)
            o_mix = forgetting_attention(q, k_sh, v_sh, dcum)
        o_mem = memory_attention(q_mem, mem, mem_norm[l], w_mem_kv[l])
        x = x + jnp.concatenate([o_mix, o_mem], axis=-1) @ w_o[l]
        x = x + conv_ffn(rms_norm_2(x, ffn_norm[l]), w_up[l], conv_w[l], conv_b[l], w_down[l])
    return rms_norm_2(x, final_norm)


def setup_inputs(seed=0):
    out = dict(first_inputs(seed))
    for name, value in second_inputs(seed + 1).items():
        if name != "x":
            out[name + "_2"] = value
    return out


def reference(
    x, rel_bias, norm1_g, w_in, ret_gn_g, conv_w, conv_b, conv_ln_g, conv_ln_b, gmlp_ln_g,
    gmlp_ln_b, gmlp_ws, gmlp_bs, swa_q_g, swa_k_g, swa_sinks, w_branch, w_out, norm2_g,
    w_ffn_in, w_ffn_out, mem_2, attn_norm_2, ffn_norm_2, mem_norm_2, w_mem_kv_2, w_o_2, w_up_2,
    conv_w_2, conv_b_2, w_down_2, a_w_in_2, a_gate_b_2, a_cmp_pos_2, a_cmp_w1_2, a_cmp_b1_2,
    a_cmp_w2_2, a_cmp_b2_2, b_w_in_2, kv_norm_2, w_kv_shared_2, b_fgate_2, final_norm_2,
):
    x = first_block(
        x, rel_bias, norm1_g, w_in, ret_gn_g, conv_w, conv_b, conv_ln_g, conv_ln_b, gmlp_ln_g,
        gmlp_ln_b, gmlp_ws, gmlp_bs, swa_q_g, swa_k_g, swa_sinks, w_branch, w_out, norm2_g,
        w_ffn_in, w_ffn_out,
    )
    return second_block(
        x, mem_2, attn_norm_2, ffn_norm_2, mem_norm_2, w_mem_kv_2, w_o_2, w_up_2, conv_w_2,
        conv_b_2, w_down_2, a_w_in_2, a_gate_b_2, a_cmp_pos_2, a_cmp_w1_2, a_cmp_b1_2,
        a_cmp_w2_2, a_cmp_b2_2, b_w_in_2, kv_norm_2, w_kv_shared_2, b_fgate_2, final_norm_2,
    )


_drawn_inputs = setup_inputs


def setup_inputs(seed=0):
    import zlib

    import numpy as np

    out = dict(_drawn_inputs(seed))
    spreads = {}
    factors = {'swa_sinks': 5.183,
     'mem_2': 8.0,
     'attn_norm_2': 8.0,
     'ffn_norm_2': 8.0,
     'mem_norm_2': 8.0,
     'w_mem_kv_2': 8.0,
     'conv_b_2': 8.0,
     'a_w_in_2': 3.767,
     'a_gate_b_2': 8.0,
     'a_cmp_pos_2': 8.0,
     'a_cmp_w1_2': 7.925,
     'a_cmp_b1_2': 26.688,
     'a_cmp_w2_2': 6.07,
     'a_cmp_b2_2': 64.0,
     'b_w_in_2': 6.371,
     'kv_norm_2': 27.069,
     'w_kv_shared_2': 3.378,
     'b_fgate_2': 200.0,
     'final_norm_2': 26.299}
    for name, (base, spread) in spreads.items():
        noise = np.random.default_rng([zlib.crc32(name.encode()), seed]).standard_normal(out[name].shape)
        drawn = base * np.exp(spread * noise) if base else spread * noise
        out[name] = __import__('jax').numpy.asarray(drawn.astype(out[name].dtype))
    for name, factor in factors.items():
        out[name] = (out[name] * factor).astype(out[name].dtype)
    return out
```

```python
import math
from contextlib import ExitStack

import numpy as np

import concourse.bass as bass
from concourse import mybir

F32 = mybir.dt.float32
ALU = mybir.AluOpType
ACT = mybir.ActivationFunctionType
AX = mybir.AxisListType

P = 128
D_MODEL = 1024
SEQ = 256
NT = SEQ // P
KT = D_MODEL // P
DEPTH = 2
EPS = 1e-6
NEG = -1e30
MIX = 512
IN_COLS = 8960
SWA_C0 = 4096
GATE_C0 = 4864
D_FF = 2816
FF_PANELS = D_FF // 256
FF_KT = D_FF // P
TRI = 3 * P
HD = 64
N_MIX = 12
N_MEM_H = 4
MIX_W = N_MIX * HD
A_IN = 1828
N_CMP = 15
CMP_PAD = 32
CMP_HID = 256
SHARED = 2 * MIX_W + N_MIX

SLOTS = 4
AHEAD = 1
SKEW = 512
PRM_LOADS = 16
SLOT_W = 2048
LOADS = 2
FILL = 16 * LOADS

R_N1, R_GN, R_CB, R_CG, R_CLB, R_BS, R_N2, R_QG, R_KG, R_END = 0, 8, 12, 16, 20, 24, 28, 36, 37, 38


PANEL_EVAC = (["AD", "AD", "AD", "AA"]
              + ["AD", "AA"]
              + ["AA", "AA"]
              + ["AD", "AD"]
              + ["AA"] * 8
              + ["DD"] * 8
              + ["DD"] * 2)
P_GATE = 10
P_BRANCH = 18
P_OUT = 26
BRANCH_ORDER = [0, 2, 3, 1]
PANEL_UNITS = [2] * 9 + [1] + [2] * 8 + [1] * 8 + [2] * 2
U_BRANCH = 35
U_OUT = 43
U_FF = 47
U_DOWN = 69
L_UNITS = 80


def taken(engine, panel):
    return sum(engine in e for e in PANEL_EVAC[:panel + 1])


PANEL2_EVAC = ["AD"] * 6 + ["DD"] * 2 + ["AD"] * 6 + ["DD"] * 2
Q_MEM, Q_OUT, Q_SHARED, Q_IN = 4, (6, 14), 8, 12
U2_CMP = 12
U2_PANEL = [0, 2, 4, 6, 8, 10, 16, 18, 53, 55, 57, 59, 61, 63, 65, 67]
U2_UP, U2_DOWN = (20, 69), (42, 91)
N2_ATT, N2_FFN, N2_MEM, N2_KV, N2_B1, N2_POS, N2_END = 0, 16, 32, 48, 56, 60, 92
NORM_ATT, NORM_MEM, NORM_FFN, NORM_FINAL = (0, 3), 1, (2, 4), 5


def taken2(engine, panel):
    return sum(engine in e for e in PANEL2_EVAC[:panel + 1])


def end_of(panel):
    return sum(PANEL_UNITS[:panel + 1])


def bucket_table():
    dist = np.clip(255 - np.arange(384), 0, 255)
    d = np.maximum(dist, 1).astype(np.float32)
    large = 16 + (np.log(d / np.float32(16)) / np.float32(math.log(8.0)) * np.float32(16)).astype(np.int32)
    bucket = np.where(dist < 16, dist, np.minimum(large, 31))
    return (np.arange(32)[:, None] == bucket[None, :]).astype(np.float32)


def angles(pos, half):
    inv = (np.float32(10000.0) ** (-np.arange(half, dtype=np.float32) / np.float32(half))).astype(np.float32)
    ang = pos.astype(np.float32)[:, None] * inv[None, :]
    c, s = np.cos(ang).astype(np.float32), np.sin(ang).astype(np.float32)
    return np.concatenate([c, c], 1), np.concatenate([-s, s], 1)


def constants():
    pos = np.arange(SEQ)
    tiles = lambda a: np.ascontiguousarray(a.reshape(NT, P, -1).transpose(1, 0, 2))
    c = {"ident": np.eye(P, dtype=np.float32)}
    c["rope_c"], c["rope_s"] = map(tiles, angles(pos, 64))
    c["rope2_c"], c["rope2_s"] = map(tiles, angles(pos, 32))
    cmp_end = np.arange(N_CMP) * 16 + 31
    c["ropec_c"], c["ropec_s"] = angles(cmp_end, 32)
    i = np.arange(P)
    s, t = i[:, None], i[None, :]
    gamma = 1.0 - 2.0 ** (-5.0 - np.arange(4))
    own = np.where(t >= s, gamma[:, None, None] ** np.maximum(t - s, 0)[None], 0.0)
    prev = gamma[:, None, None] ** (P + t - s)[None]
    c["decay"] = np.ascontiguousarray((np.concatenate([own, prev, own], 2) * P ** -0.5)
                                      .transpose(1, 0, 2)).astype(np.float32)
    c["bucket"] = bucket_table()
    dist = 255 - np.arange(384)
    c["window"] = np.tile(np.where((dist >= 0) & (dist < P), 0.0, NEG).astype(np.float32), (8, 1))
    c["upper"] = (t >= s).astype(np.float32)
    low = np.where(t <= s, 0.0, NEG).astype(np.float32)
    c["causal"] = np.concatenate([low, np.zeros((P, P), np.float32), low], 1)
    ok = tiles((cmp_end[None, :] <= pos[:, None]).astype(np.float32))
    c["cmp_ok"] = ok
    c["cmp_neg"] = np.where(ok > 0, 0.0, NEG).astype(np.float32)
    return c


class Signal:

    def __init__(self, sem, per, ahead=0):
        self.sem, self.per, self.ahead = sem, per, ahead

    def __call__(self, layer, k):
        return self.sem, layer * self.per + (k + self.ahead)


class Chain:

    def __init__(self, engine, sem):
        self.engine, self.sem, self.n = engine, sem, 0

    def link(self, ins):
        self.mark(ins)
        self.engine.wait_ge(self.sem, self.n)

    def mark(self, ins):
        self.n += 1
        ins.then_inc(self.sem, 1)
        return self.n

    def restart(self):
        self.engine.wait_ge(self.sem, self.n)
        self.engine.sem_clear(self.sem)
        self.n = 0


def build(nc, t, out):
    ctx = ExitStack()
    with ctx:
        def sb(name, shape):
            return ctx.enter_context(nc.sbuf_tensor(name, shape, F32))

        def sem(name):
            return ctx.enter_context(nc.semaphore(name))

        def sig(name, per, ahead=0):
            return Signal(sem(name), per, ahead)

        scratch = nc.dram_tensor("bias_rows", (8, P * SKEW + TRI), F32, kind="Internal").ap()

        const = {}
        for name, shape in [("ident", [P, P]), ("rope_c", [P, NT, P]), ("rope_s", [P, NT, P]),
                            ("decay", [P, 4, TRI]), ("upper", [P, P])]:
            const[name] = sb(name, shape)
        ident, decay, upper = const["ident"], const["decay"], const["upper"]
        x = sb("x", [P, NT, D_MODEL])
        h = sb("h", [P, NT, D_MODEL])
        hT = sb("hT", [P, KT, SEQ])
        ring = sb("ring", [P, SLOTS, SLOT_W])
        tmp = sb("tmp", [P, NT, D_MODEL])
        zr = sb("zr", [P, NT, 4, MIX])
        zc = sb("zc", [P, NT, 2, MIX])
        zg = sb("zg", [P, NT, 2, MIX])
        zs = sb("zs", [P, NT, 768])
        gates = sb("gates", [P, NT, 4, D_MODEL])
        gates_flat = gates[:, :, :, :].rearrange("p t n d -> p (t n d)")
        uT = gates_flat[:, 0:FF_KT * SEQ].rearrange("p (f s) -> p f s", s=SEQ)
        const["bucket"] = gates_flat[0:32, 6656:6656 + TRI]
        const["window"] = gates_flat[0:8, 7040:7040 + TRI]
        vrow = gates_flat[0:8, 7808:7808 + TRI]
        ysT = sb("ysT", [P, 4, 4, SEQ])
        mix = sb("mix", [P, NT, D_MODEL])
        qkT = zr[:, 0, 0:2, :]
        kTt = zr[:, 1, 0:2, :]
        yr = zr[:, :, 0, :]
        zr_flat = zr[:, :, :, :].rearrange("p t a b -> p (t a b)")
        swq = zr_flat[:, 0:1024].rearrange("p (c s) -> p c s", s=SEQ)
        swk = zr_flat[:, 1024:1536].rearrange("p (c s) -> p c s", s=SEQ)
        kdup = zr_flat[:, 1536:2048].rearrange("p (t c) -> p t c", t=NT)
        pT = zr_flat[:, 2048:3072].rearrange("p (a c) -> p a c", a=2)
        cacc = zr_flat[:, 3072:4096].rearrange("p (c s) -> p c s", s=SEQ)
        S = sb("S", [P, 8, TRI])
        bias = sb("bias", [P, 8, TRI])
        prm_raw = sb("prm_raw", [R_END, P])
        cw_raw = sb("cw_raw", [124, P])
        ws_raw = sb("ws_raw", [P, 4, P])
        prm = sb("prm", [P, R_END])
        cw = sb("cw", [P, 124])
        wsT = sb("wsT", [P, 4, P])
        lng = sb("lng", [P, MIX])
        lnb = sb("lnb", [P, MIX])
        sinks = sb("sinks", [P, 8])
        uTp = sb("uTp", [P, 4, 30 + SEQ])
        ss = sb("ss", [P, NT])
        ms = sb("ms", [P, NT])
        rstd = sb("rstd", [P, NT])
        half = sb("half", [P, 24])
        st = sb("st", [P, 8, 6])
        mv = sb("mv", [P, 8, 2])
        var = sb("var", [P, 24])
        rs8 = sb("rs8", [P, 24])
        ssw = sb("ssw", [P, 24])
        mx = sb("mx", [P, N_MIX, 2])
        nm = sb("nm", [P, N_MIX, 2])
        rsum = sb("rsum", [P, N_MIX, 2])
        es = sb("es", [P, N_MIX, 2])
        zc_flat = zc[:, :, :, :].rearrange("p t a b -> p (t a b)")
        sg = zc_flat[:, 0:1024].rearrange("p (a t c) -> p a t c", a=2, t=NT)
        uu = zc_flat[:, 1024:2048].rearrange("p (a t c) -> p a t c", a=2, t=NT)
        rel = sb("rel", [32, 8])
        scr = S[:, 0:4, :]
        yg = zg[:, :, 1, :]

        decay_flat = decay[:, :, :].rearrange("p a b -> p (a b)")
        c2, at = {}, 0
        for name, shape in [("causal", [P, TRI]), ("rope2_c", [P, NT, HD]), ("rope2_s", [P, NT, HD]),
                            ("cmp_ok", [P, NT, N_CMP]), ("cmp_neg", [P, NT, N_CMP]),
                            ("ropec_c", [N_CMP, HD]), ("ropec_s", [N_CMP, HD])]:
            size = shape[-1] * (shape[1] if len(shape) == 3 else 1)
            c2[name] = decay_flat[0:shape[0], at:at + size]
            if len(shape) == 3:
                c2[name] = c2[name].rearrange("p (a b) -> p a b", a=shape[1])
            at += size

        def piece(flat, start, size, pattern=None, **sizes):
            part = flat[:, start:start + size]
            return part.rearrange(pattern, **sizes) if pattern else part
        w2c = piece(decay_flat, at, 256, "p (v k c) -> p v k c", v=2, k=2)
        b2c = piece(decay_flat, at + 256, 128, "p (v c) -> p v c", v=2)
        gate_b = piece(decay_flat, at + 384, 36)
        f_b = piece(decay_flat, at + 420, N_MIX)
        S_flat = S[:, :, :].rearrange("p a b -> p (a b)")
        mem = piece(S_flat, 0, 2048, "p (t d) -> p t d", t=NT)
        final_g = piece(S_flat, 2048, D_MODEL)
        tmp_flat = tmp[:, :, :].rearrange("p t d -> p (t d)")
        prm2_raw = tmp[0:N2_END, 0, 0:P]
        cv_raw = tmp[0:44, 1, :].rearrange("p (a c) -> p a c", c=P)
        prm2 = sb("prm2", [P, N2_END])
        cvp = uTp[:, :, :].rearrange("p c s -> p (c s)")[:, 0:352].rearrange(
            "p (f k r) -> p f k r", f=2, k=4)
        z2 = piece(zr_flat, 0, NT * A_IN, "p (t c) -> p t c", t=NT)
        zk = piece(zr_flat, 0, NT * SHARED, "p (t c) -> p t c", t=NT)
        zq = piece(zc_flat, 0, 2048, "p (t c) -> p t c", t=NT)
        memT = [zg[:, :, :, :].rearrange("p t a b -> p (t a b)").rearrange("p (c s) -> p c s", s=SEQ),
                mix[:, :, :].rearrange("p t d -> p (t d)").rearrange("p (c s) -> p c s", s=SEQ)]
        hsT = memT[1]
        bias_flat = bias[:, :, :].rearrange("p a b -> p (a b)")
        mkv = [piece(bias_flat, 1024 * f, 1024, "p (t c) -> p t c", t=NT) for f in range(2)]
        mkT = [piece(bias_flat, 2048 + 512 * f, 512, "p (c s) -> p c s", s=SEQ) for f in range(2)]
        ysT_flat = ysT[:, :, :, :].rearrange("p b c s -> p (b c s)")
        qT2 = piece(ysT_flat, 0, 1536, "p (c s) -> p c s", s=SEQ)
        qmT = piece(ysT_flat, 1536, 512, "p (c s) -> p c s", s=SEQ)
        kT2 = piece(ysT_flat, 2048, 1536, "p (c s) -> p c s", s=SEQ)
        u2 = piece(zc_flat, 0, 1024, "p (c s) -> p c s", s=SEQ)
        Sc = piece(zc_flat, 1024, 768, "p (t h n) -> p t h n", t=NT, n=CMP_PAD)
        kcr = piece(gates_flat, 4128, 256, "p (g c) -> p g c", g=2)
        kvd = piece(gates_flat, 5120, 1024, "p (t c) -> p t c", t=NT)
        kd2 = piece(gates_flat, 6144, 1024, "p (t c) -> p t c", t=NT)
        kct = piece(zc_flat, 1920, 128, "p (g c) -> p g c", g=2)
        blocks = piece(tmp_flat, 0, 2048, "p (v m g n) -> p v m g n", v=2, m=16, g=2)
        S4 = piece(gates_flat, 0, 4 * 512, "p (a c) -> p a c", a=4)
        pT4 = piece(gates_flat, 2048, 2 * 512, "p (a c) -> p a c", a=2)
        pcT = piece(gates_flat, 3072, 768, "p (t a c) -> p t a c", t=NT, c=P)
        kvc = piece(gates_flat, 3840, 256, "p (v g c) -> p v g c", v=2, g=2)
        kcT = piece(gates_flat, 4096, 32, "p (g c) -> p g c", g=2)
        h1T = piece(gates_flat, 7168, 1024, "p (v k g n) -> p v k g n", v=2, k=2, g=2)
        gsig = piece(gates_flat, 4384, 72, "p (t h b) -> p t h b", t=NT, b=3)
        coef = piece(gates_flat, 4456, 24, "p (h t) -> p h t", t=NT)
        mxc = piece(gates_flat, 4480, 24, "p (t h) -> p t h", t=NT)
        smc = piece(gates_flat, 4504, 24, "p (t h) -> p t h", t=NT)
        xf = piece(gates_flat, 4528, 24, "p (t h) -> p t h", t=NT)
        ef = piece(gates_flat, 4552, 24, "p (t h) -> p t h", t=NT)
        nlf = piece(gates_flat, 4576, 24, "p (t h) -> p t h", t=NT)
        dcum = piece(gates_flat, 4600, 24, "p (t h) -> p t h", t=NT)
        upones = piece(gates_flat, 4624, SEQ)
        rsums = piece(gates_flat, 4896, 48, "p (a h t) -> p a h t", a=2, t=NT)
        zcv = piece(zc_flat, 0, 2048, "p (a t c) -> p a t c", a=2, t=NT)
        accv = piece(mix[:, :, :].rearrange("p t d -> p (t d)"), 0, 2048, "p (a c s) -> p a c s", a=2, c=4)

        G = [ctx.enter_context(nc.psum_tensor(f"G{i}", [P, 512], F32)) for i in range(4)]
        T = [ctx.enter_context(nc.psum_tensor(f"T{i}", [P, 512], F32)) for i in range(4)]

        const_in = sem("const_in")
        x_in = sem("x_in")
        rel_in = sem("rel_in")
        brow_psum, brow_ready, brow_out, bias_in = sem("brow_psum"), sem("brow_ready"), sem("brow_out"), sem("bias_in")
        half_ready = sem("half_ready")
        pad_ready = sem("pad_ready")
        out_done = sem("out_done")
        w_full = [sig(f"w_full{i}", FILL * L_UNITS // SLOTS) for i in range(SLOTS)]
        unit_done = sig("unit_done", L_UNITS)
        prm_in = sig("prm_in", 16 * PRM_LOADS)
        prm_psum, prm_ready = sig("prm_psum", 1), sig("prm_ready", 1)
        x_new, sumsq, rstd_ready, h_ready = sig("x_new", 2), sig("sumsq", 2), sig("rstd_ready", 2), sig("h_ready", 2)
        hT_psum, hT_a, hT_d = sig("hT_psum", 8), sig("hT_a", 2), sig("hT_d", 2)
        z_a = sig("z_a", taken("A", 99))
        z_d = sig("z_d", taken("D", 99))
        rot_ready, rqk_psum, qT_ready, kT_ready = sig("rot_ready", 1), sig("rqk_psum", 4), sig("qT_ready", 1), sig("kT_ready", 1)
        rsc_psum, rsc_ready, ry_psum, ry_stat = sig("rsc_psum", 4), sig("rsc_ready", 4), sig("ry_psum", 1), sig("ry_stat", 1)
        ry_rstd, rya_ready, rya_psum, ysT_ret = sig("ry_rstd", 1), sig("rya_ready", 1), sig("rya_psum", 1), sig("ysT_ret", 1)
        cu_ready, cu_psum, cuT_ready = sig("cu_ready", 1), sig("cu_psum", 1), sig("cuT_ready", 1)
        cv_ready, cv_psum, cv_stat, cv_rstd = sig("cv_ready", 1), sig("cv_psum", 1), sig("cv_stat", 1), sig("cv_rstd", 1)
        cn_ready, cn_psum, ysT_conv = sig("cn_ready", 1), sig("cn_psum", 1), sig("ysT_conv", 1)
        gv_stat, gv_rstd, gv_norm, gv_ready = sig("gv_stat", 1), sig("gv_rstd", 1), sig("gv_norm", 1), sig("gv_ready", 1)
        gs_psum, gy_ready, gy_psum, ysT_gmlp = sig("gs_psum", 1), sig("gy_ready", 1), sig("gy_psum", 1), sig("ysT_gmlp", 1)
        sw_sumsq, sw_rstd, sw_norm, sw_psum = sig("sw_sumsq", 1), sig("sw_rstd", 1), sig("sw_norm", 1), sig("sw_psum", 1)
        sw_qT, sw_kT = sig("sw_qT", 1), sig("sw_kT", 1)
        sw_sc, sw_nm, sw_exp, sw_tr, sw_pT = sig("sw_sc", 8), sig("sw_nm", 8), sig("sw_exp", 8), sig("sw_tr", 8), sig("sw_pT", 8)
        sw_o, sw_sink, sw_esink, sy_ready, sy_psum, ysT_swa = (sig("sw_o", 8), sig("sw_sink", 1), sig("sw_esink", 1),
                                                               sig("sy_ready", 1), sig("sy_psum", 1), sig("ysT_swa", 1))
        mixT_psum, mixT_a, mixT_d = sig("mixT_psum", 4), sig("mixT_a", 1), sig("mixT_d", 1)
        ff_sg, ff_u, ff_tr, ff_uT = [sig(n, FF_PANELS, AHEAD) for n in ("ff_sg", "ff_u", "ff_tr", "ff_uT")]
        ff_o = sig("ff_o", 1)
        d_chain, a_chain, g_chain = sem("d_chain"), sem("a_chain"), sem("g_chain")

        c2_in, mem_in, prm2_in, hold_d, hold_g = sem("c2_in"), sem("mem_in"), sem("prm2_in"), sem("hold_d"), sem("hold_g")
        prm2_psum, prm2_ready = sem("prm2_psum"), sem("prm2_ready")
        z2_a, z2_d = sem("z2_a"), sem("z2_d")
        kvd_ready = sem("kvd_ready")
        rot2, blocks_ready, up_ready = sem("rot2"), sem("blocks_ready"), sem("up_ready")
        cmpT_psum, u2_a, u2_d, hid_ready = sem("cmpT_psum"), sem("u2_a"), sem("u2_d"), sem("hid_ready")
        kvc_psum, kcr_ready, kcT_psum, kcT_ready = sem("kvc_psum"), sem("kcr_ready"), sem("kcT_psum"), sem("kcT_ready")
        turn_psum, turn_a, turn_d = sem("turn_psum"), sem("turn_a"), sem("turn_d")
        gate_in, gate_ready = sem("gate_in"), sem("gate_ready")
        csc_psum, csc_ready, cexp, cprob, cprobT, pcT_ready = (sem(n) for n in ("csc_psum", "csc_ready", "cexp", "cprob", "cprobT", "pcT_ready"))
        at_sc, at_nm, at_exp, at_tr, at_pT, at_o, at_sum = (sem(n) for n in ("at_sc", "at_nm", "at_exp", "at_tr", "at_pT", "at_o", "at_sum"))
        oT_psum, oT_a, oT_d = sem("oT_psum"), sem("oT_a"), sem("oT_d")
        fg_in, fg_exp, fg_ln, fg_ready, fg_cum = (sem(n) for n in ("fg_in", "fg_exp", "fg_ln", "fg_ready", "fg_cum"))
        cf_za, cf_zd, cf_tr, cf_tap, cf_cv, cf_silu, cf_uT = (sem(n) for n in ("cf_za", "cf_zd", "cf_tr", "cf_tap", "cf_cv", "cf_silu", "cf_uT"))

        JOBS = ([(0, "slc", i) for i in range(N_MIX)] + [(0, "win", i) for i in range(N_MIX)]
                + [(0, "mem", i) for i in range(N_MEM_H)]
                + [(1, "fgt", i) for i in range(N_MIX)] + [(1, "mem", i) for i in range(N_MEM_H)])
        LAST = [j for j, (f, kind, i) in enumerate(JOBS) if i == (N_MEM_H if kind == "mem" else N_MIX) - 1]

        def groups_before(j):
            return sum(j > e for e in LAST)

        block = ctx.enter_context(nc.Block())

        w_in2 = t["w_in"].rearrange("l k c -> (l k) c")
        w_br2 = t["w_branch"].rearrange("l n k c -> (l n k) c")
        w_out2 = t["w_out"].rearrange("l k c -> (l k) c")
        w_ffi2 = t["w_ffn_in"].rearrange("l k c -> (l k) c")
        w_ffo2 = t["w_ffn_out"].rearrange("l k c -> (l k) c")

        def rows(w, r0, k, c0, w_cols):
            return w[bass.ds(r0, k * P), :].rearrange("(k p) c -> p k c", p=P)[:, :, bass.ds(c0, w_cols)]

        def slot(i, k):
            return ring[:, i % SLOTS, :].rearrange("p (k c) -> p k c", k=k)

        @block.sync
        def _(sp):
            sp.dma_start(x[:, :, :], t["x"][0].rearrange("(t p) d -> p t d", p=P)).then_inc(x_in, 16)
            for name, tile in const.items():
                sp.dma_start(tile[tuple(slice(None) for _ in tile.shape)], t[name]).then_inc(const_in, 16)
            sp.dma_start(rel[:, :], t["rel_bias"]).then_inc(rel_in, 16)

            def load(layer, n, pieces):
                sp.wait_ge(*unit_done(layer, n + 1))
                for dst, src in pieces:
                    sp.dma_start(dst, src).then_inc(w_full[n % SLOTS].sem, 16)

            def split_k(n, w, r0, k, c0, w_cols):
                dst = slot(n, k) if w_cols * k == SLOT_W else ring[:, n % SLOTS, 0:k * w_cols].rearrange(
                    "p (k c) -> p k c", k=k)
                a = k // 2
                return [(dst[:, 0:a, :], rows(w, r0, a, c0, w_cols)),
                        (dst[:, a:k, :], rows(w, r0 + a * P, k - a, c0, w_cols))]

            def gate_up(n, w, r0, k0, j, half_width):
                dst = slot(n, 4).rearrange("p k (a c) -> p k a c", a=2)
                return [(dst[:, :, a, :], rows(w, r0 + k0, 4, j * 256 + a * half_width, 256)) for a in range(2)]

            with sp.Fori(0, DEPTH) as l:
                def prm_load(dst, src):
                    sp.dma_start(dst, src).then_inc(prm_in.sem, 16)

                def vec(name, r0, n):
                    prm_load(prm_raw[r0:r0 + n, :], t[name][bass.ds(l, 1), :].rearrange("a (r p) -> (a r) p", p=P))
                vec("norm1_g", R_N1, 8)
                vec("ret_gn_g", R_GN, 4)
                vec("conv_b", R_CB, 4)
                vec("conv_ln_g", R_CG, 4)
                vec("conv_ln_b", R_CLB, 4)
                vec("norm2_g", R_N2, 8)
                prm_load(prm_raw[R_BS:R_BS + 4, :], t["gmlp_bs"][bass.ds(l, 1), :, :].rearrange("a g s -> (a g) s"))
                for r, name in ((R_QG, "swa_q_g"), (R_KG, "swa_k_g")):
                    for a in range(2):
                        prm_load(prm_raw[r:r + 1, a * HD:(a + 1) * HD], t[name][bass.ds(l, 1), :])
                prm_load(cw_raw[:, :], t["conv_w"][bass.ds(l, 1), :, :, :].rearrange("a k o (c p) -> (a k o c) p", p=P))
                prm_load(ws_raw[:, :, :], t["gmlp_ws"][bass.ds(l, 1), :, :, :].rearrange("a g t s -> t (a g) s"))
                prm_load(lng[:, :], t["gmlp_ln_g"][bass.ds(l, 1), :].to_broadcast([P, MIX]))
                prm_load(lnb[:, :], t["gmlp_ln_b"][bass.ds(l, 1), :].to_broadcast([P, MIX]))
                prm_load(sinks[:, :], t["swa_sinks"][bass.ds(l, 1), :].to_broadcast([P, 8]))

                n = 0
                for c0 in [512 * p for p in range(9)] + [None] + [GATE_C0 + 512 * p for p in range(8)]:
                    if c0 is None:
                        load(l, n, split_k(n, w_in2, l * D_MODEL, 8, SWA_C0 + 512, 256))
                        n += 1
                        continue
                    for k0 in (0, 4):
                        load(l, n, split_k(n, w_in2, l * D_MODEL + k0 * P, 4, c0, 512))
                        n += 1
                for b in BRANCH_ORDER:
                    for hf in range(2):
                        load(l, n, split_k(n, w_br2, l * 4 * MIX + b * MIX, 4, hf * 512, 512))
                        n += 1
                for hf in range(2):
                    for k0 in (0, 4):
                        load(l, n, split_k(n, w_out2, l * D_MODEL + k0 * P, 4, hf * 512, 512))
                        n += 1
                assert n == U_FF

                def ff_panel(j, n, count):
                    for k0 in (0, 4):
                        m = n + k0 // 4
                        sp.wait_ge(unit_done.sem, count + k0 // 4 + 1)
                        for dst, src in gate_up(m, w_ffi2, l * D_MODEL, k0 * P, j, D_FF):
                            sp.dma_start(dst, src).then_inc(w_full[m % SLOTS].sem, 16)
                ff_panel(0, U_FF, l * L_UNITS + U_FF)
                with sp.Fori(0, FF_PANELS // 2) as i:
                    for a in (1, 2):
                        ff_panel(i * 2 + a, U_FF + 2 * a, l * L_UNITS + i * 4 + (U_FF + 2 * a))
                n = U_DOWN
                for u in range(FF_KT // 2):
                    load(l, n, split_k(n, w_ffo2, l * D_FF + u * 2 * P, 2, 0, D_MODEL))
                    n += 1
                assert n == L_UNITS
            sp.wait_ge(*unit_done(DEPTH, 1))
            for name, tile in c2.items():
                sp.dma_start(tile, t[name]).then_inc(c2_in, 16)
            sp.dma_start(w2c, t["a_cmp_w2_2"][0].rearrange("v (k p) c -> p v k c", p=P)).then_inc(c2_in, 16)
            sp.dma_start(b2c, t["a_cmp_b2_2"].rearrange("o v c -> o (v c)").to_broadcast([P, 2 * HD])
                         .rearrange("p (v c) -> p v c", v=2)).then_inc(c2_in, 16)
            sp.dma_start(gate_b, t["a_gate_b_2"].to_broadcast([P, 36])).then_inc(c2_in, 16)
            sp.dma_start(f_b, t["b_fgate_2"].unsqueeze(0).to_broadcast([P, N_MIX])).then_inc(c2_in, 16)
            sp.dma_start(final_g, t["final_norm_2"].unsqueeze(0).to_broadcast([P, D_MODEL])).then_inc(c2_in, 16)
            sp.dma_start(mem, t["mem_2"][0].rearrange("(t p) d -> p t d", p=P)).then_inc(mem_in, 16)
            for name, r0, pattern in (("attn_norm_2", N2_ATT, "l (r p) -> (l r) p"), ("ffn_norm_2", N2_FFN, "l (r p) -> (l r) p"),
                                      ("mem_norm_2", N2_MEM, "l (r p) -> (l r) p"), ("kv_norm_2", N2_KV, "(r p) -> r p"),
                                      ("a_cmp_b1_2", N2_B1, "o v (r p) -> (o v r) p")):
                src = t[name].rearrange(pattern, p=P)
                sp.dma_start(prm2_raw[r0:r0 + src.shape[0], :], src).then_inc(prm2_in, 16)
            sp.dma_start(prm2_raw[N2_POS:N2_END, :], t["a_cmp_pos_2"].rearrange("o v (m j) d -> (o v m) (j d)", j=2)).then_inc(prm2_in, 16)
            for f in range(2):
                sp.dma_start(cv_raw[:, 4 * f:4 * f + 3, :], t["conv_w_2"][f].rearrange("k (r p) -> r k p", p=P)).then_inc(prm2_in, 16)
                sp.dma_start(cv_raw[:, 4 * f + 3, :], t["conv_b_2"][f].rearrange("(r p) -> r p", p=P)).then_inc(prm2_in, 16)

            def load_panel(n, w, c0, cols, r0=0):
                for a in range(2):
                    load(DEPTH, n + a, split_k(n + a, w, r0 + a * 4 * P, 4, c0, cols))

            def load_ffn(f):
                w_up2 = t["w_up_2"][f]
                for j in range(2):
                    for a in range(2):
                        m = U2_UP[f] + 2 * j + a
                        load(DEPTH, m, gate_up(m, w_up2, 0, 4 * P * a, j, D_FF))
                with sp.Fori(0, (FF_PANELS - 3) // 2) as i:
                    for b in (2, 3):
                        for a in range(2):
                            m = U2_UP[f] + 2 * b + a
                            sp.wait_ge(unit_done.sem, DEPTH * L_UNITS + m + 1 + i * 4)
                            for dst, src in gate_up(m, w_up2, 0, 4 * P * a, i * 2 + b, D_FF):
                                sp.dma_start(dst, src).then_inc(w_full[m % SLOTS].sem, 16)
                for a in range(2):
                    m = U2_UP[f] + 20 + a
                    load(DEPTH, m, gate_up(m, w_up2, 0, 4 * P * a, 10, D_FF))
                for u in range(FF_KT // 2):
                    load(DEPTH, U2_DOWN[f] + u, split_k(U2_DOWN[f] + u, t["w_down_2"][f], u * 2 * P, 2, 0, D_MODEL))

            for q, c0 in enumerate((0, 512, 1024, 1536)):
                load_panel(U2_PANEL[q], t["a_w_in_2"][0], c0, min(512, A_IN - c0))
            for f in range(2):
                load_panel(U2_PANEL[Q_MEM + f], t["w_mem_kv_2"][f], 0, 512)
            for kv in range(2):
                for a in range(2):
                    n = U2_CMP + 2 * kv + a
                    load(DEPTH, n, split_k(n, t["a_cmp_w1_2"][0, kv], a * 8 * P, 8, 0, CMP_HID))
            for f in range(2):
                if f:
                    for q, c0 in enumerate((0, 512, 1024, 1536)):
                        load_panel(U2_PANEL[Q_SHARED + q], t["w_kv_shared_2"], c0, min(512, SHARED - c0))
                    for q in range(2):
                        load_panel(U2_PANEL[Q_IN + q], t["b_w_in_2"][0], 512 * q, 512)
                for hf in range(2):
                    load_panel(U2_PANEL[Q_OUT[f] + hf], t["w_o_2"][f], 512 * hf, 512)
                load_ffn(f)
            sp.wait_ge(*h_ready(DEPTH, NORM_FINAL + 1))
            sp.dma_start(out[0].rearrange("(t p) d -> p t d", p=P), h[:, :, :]).then_inc(out_done, 16)
            sp.wait_ge(out_done, 16)

        @block.gpsimd
        def _(g):
            ch = Chain(g, g_chain)
            nc.gpsimd.memset(half[:, :], -0.5).then_inc(half_ready, 1)
            nc.gpsimd.memset(uTp[:, :, 0:30], 0.0).then_inc(pad_ready, 1)
            g.wait_ge(brow_ready, 1)
            g.dma_start(bass.AP(scratch.tensor, scratch.offset, [[P * SKEW + TRI, 8], [SKEW + 1, P], [1, TRI]]),
                        vrow[:, :].unsqueeze(1).to_broadcast([8, P, TRI])).then_inc(brow_out, 16)
            g.wait_ge(brow_out, 16)
            for c0, off in ((0, 255), (P, 127), (2 * P, 255)):
                src = bass.AP(scratch.tensor, scratch.offset + off, [[SKEW, P], [P * SKEW + TRI, 8], [1, P]])
                g.dma_start(bias[:, :, c0:c0 + P], src).then_inc(bias_in, 16)

            def rsqrt(src, dst, n, scale, done):
                g.sem_inc(hold_g, 1)
                ch.link(nc.gpsimd.tensor_scalar(var[:, 0:n], src, scale, EPS, ALU.mult, ALU.add))
                nc.gpsimd.tensor_tensor(dst, var[:, 0:n], half[:, 0:n], ALU.pow).then_inc(done, 1)

            def norm(layer, k):
                g.wait_ge(*sumsq(layer, k + 1))
                rsqrt(ss[:, :], rstd[:, :], NT, 1.0 / D_MODEL, rstd_ready.sem)

            g.wait_ge(half_ready, 1)
            with g.Fori(0, DEPTH) as l:
                norm(l, 0)
                g.wait_ge(*ry_stat(l, 1))
                rsqrt(mv[:, :, 1], rs8[:, 0:8], 8, 1.0, ry_rstd.sem)
                g.wait_ge(*gv_stat(l, 1))
                rsqrt(mv[:, 0:2, 1], rs8[:, 0:2], 2, 1.0, gv_rstd.sem)
                g.wait_ge(*gv_norm(l, 1))
                g.wait_ge(*prm_in(l, 16 * PRM_LOADS))
                for s in range(NT):
                    ch.link(nc.gpsimd.tensor_tensor(tmp[:, s, 0:MIX], tmp[:, s, 0:MIX], lng[:, :], ALU.mult))
                    ins = nc.gpsimd.tensor_tensor(tmp[:, s, 0:MIX], tmp[:, s, 0:MIX], lnb[:, :], ALU.add)
                ins.then_inc(gv_ready.sem, 1)
                g.wait_ge(*sw_sumsq(l, 1))
                rsqrt(ssw[:, 0:20], rs8[:, 0:20], 20, 1.0 / HD, sw_rstd.sem)
                g.wait_ge(*cv_stat(l, 1))
                rsqrt(mv[:, 0:2, 1], rs8[:, 0:2], 2, 1.0, cv_rstd.sem)
                norm(l, 1)
                ch.restart()
            for k in range(NORM_FINAL + 1):
                norm(DEPTH, k)

        @block.tensor
        def _(pe):
            mm = nc.tensor.matmul
            tr = nc.tensor.transpose
            pe.wait_ge(const_in, 16 * len(const))
            pe.sem_inc(unit_done.sem, SLOTS)
            pe.sem_inc(ff_tr.sem, AHEAD)
            pe.wait_ge(rel_in, 16)
            mm(T[3][0:8, 0:TRI], rel[:, :], const["bucket"][:, :], start=True, stop=True).then_inc(brow_psum, 1)
            pe.wait_ge(brow_ready, 1)

            def turn(bank, at, src, s, c0):
                return tr(bank[:, at:at + P], src[:, s, c0:c0 + P], ident[:, :])

            def rows8(src, banks):
                for c in range(4):
                    for s in range(NT):
                        ins = turn(banks[c // 2], (c % 2) * SEQ + s * P, src, s, c * P)
                return ins

            def rows16(src, done):
                for c in range(8):
                    for s in range(NT):
                        ins = turn(T[c // 2], (c % 2) * SEQ + s * P, src, s, c * P)
                    if c % 2:
                        ins.then_inc(done, 1)

            def multiply(banks, act, k0, weights, first, last):
                for s in range(NT):
                    for kk, w in enumerate(weights):
                        ins = mm(banks[s][:, 0:w.shape[-1]], act(k0 + kk, s), w,
                                 start=first and kk == 0, stop=last and kk == len(weights) - 1)
                ins.then_inc(unit_done.sem, 1)

            def of_hT(k, s):
                return hT[:, k, s * P:(s + 1) * P]

            with pe.Fori(0, DEPTH) as l:
                def arrived(n):
                    pe.wait_ge(*w_full[n % SLOTS](l, FILL * (n // SLOTS + 1)))

                def banks_of(q):
                    if q >= 2:
                        pe.wait_ge(*z_a(l, taken("A", q - 2)))
                        pe.wait_ge(*z_d(l, taken("D", q - 2)))
                    return G[2 * (q % 2)], G[2 * (q % 2) + 1]

                def half_panel(q, a, act=of_hT):
                    n = end_of(q) - 2 + a
                    banks = banks_of(q)
                    arrived(n)
                    w = slot(n, 4)
                    multiply(banks, act, 4 * a, [w[:, k, :] for k in range(4)], a == 0, a == 1)

                def panel(q):
                    half_panel(q, 0)
                    half_panel(q, 1)

                pe.wait_ge(*prm_in(l, 16 * PRM_LOADS))
                for c in range(4):
                    tr(T[2][:, c * P:(c + 1) * P], ws_raw[:, c, :], ident[:, :])
                tr(T[1][:, 0:124], cw_raw[:, :], ident[0:124, 0:124])
                ins = tr(T[0][:, 0:R_END], prm_raw[:, :], ident[0:R_END, 0:R_END])
                ins.then_inc(prm_psum.sem, 1)
                pe.wait_ge(*prm_ready(l, 1))

                pe.wait_ge(*h_ready(l, 1))
                rows16(h, hT_psum.sem)
                pe.wait_ge(*hT_a(l, 1))
                pe.wait_ge(*hT_d(l, 1))
                for q in range(4):
                    panel(q)
                pe.wait_ge(*rot_ready(l, 1))
                rows16(h, rqk_psum.sem)
                panel(4)
                pe.wait_ge(*qT_ready(l, 1))
                pe.wait_ge(*kT_ready(l, 1))
                for i in range(4):
                    q_h, k_h = qkT[:, i // 2, (i % 2) * SEQ:(i % 2 + 1) * SEQ], kTt[:, i // 2, (i % 2) * SEQ:(i % 2 + 1) * SEQ]
                    mm(T[i][:, 0:SEQ], k_h[:, 0:P], q_h, start=True, stop=True)
                    mm(T[i][:, SEQ:TRI], k_h[:, P:SEQ], q_h[:, P:SEQ], start=True, stop=True).then_inc(rsc_psum.sem, 1)
                panel(5)
                pe.wait_ge(*rsc_ready(l, 4))
                pe.wait_ge(*z_a(l, taken("A", 2)))
                pe.wait_ge(*z_d(l, taken("D", 2)))
                for i in range(4):
                    v = [zr[:, s, 2, i * P:(i + 1) * P] for s in range(NT)]
                    cols = slice(i * P, (i + 1) * P)
                    mm(T[0][:, cols], scr[:, i, 0:P], v[0], start=True, stop=True)
                    mm(T[1][:, cols], scr[:, i, P:SEQ], v[0], start=True, stop=False)
                    ins = mm(T[1][:, cols], scr[:, i, SEQ:TRI], v[1], start=False, stop=True)
                ins.then_inc(ry_psum.sem, 1)
                panel(6)
                pe.wait_ge(*cu_ready(l, 1))
                rows8(mix, T[2:4]).then_inc(cu_psum.sem, 1)
                panel(7)
                pe.wait_ge(*rya_ready(l, 1))
                rows8(yr, T[0:2]).then_inc(rya_psum.sem, 1)
                panel(8)
                pe.wait_ge(*gv_ready(l, 1))
                pe.wait_ge(*cuT_ready(l, 1))
                for s in range(NT):
                    for c in range(4):
                        ins = mm(T[2 + s][:, c * P:(c + 1) * P], wsT[:, c, :], tmp[:, s, c * P:(c + 1) * P],
                                 start=True, stop=True)
                ins.then_inc(gs_psum.sem, 1)
                q, n = 9, end_of(9) - 1
                banks = banks_of(q)
                arrived(n)
                w = slot(n, 8)
                multiply(banks, of_hT, 0, [w[:, k, :] for k in range(8)], True, True)
                pe.wait_ge(*gy_ready(l, 1))
                rows8(yg, T[2:4]).then_inc(gy_psum.sem, 1)

                def scores(i):
                    part = slice((i % 2) * HD, (i % 2 + 1) * HD)
                    q_h, k_h = swq[part, i // 2, :], swk[part, i // 4, :]
                    if i:
                        pe.wait_ge(*sw_nm(l, i))
                    mm(T[0][:, 0:P], q_h[:, 0:P], k_h[:, 0:P], start=True, stop=True)
                    mm(T[0][:, P:TRI], q_h[:, P:SEQ], k_h, start=True, stop=True).then_inc(sw_sc.sem, 1)

                def probs_T(i):
                    pe.wait_ge(*sw_exp(l, i + 1))
                    if i:
                        pe.wait_ge(*sw_pT(l, i))
                    for c in range(3):
                        ins = tr(T[1][:, c * P:(c + 1) * P], S[:, i, c * P:(c + 1) * P], ident[:, :])
                    ins.then_inc(sw_tr.sem, 1)

                def values(i):
                    pe.wait_ge(*sw_pT(l, i + 1))
                    v = [zs[:, s, 640 + (i // 4) * HD:640 + (i // 4 + 1) * HD] for s in range(NT)]
                    cols = slice(i * HD, (i + 1) * HD)
                    p = pT[:, i % 2, :]
                    mm(T[2][:, cols], p[:, 0:P], v[0], start=True, stop=True)
                    mm(T[3][:, cols], p[:, P:SEQ], v[0], start=True, stop=False)
                    mm(T[3][:, cols], p[:, SEQ:TRI], v[1], start=False, stop=True).then_inc(sw_o.sem, 1)

                for u in range(16):
                    half_panel(P_GATE + u // 2, u % 2)
                    if u == 0:
                        pe.wait_ge(*sw_norm(l, 1))
                        pe.wait_ge(*ysT_ret(l, 1))
                        pe.wait_ge(*ysT_gmlp(l, 1))
                        rows8(tmp, T[0:2])
                        for kv in range(2):
                            for s in range(NT):
                                ins = tr(T[2][:, kv * SEQ + s * P:kv * SEQ + (s + 1) * P],
                                         kdup[:, s, kv * P:(kv + 1) * P], ident[:, :])
                        ins.then_inc(sw_psum.sem, 1)
                    if u == 1:
                        pe.wait_ge(*sw_qT(l, 1))
                        pe.wait_ge(*sw_kT(l, 1))
                    if 1 <= u <= 8:
                        scores(u - 1)
                    if 2 <= u <= 9:
                        probs_T(u - 2)
                    if 3 <= u <= 10:
                        values(u - 3)
                    if u == 12:
                        pe.wait_ge(*sy_ready(l, 1))
                        rows8(mix, T[0:2]).then_inc(sy_psum.sem, 1)
                    if u == 13:
                        pe.wait_ge(*cv_ready(l, 1))
                        for s in range(NT):
                            for c in range(4):
                                ins = tr(T[2 + s][:, c * P:(c + 1) * P], cacc[:, c, s * P:(s + 1) * P], ident[:, :])
                        ins.then_inc(cv_psum.sem, 1)

                for i, b in enumerate(BRANCH_ORDER):
                    if b == 2:
                        pe.wait_ge(*cn_ready(l, 1))
                        pe.wait_ge(*ysT_swa(l, 1))
                        rows8(h, T[0:2]).then_inc(cn_psum.sem, 1)
                    if b == 3:
                        pe.wait_ge(*ysT_swa(l, 1))
                    if b == 1:
                        pe.wait_ge(*ysT_conv(l, 1))
                    for hf in range(2):
                        q = P_BRANCH + 2 * i + hf
                        n = end_of(q) - 1
                        banks = banks_of(q)
                        arrived(n)
                        w = slot(n, 4)
                        multiply(banks, lambda k, s: ysT[:, b, k, s * P:(s + 1) * P],
                                 0, [w[:, k, :] for k in range(4)], True, True)
                pe.wait_ge(*z_d(l, taken("D", P_OUT - 1)))
                rows16(mix, mixT_psum.sem)
                pe.wait_ge(*mixT_a(l, 1))
                pe.wait_ge(*mixT_d(l, 1))
                panel(P_OUT)
                panel(P_OUT + 1)

                pe.wait_ge(*h_ready(l, 2))
                rows16(h, hT_psum.sem)
                pe.wait_ge(*hT_a(l, 2))
                pe.wait_ge(*hT_d(l, 2))

                def ff_panel(parity, n, fill, j):
                    if j is not None:
                        pe.wait_ge(ff_u.sem, j)
                    for a in range(2):
                        m = n + a
                        pe.wait_ge(w_full[m % SLOTS].sem, fill + FILL * ((n + a) // SLOTS))
                        w = slot(m, 4)
                        multiply(G[2 * parity:2 * parity + 2], of_hT, 4 * a, [w[:, k, :] for k in range(4)],
                                 a == 0, a == 1)

                def ff_turn(parity, done, free):
                    pe.wait_ge(ff_u.sem, done)
                    if free is not None:
                        pe.wait_ge(ff_uT.sem, free)
                    for c in range(2):
                        for s in range(NT):
                            ins = turn(T[parity], c * SEQ + s * P, uu[:, parity, :, :], s, c * P)
                    ins.then_inc(ff_tr.sem, 1)

                layer_fill = l * (FILL * L_UNITS // SLOTS) + FILL
                panels_before = l * FF_PANELS + AHEAD
                ff_panel(0, U_FF, layer_fill, None)
                with pe.Fori(0, FF_PANELS // 2) as i:
                    ff_panel(1, U_FF + 2, layer_fill + i * FILL, panels_before + i * 2)
                    ff_turn(0, panels_before + i * 2 + 1, panels_before + i * 2)
                    ff_panel(0, U_FF + 4, layer_fill + i * FILL, panels_before + i * 2 + 1)
                    ff_turn(1, panels_before + i * 2 + 2, panels_before + i * 2)
                ff_turn(0, panels_before + FF_PANELS, panels_before + FF_PANELS - 1)
                pe.wait_ge(*ff_u(l, FF_PANELS))
                for u in range(FF_KT // 2):
                    n = U_DOWN + u
                    if u == 0:
                        pe.wait_ge(*ff_uT(l, FF_PANELS - 1))
                    if u == FF_KT // 2 - 1:
                        pe.wait_ge(*ff_uT(l, FF_PANELS))
                    arrived(n)
                    w = slot(n, 2)
                    for s in range(NT):
                        for kk in range(2):
                            for hf in range(2):
                                k = 2 * u + kk
                                ins = mm(G[2 * s + hf][:, :], uT[:, k, s * P:(s + 1) * P],
                                         w[:, kk, hf * 512:(hf + 1) * 512], start=k == 0, stop=k == FF_KT - 1)
                    ins.then_inc(unit_done.sem, 1)

            def arrived2(n):
                pe.wait_ge(*w_full[n % SLOTS](DEPTH, FILL * (n // SLOTS + 1)))

            def unit2(n, k, cols):
                return ring[:, n % SLOTS, 0:k * cols].rearrange("p (k c) -> p k c", k=k)

            def panel2(q, src, cols=512):
                if q % 2 or q not in (Q_OUT[0], Q_SHARED, Q_OUT[1]):
                    if q >= 2:
                        pe.wait_ge(z2_a, taken2("A", q - 2))
                        pe.wait_ge(z2_d, taken2("D", q - 2))
                for a in range(2):
                    n = U2_PANEL[q] + a
                    arrived2(n)
                    w = unit2(n, 4, cols)
                    multiply(G[2 * (q % 2):2 * (q % 2) + 2], lambda k, s: src[:, k, s * P:(s + 1) * P], 4 * a,
                             [w[:, k, :] for k in range(4)], a == 0, a == 1)

            def normed(k):
                pe.wait_ge(*h_ready(DEPTH, k + 1))
                rows16(h, hT_psum.sem)

            def have_hT(k):
                pe.wait_ge(*hT_a(DEPTH, k + 1))
                pe.wait_ge(*hT_d(DEPTH, k + 1))

            def twice(cols):
                return cols.unsqueeze(1).to_broadcast([P, 2, HD])

            def turn_pair(bank, half_, src, s, c0):
                return tr(bank[:, half_ * SEQ + s * P:half_ * SEQ + (s + 1) * P], src[:, s, c0:c0 + P], ident[:, :])

            pe.wait_ge(prm2_in, 16 * 10)
            tr(T[0][:, 0:N2_END], prm2_raw, ident[0:N2_END, 0:N2_END])
            for a in range(8):
                ins = tr(T[1][:, 44 * a:44 * (a + 1)], cv_raw[:, a, :], ident[0:44, 0:44])
            ins.then_inc(prm2_psum, 1)
            pe.wait_ge(prm2_ready, 1)

            def attention(f, row_terms=None):
                jobs = [j for j, job in enumerate(JOBS) if job[0] == f]

                def scores(j):
                    _, kind, i = JOBS[j]
                    bank = T[j % 2]
                    part = slice((i % 2) * HD, (i % 2 + 1) * HD)
                    if j >= 2:
                        pe.wait_ge(at_exp if JOBS[j - 2][1] == "mem" else at_nm, j - 1)
                    if kind == "mem":
                        for s in range(NT):
                            ins = mm(bank[:, s * SEQ:(s + 1) * SEQ], qmT[part, i // 2, s * P:(s + 1) * P],
                                     mkT[f][part, i // 2, :], start=True, stop=True)
                        ins.then_inc(at_sc, 1)
                        return
                    q_h = qT2[part, i // 2, :]
                    k_h = kT2[part, {"slc": i // 6, "win": 2 + i // 6, "fgt": i // 2}[kind], :]
                    fgt = kind == "fgt"
                    mm(bank[:, 0:P], q_h[:, 0:P], k_h[:, 0:P], start=True, stop=not fgt)
                    if fgt:
                        n0, n1 = (nlf[:, s, i:i + 1].to_broadcast([P, P]) for s in range(NT))
                        mm(bank[:, 0:P], n0, upones[:, 0:P], start=False, stop=True)
                    ins = mm(bank[:, P:TRI], q_h[:, P:SEQ], k_h, start=True, stop=not fgt)
                    if fgt:
                        mm(bank[:, P:TRI], n0, upones, start=False, stop=False)
                        ins = mm(bank[:, SEQ:TRI], n1, upones[:, 0:P], start=False, stop=True)
                    ins.then_inc(at_sc, 1)

                def probs_T(j):
                    pe.wait_ge(at_exp, j + 1)
                    if j >= 2:
                        pe.wait_ge(at_pT, j - 1)
                    for c in range(4 if JOBS[j][1] == "mem" else 3):
                        ins = tr(T[2 + j % 2][:, c * P:(c + 1) * P], S4[:, j % 4, c * P:(c + 1) * P], ident[:, :])
                    ins.then_inc(at_tr, 1)

                def values(j):
                    _, kind, i = JOBS[j]
                    pe.wait_ge(at_pT, j + 1)
                    if i == 0:
                        pe.wait_ge(at_sum, groups_before(j) + 1)
                    p = pT4[:, j % 2, :]
                    if kind == "mem":
                        cols = slice(i * HD, (i + 1) * HD)
                        for s in range(NT):
                            for c in range(2):
                                ins = mm(G[2 * s][:, cols], p[:, (2 * s + c) * P:(2 * s + c + 1) * P],
                                         mkv[f][:, c, 256 + i * HD:256 + (i + 1) * HD], start=c == 0, stop=c == 1)
                        ins.then_inc(at_o, 1)
                        return
                    if kind == "fgt":
                        v_h = [zk[:, s, MIX_W + i * HD:MIX_W + (i + 1) * HD] for s in range(NT)]
                    else:
                        c0 = {"slc": 1152, "win": 1408}[kind] + (i // 6) * HD
                        v_h = [z2[:, s, c0:c0 + HD] for s in range(NT)]
                    cols = slice((i % 6) * HD, (i % 6 + 1) * HD)
                    mm(G[i // 6][:, cols], p[:, 0:P], v_h[0], start=True, stop=True)
                    mm(G[2 + i // 6][:, cols], p[:, P:SEQ], v_h[0], start=True, stop=False)
                    mm(G[2 + i // 6][:, cols], p[:, SEQ:TRI], v_h[1], start=False, stop=True).then_inc(at_o, 1)

                for step in range(len(jobs) + 2):
                    if step < len(jobs):
                        scores(jobs[step])
                    if 1 <= step <= len(jobs):
                        probs_T(jobs[step - 1])
                    if step >= 2:
                        values(jobs[step - 2])

            def out_and_ffn(f):
                pe.wait_ge(at_sum, 1 + (3 if f == 0 else 5))
                rows16(h, oT_psum)
                pe.wait_ge(oT_a, f + 1)
                pe.wait_ge(oT_d, f + 1)
                panel2(Q_OUT[f], hT)
                panel2(Q_OUT[f] + 1, hT)
                normed(NORM_FFN[f])
                have_hT(NORM_FFN[f])
                done = f * FF_PANELS

                def up(j, parity, n, count):
                    pe.wait_ge(cf_za, done + j - 1)
                    pe.wait_ge(cf_zd, done + j - 1)
                    up_units(parity, n, count)

                def up_units(parity, n, count):
                    for a in range(2):
                        m = n + a
                        pe.wait_ge(w_full[m % SLOTS].sem, count + FILL * (m // SLOTS + 1))
                        w = slot(m, 4)
                        multiply(G[2 * parity:2 * parity + 2], of_hT, 4 * a, [w[:, k, :] for k in range(4)],
                                 a == 0, a == 1)

                def channels(j, parity, first=False):
                    pe.wait_ge(cf_za, done + j + 1)
                    pe.wait_ge(cf_zd, done + j + 1)
                    if not first:
                        pe.wait_ge(cf_cv, AHEAD + done + j - 1)
                    for b in range(2):
                        for c in range(2):
                            for s in range(NT):
                                ins = turn(T[2 * parity + b], c * SEQ + s * P, zcv[:, parity, :, :], s, (2 * b + c) * P)
                        ins.then_inc(cf_tr, 1)

                base = DEPTH * FILL * L_UNITS // SLOTS
                n = U2_UP[f]
                up_units(0, n, base)
                up_units(1, n + 2, base)
                channels(0, 0, True)
                with pe.Fori(0, (FF_PANELS - 3) // 2) as i:
                    up(i * 2 + 2, 0, n + 4, base + i * FILL)
                    channels(i * 2 + 1, 1)
                    up(i * 2 + 3, 1, n + 6, base + i * FILL)
                    channels(i * 2 + 2, 0)
                up(10, 0, n + 20, base)
                channels(9, 1)
                channels(10, 0)
                for u in range(FF_KT // 2):
                    if u == 0 or u >= 8:
                        pe.wait_ge(cf_uT, done + (8 if u == 0 else u + 1))
                    n = U2_DOWN[f] + u
                    arrived2(n)
                    w = slot(n, 2)
                    for s in range(NT):
                        for kk in range(2):
                            for hf in range(2):
                                k = 2 * u + kk
                                ins = mm(G[2 * s + hf][:, :], uT[:, k, s * P:(s + 1) * P],
                                         w[:, kk, hf * 512:(hf + 1) * 512], start=k == 0, stop=k == FF_KT - 1)
                    ins.then_inc(unit_done.sem, 1)

            normed(NORM_ATT[0])
            have_hT(NORM_ATT[0])
            for q in range(2):
                panel2(q, hT)
            normed(NORM_MEM)
            panel2(2, hT)
            have_hT(NORM_MEM)
            panel2(3, hT, A_IN - 1536)
            pe.wait_ge(kvd_ready, 1)
            for kv in range(2):
                for g2 in range(2):
                    for s in range(NT):
                        ins = tr(T[kv][:, g2 * SEQ + s * P:g2 * SEQ + (s + 1) * P],
                                 kvd[:, s, (2 * kv + g2) * P:(2 * kv + g2 + 1) * P], ident[:, :])
            ins.then_inc(cmpT_psum, 1)
            panel2(Q_MEM, memT[0])
            panel2(Q_MEM + 1, memT[1])
            pe.wait_ge(blocks_ready, 1)
            for kv in range(2):
                n = U2_CMP + 2 * kv
                arrived2(n)
                arrived2(n + 1)
                for ht in range(2):
                    for m in range(16):
                        w = unit2(n + m // 8, 8, CMP_HID)
                        ins = mm(T[2][:, (2 * kv + ht) * HD:(2 * kv + ht + 1) * HD], w[:, m % 8, ht * P:(ht + 1) * P],
                                 blocks[:, kv, m, :, :], start=m == 0, stop=m == 15)
                        if ht == 1 and m % 8 == 7:
                            ins.then_inc(unit_done.sem, 1)
            pe.wait_ge(rot2, 1)
            pe.wait_ge(u2_a, 1)
            pe.wait_ge(u2_d, 1)
            for c in range(4):
                for s in range(NT):
                    ins = turn_pair(T[c // 2], c % 2, h, s, c * P)
            ins.then_inc(turn_psum, 1)
            pe.wait_ge(hid_ready, 1)
            for kv in range(2):
                for g2 in range(2):
                    for ht in range(2):
                        ins = mm(T[3][:, (2 * kv + g2) * HD:(2 * kv + g2 + 1) * HD],
                                 h1T[:, kv, ht, g2, :],
                                 w2c[:, kv, ht, :], start=ht == 0, stop=ht == 1)
            ins.then_inc(kvc_psum, 1)
            pe.wait_ge(kcr_ready, 1)
            for g2 in range(2):
                ins = tr(T[3][:, g2 * 16:g2 * 16 + N_CMP], kcr[0:N_CMP, g2, :],
                         ident[0:N_CMP, 0:N_CMP])
            ins.then_inc(kcT_psum, 1)
            for c in range(4, 6):
                for s in range(NT):
                    ins = turn_pair(T[2], c % 2, h, s, c * P)
            ins.then_inc(turn_psum, 1)
            pe.wait_ge(turn_a, 1)
            for c in range(2):
                for s in range(NT):
                    ins = turn_pair(T[1], c, z2, s, 1572 + c * P)
            ins.then_inc(turn_psum, 1)
            pe.wait_ge(kcT_ready, 1)
            for br in range(2):
                for g2 in range(2):
                    for s in range(NT):
                        c0 = (2 * br + g2) * P
                        ins = tr(T[3 * br][:, g2 * SEQ + s * P:g2 * SEQ + (s + 1) * P], kd2[:, s, c0:c0 + P], ident[:, :])
            ins.then_inc(turn_psum, 1)
            pe.wait_ge(turn_d, 1)
            pe.wait_ge(turn_a, 2)
            pe.wait_ge(z2_a, taken2("A", Q_MEM + 1))
            pe.wait_ge(z2_d, taken2("D", Q_MEM + 1))
            for f in range(2):
                for c in range(2):
                    for s in range(NT):
                        ins = turn_pair(T[2 - f], c, mkv[f], s, c * P)
            ins.then_inc(turn_psum, 1)
            pe.wait_ge(turn_a, 4)
            pe.wait_ge(turn_d, 2)
            for s in range(NT):
                for i in range(N_MIX):
                    part = slice((i % 2) * HD, (i % 2 + 1) * HD)
                    at_c = (s * 6 + i // 2) * N_CMP
                    ins = mm(T[i % 2][:, at_c:at_c + N_CMP], qT2[part, i // 2, s * P:(s + 1) * P],
                       kcT[part, i // 6, 0:N_CMP], start=True, stop=True)
            ins.then_inc(csc_psum, 1)
            pe.wait_ge(cprob, 1)
            for s in range(NT):
                for c in range(3):
                    ins = tr(T[2 + s][:, c * P:(c + 1) * P], Sc[:, s, 4 * c:4 * c + 4, :].rearrange("p h n -> p (h n)"), ident[:, :])
            ins.then_inc(cprobT, 1)
            pe.wait_ge(pcT_ready, 1)
            for s in range(NT):
                for i in range(N_MIX):
                    part = slice(32 * (i % 4), 32 * (i % 4) + N_CMP)
                    at_c = (s * 3 + i // 4) * HD
                    ins = mm(G[i % 4][:, at_c:at_c + HD], pcT[part, s, i // 4, :],
                             kvc[part, 1, i // 6, :], start=True, stop=True)
            ins.then_inc(at_o, 1)
            attention(0)
            out_and_ffn(0)

            normed(NORM_ATT[1])
            have_hT(NORM_ATT[1])
            for q in range(4):
                panel2(Q_SHARED + q, hsT, min(512, SHARED - 512 * q))
            for q in range(2):
                panel2(Q_IN + q, hT)
            pe.wait_ge(z2_a, taken2("A", Q_IN + 1))
            pe.wait_ge(z2_d, taken2("D", Q_IN + 1))
            for c in range(8):
                for s in range(NT):
                    ins = turn_pair(T[c // 2], c % 2, zq, s, c * P)
            ins.then_inc(turn_psum, 1)
            pe.wait_ge(turn_a, 5)
            pe.wait_ge(turn_d, 3)
            for c in range(6):
                for s in range(NT):
                    ins = turn_pair(T[c // 2], c % 2, zk, s, c * P)
            ins.then_inc(turn_psum, 1)
            pe.wait_ge(fg_ready, 1)
            mm(T[3][:, 0:N_MIX], upones[:, 0:P], nlf[:, 0, :], start=True, stop=True)
            mm(T[3][:, N_MIX:2 * N_MIX], upones[:, 0:P], nlf[:, 1, :], start=True, stop=False)
            mm(T[3][:, N_MIX:2 * N_MIX], upones[:, P:SEQ], nlf[:, 0, :], start=False, stop=True).then_inc(fg_cum, 1)
            pe.wait_ge(turn_a, 6)
            pe.wait_ge(turn_d, 4)
            attention(1)
            out_and_ffn(1)

        @block.scalar
        def _(act):
            def copy(dst, src, func=ACT.Copy, **more):
                return nc.scalar.activation(dst, src, func, **more)

            act.sem_inc(ff_sg.sem, AHEAD)
            act.sem_inc(ff_uT.sem, AHEAD)
            with act.Fori(0, DEPTH) as l:
                def multiplied(n):
                    act.wait_ge(*unit_done(l, SLOTS + n))

                def norm_sums(k):
                    act.wait_ge(*x_new(l, k + 1))
                    for s in range(NT):
                        ins = copy(h[:, s, :], x[:, s, :], ACT.Square, accum_out=ss[:, s:s + 1])
                    ins.then_inc(sumsq.sem, 1)

                def norm_T(k, row):
                    for c in range(4):
                        act.wait_ge(*hT_psum(l, 4 * k + c // 2 + 1))
                        ins = copy(hT[:, c, :], T[c // 2][:, (c % 2) * SEQ:(c % 2 + 1) * SEQ],
                                   scale=prm[:, row + c:row + c + 1])
                    ins.then_inc(hT_a.sem, 1)

                def take(q, dst, func=ACT.Copy, tiles=(0,), **more):
                    multiplied(end_of(q))
                    for s in tiles:
                        b = G[2 * (q % 2) + s]
                        ins = copy(dst(s), b[:, 0:dst(s).shape[-1]], func, **more)
                    ins.then_inc(z_a.sem, 1)

                norm_sums(0)
                act.wait_ge(*prm_ready(l, 1))
                norm_T(0, R_N1)
                for q in range(3):
                    take(q, lambda s: zr[:, s, q, :])
                take(3, lambda s: zr[:, s, 3, :], ACT.Silu, (0, 1))
                for b in range(2):
                    act.wait_ge(*rqk_psum(l, b + 1))
                    if b == 0:
                        act.wait_ge(*rot_ready(l, 1))
                    ins = copy(qkT[:, b, :], T[b][:, :])
                ins.then_inc(qT_ready.sem, 1)
                take(4, lambda s: zc[:, s, 0, :])
                take(5, lambda s: zc[:, s, 1, :], ACT.Tanh, (0, 1), scale=0.5)
                take(6, lambda s: zg[:, s, 0, :], ACT.Gelu_apprx_tanh, (0, 1))
                act.wait_ge(*cu_psum(l, 1))
                act.wait_ge(pad_ready, 1)
                for b in range(2):
                    ins = copy(uTp[:, 2 * b:2 * b + 2, 30:30 + SEQ],
                               T[2 + b][:, :].rearrange("p (c s) -> p c s", c=2), scale=0.5)
                ins.then_inc(cuT_ready.sem, 1)
                take(7, lambda s: zg[:, s, 1, :], ACT.Gelu_apprx_tanh, (0, 1))
                act.wait_ge(*rya_psum(l, 1))
                for c in range(4):
                    ins = copy(ysT[:, 0, c, :], T[c // 2][:, (c % 2) * SEQ:(c % 2 + 1) * SEQ],
                               scale=prm[:, R_GN + c:R_GN + c + 1])
                ins.then_inc(ysT_ret.sem, 1)
                take(8, lambda s: zs[:, s, 0:512])
                take(9, lambda s: zs[:, s, 512:768])
                act.wait_ge(*gy_psum(l, 1))
                for b in range(2):
                    ins = copy(ysT[:, 2, 2 * b:2 * b + 2, :], T[2 + b][:, :].rearrange("p (c s) -> p c s", c=2))
                ins.then_inc(ysT_gmlp.sem, 1)

                for u in range(16):
                    if u % 2:
                        i = u // 2
                        take(P_GATE + i, lambda s: gates[:, s, i // 2, (i % 2) * 512:(i % 2 + 1) * 512],
                             ACT.Tanh, (0, 1), scale=0.5)
                    if u == 0:
                        act.wait_ge(*sw_psum(l, 1))
                        copy(swk[:, :, :], T[2][:, :].rearrange("p (c s) -> p c s", c=2),
                             scale=prm[:, R_KG:R_KG + 1]).then_inc(sw_kT.sem, 1)
                    if 1 <= u <= 8:
                        i = u - 1
                        act.wait_ge(*sw_nm(l, i + 1))
                        copy(S[:, i, 0:P], S[:, i, 0:P], ACT.Exp, bias=nm[:, i, 0:1], accum_out=rsum[:, i, 0:1])
                        copy(S[:, i, P:TRI], S[:, i, P:TRI], ACT.Exp, bias=nm[:, i, 1:2],
                             accum_out=rsum[:, i, 1:2]).then_inc(sw_exp.sem, 1)
                    if 2 <= u <= 9:
                        i = u - 2
                        act.wait_ge(*sw_tr(l, i + 1))
                        if i >= 2:
                            act.wait_ge(*sw_o(l, i - 1))
                        copy(pT[:, i % 2, 0:TRI], T[1][:, 0:TRI]).then_inc(sw_pT.sem, 1)
                    if u == 10:
                        act.wait_ge(*sw_sink(l, 1))
                        copy(es[:, 0:8, :], es[:, 0:8, :], ACT.Exp).then_inc(sw_esink.sem, 1)
                    if u == 12:
                        act.wait_ge(*sy_psum(l, 1))
                        for b in range(2):
                            ins = copy(ysT[:, 3, 2 * b:2 * b + 2, :], T[b][:, :].rearrange("p (c s) -> p c s", c=2))
                        ins.then_inc(ysT_swa.sem, 1)
                act.wait_ge(*cn_psum(l, 1))
                for c in range(4):
                    ins = copy(ysT[:, 1, c, :], T[c // 2][:, (c % 2) * SEQ:(c % 2 + 1) * SEQ], ACT.Silu,
                               scale=prm[:, R_CG + c:R_CG + c + 1], bias=prm[:, R_CLB + c:R_CLB + c + 1])
                ins.then_inc(ysT_conv.sem, 1)
                for b in range(2):
                    act.wait_ge(*mixT_psum(l, b + 1))
                    ins = copy(hT[:, 2 * b:2 * b + 2, :], T[b][:, :].rearrange("p (c s) -> p c s", c=2), scale=0.5)
                ins.then_inc(mixT_a.sem, 1)
                norm_sums(1)
                norm_T(1, R_N2)

                def ff_silu(parity, units, free):
                    act.wait_ge(unit_done.sem, units)
                    if free is not None:
                        act.wait_ge(ff_u.sem, free)
                    for s in range(NT):
                        ins = copy(sg[:, parity, s, :], G[2 * parity + s][:, 0:256], ACT.Silu)
                    ins.then_inc(ff_sg.sem, 1)

                def ff_take(parity, done, j):
                    act.wait_ge(ff_tr.sem, done)
                    copy(uT[:, bass.ds(j * 2, 2), :], T[parity][:, :].rearrange("p (c s) -> p c s", c=2)
                         ).then_inc(ff_uT.sem, 1)

                units = l * L_UNITS + (SLOTS + U_FF)
                before = l * FF_PANELS + AHEAD
                ff_silu(0, units + 2, None)
                with act.Fori(0, FF_PANELS // 2) as i:
                    ff_silu(1, units + i * 4 + 4, before + i * 2)
                    ff_take(0, before + i * 2 + 1, i * 2)
                    ff_silu(0, units + i * 4 + 6, before + i * 2 + 1)
                    ff_take(1, before + i * 2 + 2, i * 2 + 1)
                ff_take(0, before + FF_PANELS, FF_PANELS - 1)

            def norm_sums2(k, src, new):
                if new:
                    act.wait_ge(*x_new(DEPTH, new))
                else:
                    act.wait_ge(mem_in, 16)
                    act.wait_ge(*h_ready(DEPTH, k))
                    act.wait_ge(*hT_psum(DEPTH, 4 * k))
                for s in range(NT):
                    ins = copy(h[:, s, :], src[:, s, :], ACT.Square, accum_out=ss[:, s:s + 1])
                ins.then_inc(sumsq.sem, 1)

            def norm_T2(k, outs):
                for c in range(4):
                    act.wait_ge(*hT_psum(DEPTH, 4 * k + c // 2 + 1))
                    for dst, row in outs:
                        ins = copy(dst[:, c, :], T[c // 2][:, (c % 2) * SEQ:(c % 2 + 1) * SEQ],
                                   scale=prm2[:, row + c:row + c + 1])
                ins.then_inc(hT_a.sem, 1)

            def take2(q, dst):
                act.wait_ge(*unit_done(DEPTH, SLOTS + U2_PANEL[q] + 2))
                copy(dst, G[2 * (q % 2)][:, 0:dst.shape[-1]]).then_inc(z2_a, 1)

            def pairs(bank):
                return bank[:, :].rearrange("p (c s) -> p c s", s=SEQ)

            def attention_a(f):
                for j, (layer, kind, i) in enumerate(JOBS):
                    if layer != f:
                        continue
                    rs = rsums[:, groups_before(j) % 2]
                    act.wait_ge(at_nm, j + 1)
                    if j >= 4:
                        act.wait_ge(at_tr, j - 3)
                    if kind == "mem":
                        bank = T[j % 2]
                        copy(S4[:, j % 4, 0:SEQ], bank[:, 0:SEQ], ACT.Exp, bias=nm[:, i, 0:1], accum_out=rs[:, i, 0:1])
                        copy(S4[:, j % 4, SEQ:512], bank[:, SEQ:512], ACT.Exp, bias=nm[:, i, 1:2],
                             accum_out=rs[:, i, 1:2]).then_inc(at_exp, 1)
                        continue
                    p = S4[:, j % 4, :]
                    copy(p[:, 0:P], p[:, 0:P], ACT.Exp, bias=nm[:, i, 0:1], accum_out=rs[:, i, 0:1])
                    copy(p[:, P:TRI], p[:, P:TRI], ACT.Exp, bias=nm[:, i, 1:2],
                         accum_out=rs[:, i, 1:2]).then_inc(at_exp, 1)

            def out_and_ffn_a(f):
                for b in range(2):
                    act.wait_ge(oT_psum, 4 * f + b + 1)
                    ins = copy(hT[:, 2 * b:2 * b + 2, :], pairs(T[b]))
                ins.then_inc(oT_a, 1)
                norm_sums2(NORM_FFN[f], x, 2 + 2 * f)
                norm_T2(NORM_FFN[f], [(hT, N2_FFN + 8 * f)])
                done = f * FF_PANELS
                units = DEPTH * L_UNITS + SLOTS + U2_UP[f]

                def take_up(j, parity, first=False):
                    act.wait_ge(unit_done.sem, units + 2 + j * 2)
                    if not first:
                        act.wait_ge(cf_tr, 2 * done + j * 2 - 2)
                    copy(zcv[:, parity, 0, :], G[2 * parity][:, :]).then_inc(cf_za, 1)

                def tap(j, parity, first=False):
                    if not first:
                        act.wait_ge(cf_uT, done + j - 1)
                    for b in range(2):
                        act.wait_ge(cf_tr, 2 * done + j * 2 + 1 + b)
                        for c in range(2):
                            tile = 22 * b + j * 2 + c
                            ins = copy(accv[:, parity, 2 * b + c, :], T[2 * parity + b][:, c * SEQ:(c + 1) * SEQ], ACT.Identity,
                                       scale=cvp[:, f, 2, bass.ds(tile, 1)], bias=cvp[:, f, 3, bass.ds(tile, 1)])
                        ins.then_inc(cf_tap, 1)

                def silu(j, parity):
                    act.wait_ge(cf_cv, AHEAD + done + j + 1)
                    copy(accv[:, parity, 0:2, :], accv[:, parity, 0:2, :], ACT.Silu).then_inc(cf_silu, 1)

                take_up(0, 0, True)
                take_up(1, 1, True)
                tap(0, 0, True)
                take_up(2, 0)
                tap(1, 1, True)
                silu(0, 0)
                with act.Fori(0, (FF_PANELS - 3) // 2) as i:
                    take_up(i * 2 + 3, 1)
                    tap(i * 2 + 2, 0)
                    silu(i * 2 + 1, 1)
                    take_up(i * 2 + 4, 0)
                    tap(i * 2 + 3, 1)
                    silu(i * 2 + 2, 0)
                tap(10, 0)
                silu(9, 1)
                silu(10, 0)

            norm_sums2(NORM_ATT[0], x, 1)
            act.wait_ge(prm2_ready, 1)
            norm_T2(NORM_ATT[0], [(hT, N2_ATT)])
            norm_sums2(NORM_MEM, mem, None)
            for q in range(2):
                take2(q, z2[:, 0, 512 * q:512 * (q + 1)])
            norm_T2(NORM_MEM, [(memT[0], N2_MEM), (memT[1], N2_MEM + 8)])
            take2(2, z2[:, 0, 1024:1536])
            take2(3, z2[:, 0, 1536:A_IN])
            act.wait_ge(cmpT_psum, 1)
            copy(u2[0:HD, 0:2, :], pairs(T[0])[0:HD])
            copy(u2[HD:P, 0:2, 0:SEQ - 1], pairs(T[0])[HD:P, :, 1:SEQ]).then_inc(u2_a, 1)
            take2(Q_MEM, mkv[0][:, 0, :])
            take2(Q_MEM + 1, mkv[1][:, 0, :])
            act.wait_ge(gate_in, 1)
            copy(gsig, gsig, ACT.Sigmoid).then_inc(gate_ready, 1)
            act.wait_ge(*unit_done(DEPTH, SLOTS + U2_CMP + 4))
            for kv in range(2):
                for ht in range(2):
                    ins = copy(h1T[:, kv, ht, :, :].rearrange("p g (a n) -> p g a n", a=4),
                               T[2][:, (2 * kv + ht) * HD:(2 * kv + ht + 1) * HD].rearrange("p (g n) -> p g n", g=2)
                               .unsqueeze(2).to_broadcast([P, 2, 4, CMP_PAD]), ACT.Gelu_apprx_tanh,
                               bias=prm2[:, N2_B1 + 2 * kv + ht:N2_B1 + 2 * kv + ht + 1])
            ins.then_inc(hid_ready, 1)
            act.wait_ge(turn_psum, 1)
            copy(qT2[:, 0:2, :], pairs(T[0]), scale=HD ** -0.5)
            copy(qT2[:, 2:4, :], pairs(T[1]), scale=HD ** -0.5).then_inc(turn_a, 1)
            act.wait_ge(turn_psum, 3)
            copy(qmT[:, :, :], pairs(T[1]), scale=HD ** -0.5).then_inc(turn_a, 1)
            act.wait_ge(turn_psum, 4)
            copy(kT2[:, 0:2, :], pairs(T[0])).then_inc(turn_a, 1)
            act.wait_ge(turn_psum, 5)
            copy(mkT[1][:, :, :], pairs(T[1])).then_inc(turn_a, 1)
            act.wait_ge(csc_ready, 1)
            copy(Sc[:, :, :, 0:N_CMP], Sc[:, :, :, 0:N_CMP], ACT.Exp).then_inc(cexp, 1)
            attention_a(0)
            out_and_ffn_a(0)

            norm_sums2(NORM_ATT[1], x, 3)
            norm_T2(NORM_ATT[1], [(hT, N2_ATT + 8), (hsT, N2_KV)])
            for q in range(4):
                take2(Q_SHARED + q, zk[:, 0, 512 * q:min(512 * (q + 1), SHARED)])
            act.wait_ge(fg_in, 1)
            copy(ef, ef, ACT.Exp).then_inc(fg_exp, 1)
            act.wait_ge(fg_exp, 1)
            copy(ef, ef, ACT.Ln, bias=1.0).then_inc(fg_ln, 1)
            for q in range(2):
                take2(Q_IN + q, zq[:, 0, 512 * q:512 * (q + 1)])
            for b in range(2):
                if b == 0:
                    act.wait_ge(turn_psum, 6)
                ins = copy(qT2[:, 2 * b:2 * b + 2, :], pairs(T[b]), scale=HD ** -0.5)
            ins.then_inc(turn_a, 1)
            act.wait_ge(turn_psum, 7)
            for b in range(2):
                ins = copy(kT2[:, 2 * b:2 * b + 2, :], pairs(T[b]))
            ins.then_inc(turn_a, 1)
            attention_a(1)
            out_and_ffn_a(1)
            norm_sums2(NORM_FINAL, x, 5)

        @block.vector
        def _(dve):
            v = nc.vector
            ch = Chain(dve, d_chain)
            dve.wait_ge(x_in, 16)
            dve.sem_inc(x_new.sem, 1)
            dve.sem_inc(ff_u.sem, AHEAD)
            dve.sem_inc(cf_cv, AHEAD)
            dve.wait_ge(brow_psum, 1)
            v.tensor_tensor(vrow[:, :], T[3][0:8, 0:TRI], const["window"][:, :], ALU.add).then_inc(brow_ready, 1)
            dve.wait_ge(const_in, 16 * len(const))

            with dve.Fori(0, DEPTH) as l:
                def multiplied(n):
                    dve.wait_ge(*unit_done(l, SLOTS + n))

                def take(q, dst):
                    multiplied(end_of(q))
                    v.tensor_copy(dst, G[2 * (q % 2) + 1][:, 0:dst.shape[-1]]).then_inc(z_d.sem, 1)

                def norm_rows(k):
                    dve.wait_ge(*rstd_ready(l, k + 1))
                    for s in range(NT):
                        ins = v.tensor_scalar(h[:, s, :], x[:, s, :], rstd[:, s:s + 1], None, ALU.mult)
                    ins.then_inc(h_ready.sem, 1)

                def norm_T(k, row):
                    for c in range(4, 8):
                        dve.wait_ge(*hT_psum(l, 4 * k + c // 2 + 1))
                        ins = v.tensor_scalar(hT[:, c, :], T[c // 2][:, (c % 2) * SEQ:(c % 2 + 1) * SEQ],
                                              prm[:, row + c:row + c + 1], None, ALU.mult)
                    ins.then_inc(hT_d.sem, 1)

                dve.wait_ge(*prm_psum(l, 1))
                v.tensor_copy(prm[:, :], T[0][:, 0:R_END])
                v.tensor_copy(cw[:, :], T[1][:, 0:124])
                v.tensor_tensor(wsT[:, :, :], T[2][:, :].rearrange("p (c s) -> p c s", c=4),
                                upper[:, :].unsqueeze(1).to_broadcast([P, 4, P]), ALU.mult).then_inc(prm_ready.sem, 1)
                norm_rows(0)
                norm_T(0, R_N1)
                take(0, zr[:, 1, 0, :])
                take(1, zr[:, 1, 1, :])
                dve.wait_ge(*z_a(l, taken("A", 1)))
                dve.wait_ge(*z_d(l, taken("D", 1)))
                for s in range(NT):
                    z = zr[:, s, 0:2, :].rearrange("p a (b c) -> p (a b) c", c=P)
                    o = h[:, s, :].rearrange("p (b c) -> p b c", c=P)
                    w = tmp[:, s, :].rearrange("p (b c) -> p b c", c=P)
                    c_t, s_t = const["rope_c"][:, s, :], const["rope_s"][:, s, :]

                    def over_heads(a):
                        return a.unsqueeze(1).to_broadcast([P, 8, a.shape[-1]])
                    v.tensor_tensor(o, z, over_heads(c_t), ALU.mult)
                    v.tensor_tensor(w[:, :, 0:64], z[:, :, 64:P], over_heads(s_t[:, 0:64]), ALU.mult)
                    ch.link(v.tensor_tensor(w[:, :, 64:P], z[:, :, 0:64], over_heads(s_t[:, 64:P]), ALU.mult))
                    ins = v.tensor_tensor(o, o, w, ALU.add)
                ins.then_inc(rot_ready.sem, 1)
                take(2, zr[:, 1, 2, :])
                for b in range(2, 4):
                    dve.wait_ge(*rqk_psum(l, b + 1))
                    ins = v.tensor_copy(kTt[:, b - 2, :], T[b][:, :])
                ins.then_inc(kT_ready.sem, 1)
                take(4, zc[:, 1, 0, :])
                for i in range(4):
                    dve.wait_ge(*rsc_psum(l, i + 1))
                    v.tensor_tensor(scr[:, i, :], T[i][:, 0:TRI], decay[:, i, :], ALU.mult).then_inc(rsc_ready.sem, 1)
                dve.wait_ge(*z_a(l, taken("A", 5)))
                dve.wait_ge(*z_d(l, taken("D", 4)))
                v.scalar_tensor_tensor(mix[:, :, 0:MIX], zc[:, :, 1, :], 1.0, zc[:, :, 0, :],
                                       ALU.add, ALU.mult).then_inc(cu_ready.sem, 1)
                dve.wait_ge(*ry_psum(l, 1))
                for s in range(NT):
                    for i in range(4):
                        ins = v.bn_stats(st[:, 4 * s + i, :], T[s][:, i * P:(i + 1) * P])
                ch.link(ins)
                for i in range(8):
                    ins = v.bn_aggr(mv[:, i, :], st[:, i, :])
                ins.then_inc(ry_stat.sem, 1)
                dve.wait_ge(*ry_rstd(l, 1))
                for s in range(NT):
                    for i in range(4):
                        j = 4 * s + i
                        ins = v.tensor_scalar(yr[:, s, i * P:(i + 1) * P], T[s][:, i * P:(i + 1) * P],
                                              mv[:, j, 0:1], rs8[:, j:j + 1], ALU.subtract, ALU.mult)
                ch.link(ins)
                dve.wait_ge(*z_a(l, taken("A", 3)))
                v.tensor_tensor(yr, yr, zr[:, :, 3, :], ALU.mult).then_inc(rya_ready.sem, 1)
                dve.wait_ge(*z_a(l, taken("A", 7)))
                for s in range(NT):
                    ins = v.bn_stats(st[:, s, :], zg[:, s, 1, :])
                ch.link(ins)
                for s in range(NT):
                    ins = v.bn_aggr(mv[:, s, :], st[:, s, :])
                ins.then_inc(gv_stat.sem, 1)
                dve.wait_ge(*gv_rstd(l, 1))
                for s in range(NT):
                    ins = v.tensor_scalar(tmp[:, s, 0:MIX], zg[:, s, 1, :], mv[:, s, 0:1], rs8[:, s:s + 1],
                                          ALU.subtract, ALU.mult)
                ins.then_inc(gv_norm.sem, 1)
                take(8, zs[:, 1, 0:512])
                dve.wait_ge(*gs_psum(l, 1))
                for s in range(NT):
                    for c in range(4):
                        cols = slice(c * P, (c + 1) * P)
                        ins = v.scalar_tensor_tensor(yg[:, s, cols], T[2 + s][:, cols], prm[:, R_BS + c:R_BS + c + 1],
                                                     zg[:, s, 0, cols], ALU.add, ALU.mult)
                ins.then_inc(gy_ready.sem, 1)
                take(9, zs[:, 1, 512:768])
                dve.wait_ge(*z_a(l, taken("A", 9)))
                dve.wait_ge(*z_d(l, taken("D", 9)))
                dve.wait_ge(*gs_psum(l, 1))
                ch.link(v.tensor_tensor(tmp[:, :, 0:640], zs[:, :, 0:640], zs[:, :, 0:640], ALU.mult))
                for s in range(NT):
                    ins = v.tensor_reduce(ssw[:, s * 10:s * 10 + 10],
                                          tmp[:, s, 0:640].rearrange("p (a b) -> p a b", b=HD), AX.X, ALU.add)
                ins.then_inc(sw_sumsq.sem, 1)
                dve.wait_ge(*sw_rstd(l, 1))
                for s in range(NT):
                    r = rs8[:, s * 10:s * 10 + 10]
                    v.tensor_tensor(tmp[:, s, 0:512].rearrange("p (a b) -> p a b", b=HD),
                                    zs[:, s, 0:512].rearrange("p (a b) -> p a b", b=HD),
                                    r[:, 0:8].unsqueeze(2).to_broadcast([P, 8, HD]), ALU.mult)
                    for a in range(2):
                        ins = v.tensor_tensor(kdup[:, s, :].rearrange("p (g a b) -> p g a b", a=2, b=HD)[:, :, a, :],
                                              zs[:, s, 512:640].rearrange("p (a b) -> p a b", b=HD),
                                              r[:, 8:10].unsqueeze(2).to_broadcast([P, 2, HD]), ALU.mult)
                ins.then_inc(sw_norm.sem, 1)

                dve.wait_ge(*cuT_ready(l, 1))
                tap_mark = [0] * 4

                def taps(k0, k1):
                    for k in range(k0, min(k1, 31)):
                        for c in range(4):
                            wk = cw[:, 4 * k + c:4 * k + c + 1]
                            u_k = uTp[:, c, k:k + SEQ]
                            if k == 0:
                                ins = v.tensor_scalar(cacc[:, c, :], u_k, wk, prm[:, R_CB + c:R_CB + c + 1],
                                                      ALU.mult, ALU.add)
                            else:
                                dve.wait_ge(ch.sem, tap_mark[c])
                                ins = v.scalar_tensor_tensor(cacc[:, c, :], u_k, wk, cacc[:, c, :], ALU.mult, ALU.add)
                            tap_mark[c] = ch.mark(ins)

                for u in range(16):
                    if u == 0:
                        dve.wait_ge(*sw_psum(l, 1))
                        for b in range(2):
                            ins = v.tensor_scalar(swq[:, 2 * b:2 * b + 2, :],
                                                  T[b][:, :].rearrange("p (c s) -> p c s", c=2),
                                                  prm[:, R_QG:R_QG + 1], HD ** -0.5, ALU.mult, ALU.mult)
                        ins.then_inc(sw_qT.sem, 1)
                    if 1 <= u <= 8:
                        i = u - 1
                        if i == 0:
                            dve.wait_ge(bias_in, 48)
                        dve.wait_ge(*sw_sc(l, i + 1))
                        dve.sem_inc(hold_d, 1)
                        for a, cols in enumerate((slice(0, P), slice(P, TRI))):
                            ins = v.tensor_tensor_reduce(out=S[:, i, cols], in0=T[0][:, cols], in1=bias[:, i, cols],
                                                         scale=1.0, scalar=sinks[:, i:i + 1], op0=ALU.add, op1=ALU.max,
                                                         accum_out=mx[:, i, a:a + 1])
                        ch.link(ins)
                        v.tensor_scalar(nm[:, i, :], mx[:, i, :], -1.0, None, ALU.mult).then_inc(sw_nm.sem, 1)
                    if u == 10:
                        ch.link(v.tensor_tensor(es[:, 0:8, :], nm[:, 0:8, :],
                                                sinks[:, :].unsqueeze(2).to_broadcast([P, 8, 2]), ALU.add))
                        dve.sem_inc(sw_sink.sem, 1)
                    if u < 11:
                        taps(3 * u, 3 * u + 3)
                    if u == 11:
                        dve.wait_ge(*sw_exp(l, 8))
                        dve.wait_ge(*sw_esink(l, 1))
                        ch.link(v.tensor_tensor(rsum[:, 0:8, :], rsum[:, 0:8, :], es[:, 0:8, :], ALU.add))
                        ch.link(v.reciprocal(rsum[:, 0:8, :], rsum[:, 0:8, :]))
                        dve.wait_ge(*sw_o(l, 8))
                        for s in range(NT):
                            ins = v.tensor_tensor(mix[:, s, 0:MIX].rearrange("p (a b) -> p a b", b=HD),
                                                  T[2 + s][:, :].rearrange("p (a b) -> p a b", b=HD),
                                                  rsum[:, 0:8, s:s + 1].to_broadcast([P, 8, HD]), ALU.mult)
                        ins.then_inc(sy_ready.sem, 1)
                        dve.wait_ge(ch.sem, ch.n)
                        dve.sem_inc(cv_ready.sem, 1)
                    if u == 13:
                        dve.wait_ge(*cv_psum(l, 1))
                        for s in range(NT):
                            ins = v.bn_stats(st[:, s, :], T[2 + s][:, :])
                        ch.link(ins)
                        for s in range(NT):
                            ins = v.bn_aggr(mv[:, s, :], st[:, s, :])
                        ins.then_inc(cv_stat.sem, 1)
                        dve.wait_ge(*cv_rstd(l, 1))
                        for s in range(NT):
                            ins = v.tensor_scalar(h[:, s, 0:MIX], T[2 + s][:, :], mv[:, s, 0:1], rs8[:, s:s + 1],
                                                  ALU.subtract, ALU.mult)
                        ins.then_inc(cn_ready.sem, 1)

                for i, b in enumerate(BRANCH_ORDER):
                    for hf in range(2):
                        q = P_BRANCH + 2 * i + hf
                        cols = slice(hf * 512, (hf + 1) * 512)
                        multiplied(end_of(q))
                        if i == 0 and hf == 0:
                            dve.wait_ge(*z_a(l, taken("A", P_GATE + 7)))
                            dve.wait_ge(*sy_psum(l, 1))
                        for s in range(NT):
                            dst = mix if i == 0 else tmp
                            ins = v.scalar_tensor_tensor(dst[:, s, cols], gates[:, s, b, cols], 1.0,
                                                         G[2 * (q % 2) + s][:, :], ALU.add, ALU.mult)
                        if i:
                            ch.link(ins)
                            ins = v.tensor_tensor(mix[:, :, cols], mix[:, :, cols], tmp[:, :, cols], ALU.add)
                        ins.then_inc(z_d.sem, 1)
                for b in range(2, 4):
                    dve.wait_ge(*mixT_psum(l, b + 1))
                    ins = v.tensor_scalar(hT[:, 2 * b:2 * b + 2, :], T[b][:, :].rearrange("p (c s) -> p c s", c=2),
                                          0.5, None, ALU.mult)
                ins.then_inc(mixT_d.sem, 1)
                for hf in range(2):
                    q = P_OUT + hf
                    cols = slice(hf * 512, (hf + 1) * 512)
                    multiplied(end_of(q))
                    for s in range(NT):
                        ins = v.tensor_tensor(x[:, s, cols], x[:, s, cols], G[2 * (q % 2) + s][:, :], ALU.add)
                    ins.then_inc(z_d.sem, 1)
                dve.wait_ge(*z_d(l, taken("D", P_OUT + 1)))
                dve.sem_inc(x_new.sem, 1)
                norm_rows(1)
                norm_T(1, R_N2)

                def ff_hidden(parity, done, free):
                    dve.wait_ge(ff_sg.sem, done)
                    if free is not None:
                        dve.wait_ge(ff_tr.sem, free)
                    for s in range(NT):
                        ins = v.tensor_tensor(uu[:, parity, s, :], sg[:, parity, s, :],
                                              G[2 * parity + s][:, 256:512], ALU.mult)
                    ins.then_inc(ff_u.sem, 1)

                before = l * FF_PANELS + AHEAD
                ff_hidden(0, before + 1, None)
                with dve.Fori(0, FF_PANELS // 2) as i:
                    ff_hidden(1, before + i * 2 + 2, before + i * 2)
                    ff_hidden(0, before + i * 2 + 3, before + i * 2 + 1)
                multiplied(L_UNITS)
                for s in range(NT):
                    for hf in range(2):
                        cols = slice(hf * 512, (hf + 1) * 512)
                        ins = v.tensor_tensor(x[:, s, cols], x[:, s, cols], G[2 * s + hf][:, :], ALU.add)
                ins.then_inc(x_new.sem, 1)
                ch.restart()

            def norm_rows2(k, src=x):
                dve.wait_ge(*rstd_ready(DEPTH, k + 1))
                for s in range(NT):
                    ins = v.tensor_scalar(h[:, s, :], src[:, s, :], rstd[:, s:s + 1], None, ALU.mult)
                ins.then_inc(h_ready.sem, 1)

            def norm_T2(k, outs):
                for c in range(4, 8):
                    dve.wait_ge(*hT_psum(DEPTH, 4 * k + c // 2 + 1))
                    for dst, row in outs:
                        ins = v.tensor_scalar(dst[:, c, :], T[c // 2][:, (c % 2) * SEQ:(c % 2 + 1) * SEQ],
                                              prm2[:, row + c:row + c + 1], None, ALU.mult)
                ins.then_inc(hT_d.sem, 1)

            def take2(q, dst):
                dve.wait_ge(*unit_done(DEPTH, SLOTS + U2_PANEL[q] + 2))
                v.tensor_copy(dst, G[2 * (q % 2) + 1][:, 0:dst.shape[-1]]).then_inc(z2_d, 1)

            def pairs(bank):
                return bank[:, :].rearrange("p (c s) -> p c s", s=SEQ)

            def rotate(dst, src, w, c_t, s_t, heads, rows_=P):
                def over(a):
                    return a.unsqueeze(1).to_broadcast([rows_, heads, a.shape[-1]])
                v.tensor_tensor(dst, src, over(c_t), ALU.mult)
                v.tensor_tensor(w[:, :, 0:32], src[:, :, 32:HD], over(s_t[:, 0:32]), ALU.mult)
                ch.link(v.tensor_tensor(w[:, :, 32:HD], src[:, :, 0:32], over(s_t[:, 32:HD]), ALU.mult))
                return v.tensor_tensor(dst, dst, w, ALU.add)

            def combine(f, branch, at_first):
                heads = lambda a: a.rearrange("p (h c) -> p h c", c=HD)
                for s in range(NT):
                    for g2 in range(2):
                        o = heads(G[2 * s + g2][:, 0:6 * HD])
                        dst = heads(h[:, s, g2 * 384:(g2 + 1) * 384])
                        w = heads(tmp[:, s, g2 * 384:(g2 + 1) * 384])
                        cf = coef[:, 6 * g2:6 * g2 + 6, s:s + 1].to_broadcast([P, 6, HD])
                        ins = v.tensor_tensor(dst if at_first else w, o, cf, ALU.mult)
                if not at_first:
                    ch.link(ins)
                    ins = v.tensor_tensor(h[:, :, 0:MIX_W], h[:, :, 0:MIX_W], tmp[:, :, 0:MIX_W], ALU.add)
                ins.then_inc(at_sum, 1)

            def attention_d(f):
                jobs = [j for j, job in enumerate(JOBS) if job[0] == f]

                def maxima(j):
                    _, kind, i = JOBS[j]
                    bank, p = T[j % 2], S4[:, j % 4, :]
                    dve.wait_ge(at_sc, j + 1)
                    if kind == "mem":
                        ins = v.tensor_reduce(mx[:, i, :], bank[:, :].rearrange("p (t c) -> p t c", t=NT), AX.X, ALU.max)
                    elif kind == "fgt":
                        for s, cols in enumerate((slice(0, P), slice(P, TRI))):
                            ins = v.scalar_tensor_tensor(p[:, cols], bank[:, cols], dcum[:, s, i:i + 1],
                                                         c2["causal"][:, cols], ALU.add, ALU.add)
                        ch.link(ins)
                        for s, cols in enumerate((slice(0, P), slice(P, TRI))):
                            ins = v.tensor_reduce(mx[:, i, s:s + 1], p[:, cols], AX.X, ALU.max)
                    else:
                        for s, cols in enumerate((slice(0, P), slice(P, TRI))):
                            ins = v.tensor_tensor_reduce(out=p[:, cols], in0=bank[:, cols], in1=c2["causal"][:, cols],
                                                         scale=1.0, scalar=-3e38, op0=ALU.add, op1=ALU.max,
                                                         accum_out=mx[:, i, s:s + 1])
                    ch.link(ins)
                    v.tensor_scalar(nm[:, i, :], mx[:, i, :], -1.0, None, ALU.mult).then_inc(at_nm, 1)

                def probs(j):
                    dve.wait_ge(at_tr, j + 1)
                    if j >= 2:
                        dve.wait_ge(at_o, j)
                    n = 512 if JOBS[j][1] == "mem" else TRI
                    v.tensor_copy(pT4[:, j % 2, 0:n], T[2 + j % 2][:, 0:n]).then_inc(at_pT, 1)

                def finish(j):
                    _, kind, _ = JOBS[j]
                    dve.wait_ge(at_exp, j + 1)
                    n = N_MEM_H if kind == "mem" else N_MIX
                    ch.link(v.reciprocal(coef[:, 0:n, :], rsums[:, groups_before(j) % 2, 0:n, :]))
                    if kind in ("slc", "win"):
                        br = 1 if kind == "slc" else 2
                        ch.link(v.tensor_tensor(coef[:, :, :], coef[:, :, :],
                                                gsig[:, :, :, br].rearrange("p t h -> p h t"), ALU.mult))
                    dve.wait_ge(at_o, j + 2)
                    if kind != "mem":
                        combine(f, kind, kind == "fgt")
                        return
                    for s in range(NT):
                        ins = v.tensor_tensor(h[:, s, MIX_W:D_MODEL].rearrange("p (h c) -> p h c", c=HD),
                                              G[2 * s][:, 0:256].rearrange("p (h c) -> p h c", c=HD),
                                              coef[:, 0:N_MEM_H, s:s + 1].to_broadcast([P, N_MEM_H, HD]), ALU.mult)
                    ins.then_inc(at_sum, 1)

                for step in range(len(jobs) + 2):
                    if step < len(jobs):
                        maxima(jobs[step])
                    if 1 <= step <= len(jobs):
                        probs(jobs[step - 1])
                    if step >= 2 and jobs[step - 2] in LAST:
                        finish(jobs[step - 2])

            def out_and_ffn_d(f):
                for b in range(2, 4):
                    dve.wait_ge(oT_psum, 4 * f + b + 1)
                    ins = v.tensor_copy(hT[:, 2 * b:2 * b + 2, :], pairs(T[b]))
                ins.then_inc(oT_d, 1)
                for hf in range(2):
                    q = Q_OUT[f] + hf
                    dve.wait_ge(*unit_done(DEPTH, SLOTS + U2_PANEL[q] + 2))
                    cols = slice(hf * 512, (hf + 1) * 512)
                    for s in range(NT):
                        ins = v.tensor_tensor(x[:, s, cols], x[:, s, cols], G[2 * (q % 2) + s][:, :], ALU.add)
                    ins.then_inc(z2_d, 1)
                dve.wait_ge(z2_d, taken2("D", Q_OUT[f] + 1))
                dve.sem_inc(x_new.sem, 1)
                norm_rows2(NORM_FFN[f])
                norm_T2(NORM_FFN[f], [(hT, N2_FFN + 8 * f)])
                done = f * FF_PANELS
                units = DEPTH * L_UNITS + SLOTS + U2_UP[f]

                def take_up(j, parity, first=False):
                    dve.wait_ge(unit_done.sem, units + 2 + j * 2)
                    if not first:
                        dve.wait_ge(cf_tr, 2 * done + j * 2 - 2)
                    v.tensor_copy(zcv[:, parity, 1, :], G[2 * parity + 1][:, :]).then_inc(cf_zd, 1)

                def conv(j, parity):
                    ch.restart()
                    mark = [0] * 4
                    for k in (1, 0):
                        for a in range(4):
                            b, c = a // 2, a % 2
                            if k == 1 and c == 0:
                                dve.wait_ge(cf_tap, 2 * done + j * 2 + 1 + b)
                            if k == 0:
                                dve.wait_ge(ch.sem, mark[a])
                            d = 2 - k
                            tile = 22 * b + j * 2 + c
                            acc = accv[:, parity, a, d:SEQ]
                            ins = v.scalar_tensor_tensor(acc, T[2 * parity + b][:, c * SEQ:(c + 1) * SEQ - d],
                                                         cvp[:, f, k, bass.ds(tile, 1)], acc, ALU.mult, ALU.add)
                            mark[a] = ch.mark(ins)
                    dve.wait_ge(ch.sem, ch.n)
                    dve.sem_inc(cf_cv, 1)

                def hidden(j, parity):
                    dve.wait_ge(cf_silu, done + j + 1)
                    v.tensor_tensor(uT[:, bass.ds(j * 2, 2), :], accv[:, parity, 0:2, :], accv[:, parity, 2:4, :],
                                    ALU.mult).then_inc(cf_uT, 1)

                take_up(0, 0, True)
                take_up(1, 1, True)
                conv(0, 0)
                take_up(2, 0)
                conv(1, 1)
                hidden(0, 0)
                ch.restart()
                with dve.Fori(0, (FF_PANELS - 3) // 2) as i:
                    take_up(i * 2 + 3, 1)
                    conv(i * 2 + 2, 0)
                    hidden(i * 2 + 1, 1)
                    take_up(i * 2 + 4, 0)
                    conv(i * 2 + 3, 1)
                    hidden(i * 2 + 2, 0)
                    ch.restart()
                conv(10, 0)
                hidden(9, 1)
                hidden(10, 0)
                dve.wait_ge(*unit_done(DEPTH, SLOTS + U2_DOWN[f] + FF_KT // 2))
                for s in range(NT):
                    for hf in range(2):
                        cols = slice(hf * 512, (hf + 1) * 512)
                        ins = v.tensor_tensor(x[:, s, cols], x[:, s, cols], G[2 * s + hf][:, :], ALU.add)
                ins.then_inc(x_new.sem, 1)

            dve.wait_ge(prm2_psum, 1)
            v.tensor_copy(prm2[:, :], T[0][:, 0:N2_END])
            v.tensor_copy(cvp.rearrange("p f k r -> p (f k r)"), T[1][:, 0:352]).then_inc(prm2_ready, 1)
            norm_rows2(NORM_ATT[0])
            norm_T2(NORM_ATT[0], [(hT, N2_ATT)])
            norm_rows2(NORM_MEM, mem)
            for q in range(2):
                take2(q, z2[:, 1, 512 * q:512 * (q + 1)])
            norm_T2(NORM_MEM, [(memT[0], N2_MEM), (memT[1], N2_MEM + 8)])

            def doubled(dst, src):
                return v.tensor_copy(dst.rearrange("p (g a c) -> p g a c", a=2, c=HD),
                                     src.rearrange("p (g c) -> p g c", c=HD).unsqueeze(2).to_broadcast([P, 4, 2, HD]))
            dve.wait_ge(z2_a, taken2("A", 1))
            dve.wait_ge(z2_d, taken2("D", 1))
            for s in range(NT):
                ins = doubled(kvd[:, s, :], z2[:, s, MIX_W:MIX_W + 256])
            ins.then_inc(kvd_ready, 1)
            take2(2, z2[:, 1, 1024:1536])
            take2(3, z2[:, 1, 1536:A_IN])
            dve.wait_ge(cmpT_psum, 1)
            v.tensor_copy(u2[0:HD, 2:4, :], pairs(T[1])[0:HD])
            v.tensor_copy(u2[HD:P, 2:4, 0:SEQ - 1], pairs(T[1])[HD:P, :, 1:SEQ]).then_inc(u2_d, 1)
            dve.wait_ge(c2_in, 16 * (len(c2) + 5))
            dve.wait_ge(z2_a, taken2("A", 3))
            dve.wait_ge(z2_d, taken2("D", 3))
            for s in range(NT):
                for c0, c1, heads in ((0, 0, 12), (1024, 768, 2), (1280, 896, 2)):
                    src, dst, w = (a[:, s, c:c + heads * HD].rearrange("p (h c) -> p h c", c=HD)
                                   for a, c in ((z2, c0), (h, c1), (tmp, c1)))
                    ins = rotate(dst, src, w, c2["rope2_c"][:, s, :], c2["rope2_s"][:, s, :], heads)
            ch.link(ins)
            for s in range(NT):
                ins = doubled(kd2[:, s, :], h[:, s, MIX_W:D_MODEL])
            ins.then_inc(rot2, 1)
            ch.link(v.memset(tmp_flat, 0.0))
            dve.wait_ge(rot2, 1)
            dve.wait_ge(u2_a, 1)
            dve.wait_ge(u2_d, 1)
            for kv in range(2):
                for g2 in range(2):
                    base = u2[:, 2 * kv + g2, :]
                    src = bass.AP(base.tensor, base.offset, [base.ap[0], [2, 16], [16, N_CMP]])
                    pos = prm2[:, N2_POS + 16 * kv:N2_POS + 16 * (kv + 1)].unsqueeze(2).to_broadcast([P, 16, N_CMP])
                    ins = v.tensor_tensor(blocks[:, kv, :, g2, 0:N_CMP], src, pos, ALU.add)
            ins.then_inc(blocks_ready, 1)
            take2(Q_MEM, mkv[0][:, 1, :])
            take2(Q_MEM + 1, mkv[1][:, 1, :])
            for s in range(NT):
                ins = v.tensor_tensor(gsig[:, s, :, :].rearrange("p h b -> p (h b)"), z2[:, s, 1536:1572], gate_b, ALU.add)
            ins.then_inc(gate_in, 1)
            v.tensor_copy(upones[:, 0:P], upper[:, :])
            v.memset(upones[:, P:SEQ], 1.0)
            ch.link(v.memset(Sc[:, :, :, :], 0.0))
            dve.wait_ge(kvc_psum, 1)
            ch.link(v.tensor_tensor(kvc, T[3][:, 0:256].rearrange("p (v g c) -> p v g c", v=2, g=2),
                                    b2c.unsqueeze(2).to_broadcast([P, 2, 2, HD]), ALU.add))
            ch.link(rotate(kcr[0:N_CMP, :, 0:HD], kvc[0:N_CMP, 0], kct[0:N_CMP], c2["ropec_c"], c2["ropec_s"], 2, N_CMP))
            v.tensor_copy(kcr[0:N_CMP, :, HD:P], kcr[0:N_CMP, :, 0:HD]).then_inc(kcr_ready, 1)
            dve.wait_ge(kcT_psum, 1)
            v.tensor_copy(kcT[:, :, 0:N_CMP], T[3][:, 0:32].rearrange("p (g c) -> p g c", g=2)[:, :, 0:N_CMP]).then_inc(kcT_ready, 1)
            dve.wait_ge(turn_psum, 2)
            v.tensor_scalar(qT2[:, 4:6, :], pairs(T[2]), HD ** -0.5, None, ALU.mult).then_inc(turn_d, 1)
            dve.wait_ge(turn_psum, 4)
            v.tensor_copy(kT2[:, 2:4, :], pairs(T[3]))
            dve.wait_ge(turn_psum, 5)
            v.tensor_copy(mkT[0][:, :, :], pairs(T[2])).then_inc(turn_d, 1)
            dve.wait_ge(csc_psum, 1)
            scv = Sc[:, :, :, 0:N_CMP]
            for s in range(NT):
                for b in range(2):
                    ins = v.tensor_tensor(scv[:, s, b::2], T[b][:, s * 90:(s + 1) * 90].rearrange("p (h n) -> p h n", n=N_CMP),
                                          c2["cmp_neg"][:, s, :].unsqueeze(1).to_broadcast([P, 6, N_CMP]), ALU.add)
            ch.link(ins)
            ch.link(v.tensor_reduce(mxc, scv, AX.X, ALU.max))
            for s in range(NT):
                ins = v.tensor_tensor(scv[:, s], scv[:, s], mxc[:, s, :].unsqueeze(2).to_broadcast([P, N_MIX, N_CMP]), ALU.subtract)
            ins.then_inc(csc_ready, 1)
            dve.wait_ge(cexp, 1)
            for s in range(NT):
                ins = v.tensor_tensor(scv[:, s], scv[:, s], c2["cmp_ok"][:, s, :].unsqueeze(1).to_broadcast([P, N_MIX, N_CMP]), ALU.mult)
            ins.then_inc(cprob, 1)
            dve.wait_ge(cprob, 1)
            ch.link(v.tensor_reduce(smc, scv, AX.X, ALU.add))
            ch.link(v.tensor_scalar(smc, smc, 1e-30, None, ALU.max))
            ch.link(v.reciprocal(smc, smc))
            dve.wait_ge(gate_ready, 1)
            ch.link(v.tensor_tensor(coef, smc.rearrange("p t h -> p h t"), gsig[:, :, :, 0].rearrange("p t h -> p h t"), ALU.mult))
            dve.wait_ge(cprobT, 1)
            for s in range(NT):
                ins = v.tensor_copy(pcT[:, s, :, :], T[2 + s][:, 0:TRI].rearrange("p (a c) -> p a c", c=P))
            ins.then_inc(pcT_ready, 1)
            dve.wait_ge(at_o, 1)
            for s in range(NT):
                for b in range(4):
                    ins = v.tensor_tensor(h[:, s, 0:MIX_W].rearrange("p (a b c) -> p a b c", b=4, c=HD)[:, :, b, :],
                                          G[b][:, s * 192:(s + 1) * 192].rearrange("p (a c) -> p a c", c=HD),
                                          coef[:, b::4, s:s + 1].to_broadcast([P, 3, HD]), ALU.mult)
            ins.then_inc(at_sum, 1)
            attention_d(0)
            out_and_ffn_d(0)

            norm_rows2(NORM_ATT[1])
            norm_T2(NORM_ATT[1], [(hT, N2_ATT + 8), (hsT, N2_KV)])
            v.tensor_copy(upones[:, 0:P], upper[:, :])
            v.memset(upones[:, P:SEQ], 1.0)
            for q in range(4):
                take2(Q_SHARED + q, zk[:, 1, 512 * q:min(512 * (q + 1), SHARED)])
            dve.wait_ge(z2_a, taken2("A", Q_SHARED + 3))
            dve.wait_ge(z2_d, taken2("D", Q_SHARED + 3))
            ch.link(v.tensor_tensor(xf, zk[:, :, 2 * MIX_W:SHARED], f_b.unsqueeze(1).to_broadcast([P, NT, N_MIX]), ALU.add))
            ch.link(v.tensor_scalar(ef, xf, -1.0, None, ALU.mult))
            v.tensor_tensor(ef, ef, xf, ALU.min).then_inc(fg_in, 1)
            ch.link(v.tensor_scalar(xf, xf, 0.0, None, ALU.min))
            dve.wait_ge(fg_ln, 1)
            v.tensor_tensor(nlf, ef, xf, ALU.subtract).then_inc(fg_ready, 1)
            for q in range(2):
                take2(Q_IN + q, zq[:, 1, 512 * q:512 * (q + 1)])
            dve.wait_ge(turn_psum, 6)
            v.tensor_scalar(qT2[:, 4:6, :], pairs(T[2]), HD ** -0.5, None, ALU.mult)
            v.tensor_scalar(qmT[:, :, :], pairs(T[3]), HD ** -0.5, None, ALU.mult).then_inc(turn_d, 1)
            dve.wait_ge(fg_cum, 1)
            v.tensor_scalar(dcum, T[3][:, 0:2 * N_MIX].rearrange("p (t h) -> p t h", t=NT), -1.0, None, ALU.mult)
            v.tensor_copy(kT2[:, 4:6, :], pairs(T[2])).then_inc(turn_d, 1)
            attention_d(1)
            out_and_ffn_d(1)
            dve.wait_ge(*rstd_ready(DEPTH, NORM_FINAL + 1))
            for s in range(NT):
                ins = v.scalar_tensor_tensor(h[:, s, :], x[:, s, :], rstd[:, s:s + 1], final_g, ALU.mult, ALU.mult)
            ins.then_inc(h_ready.sem, 1)


def kernel(**inputs):
    import numpy as _np
    import concourse.bacc as _bacc
    from concourse.bass_utils import run_bass_kernel_spmd as _run

    nc = _bacc.Bacc("TRN2", target_bir_lowering=False, num_devices=1)
    arrays, t = {}, {}
    for name, a in list(inputs.items()) + list(constants().items()):
        a = _np.ascontiguousarray(a)
        arrays[f"in_{name}"] = a
        t[name] = nc.dram_tensor(f"in_{name}", a.shape, mybir.dt.from_np(a.dtype), kind="ExternalInput").ap()
    out = nc.dram_tensor("out", (1, SEQ, D_MODEL), F32, kind="ExternalOutput").ap()
    build(nc, t, out)
    r = _run(nc, [arrays], core_ids=[0])
    return r.results[0]["out"]
```

```python
import math
from contextlib import ExitStack

import numpy as np

import concourse.bass as bass
from concourse import mybir

F32 = mybir.dt.float32
F32R = mybir.dt.float32r
ALU = mybir.AluOpType
ACT = mybir.ActivationFunctionType
AX = mybir.AxisListType

P = 128
D_MODEL = 1024
SEQ = 256
NT = SEQ // P
KT = D_MODEL // P
DEPTH = 2
EPS = 1e-6
NEG = -1e30
MIX = 512
IN_COLS = 8960
SWA_C0 = 4096
GATE_C0 = 4864
D_FF = 2816
FF_PANELS = D_FF // 256
FF_KT = D_FF // P
TRI = 3 * P
HD = 64
N_MIX = 12
N_MEM_H = 4
MIX_W = N_MIX * HD
A_IN = 1828
N_CMP = 15
CMP_PAD = 32
CMP_HID = 256
SHARED = 2 * MIX_W + N_MIX

SLOTS = 4
AHEAD = 1
SKEW = 512
PRM_LOADS = 16
SLOT_W = 2048
LOADS = 2
FILL = 16 * LOADS
HALF_W = SLOT_W // 2
HI_SLOTS = 4
USED_AHEAD = 2

R_N1, R_GN, R_CB, R_CG, R_CLB, R_BS, R_N2, R_QG, R_KG, R_END = 0, 8, 12, 16, 20, 24, 28, 36, 37, 38


PANEL_EVAC = (["AD", "AD", "AD", "AA"]
              + ["AD", "AA"]
              + ["AA", "AA"]
              + ["AD", "AD"])
PANEL_UNITS = [2] * 9 + [1]
MIX_ORDER = [("gate", 0), ("branch", 0), ("gate", 2), ("branch", 2), ("gate", 3), ("gate", 1), ("branch", 3), ("branch", 1)]
BRANCH_ORDER = [b for kind, b in MIX_ORDER if kind == "branch"]
PLACE = {0: 0, 2: 1, 3: 0, 1: 1}
P_GATE, P_BRANCH, MIX_STEPS = {}, {}, []
U_MIX = sum(PANEL_UNITS)
for kind, b in MIX_ORDER:
    (P_GATE if kind == "gate" else P_BRANCH)[b] = len(PANEL_EVAC)
    for hf in range(2):
        MIX_STEPS += [(kind, b, hf, a, len(PANEL_EVAC)) for a in range(2 if kind == "gate" else 1)]
        PANEL_EVAC += ["AA" if kind == "gate" else "DD"]
        PANEL_UNITS += [2 if kind == "gate" else 1]
P_OUT = len(PANEL_EVAC)
PANEL_EVAC += ["DD"] * 2
PANEL_UNITS += [2] * 2
U_OUT = U_MIX + len(MIX_STEPS)
U_FF = U_OUT + 4
U_DOWN = U_FF + 2 * FF_PANELS
L_UNITS = U_DOWN + FF_KT // 2


def taken(engine, panel):
    return sum(engine in e for e in PANEL_EVAC[:panel + 1])


PANEL2_EVAC = ["AD"] * 6 + ["DD"] * 2 + ["AD"] * 6 + ["DD"] * 2
Q_MEM, Q_OUT, Q_SHARED, Q_IN = 4, (6, 14), 8, 12
U2_CMP = 12
U2_PANEL = [0, 2, 4, 6, 8, 10, 16, 18, 53, 55, 57, 59, 61, 63, 65, 67]
U2_UP, U2_DOWN = (20, 69), (42, 91)
U2_WHOLE = range(8, 16)
U2_SHORT = {6: 4 * 292, 7: 4 * 292, 59: 4 * 12, 60: 4 * 12}
NORMS_SPLIT = (0, 2, 3, 4)
N2_ATT, N2_FFN, N2_MEM, N2_KV, N2_B1, N2_POS, N2_END = 0, 16, 32, 48, 56, 60, 92
NORM_ATT, NORM_MEM, NORM_FFN, NORM_FINAL = (0, 3), 1, (2, 4), 5


def taken2(engine, panel):
    return sum(engine in e for e in PANEL2_EVAC[:panel + 1])


def split_before(n):
    return n - sum(u < n for u in U2_WHOLE)


def half_size(n, second=False):
    return (U2_SHORT.get(n, SLOT_W) if second else SLOT_W) // 2


def end_of(panel):
    return sum(PANEL_UNITS[:panel + 1])


def bucket_table():
    dist = np.clip(255 - np.arange(384), 0, 255)
    d = np.maximum(dist, 1).astype(np.float32)
    large = 16 + (np.log(d / np.float32(16)) / np.float32(math.log(8.0)) * np.float32(16)).astype(np.int32)
    bucket = np.where(dist < 16, dist, np.minimum(large, 31))
    return (np.arange(32)[:, None] == bucket[None, :]).astype(np.float32)


def angles(pos, half):
    inv = (np.float32(10000.0) ** (-np.arange(half, dtype=np.float32) / np.float32(half))).astype(np.float32)
    ang = pos.astype(np.float32)[:, None] * inv[None, :]
    c, s = np.cos(ang).astype(np.float32), np.sin(ang).astype(np.float32)
    return np.concatenate([c, c], 1), np.concatenate([-s, s], 1)


def constants():
    pos = np.arange(SEQ)
    tiles = lambda a: np.ascontiguousarray(a.reshape(NT, P, -1).transpose(1, 0, 2))
    c = {"ident": np.eye(P, dtype=np.float32)}
    c["rope_c"], c["rope_s"] = map(tiles, angles(pos, 64))
    c["rope2_c"], c["rope2_s"] = map(tiles, angles(pos, 32))
    cmp_end = np.arange(N_CMP) * 16 + 31
    c["ropec_c"], c["ropec_s"] = angles(cmp_end, 32)
    i = np.arange(P)
    s, t = i[:, None], i[None, :]
    gamma = 1.0 - 2.0 ** (-5.0 - np.arange(4))
    own = np.where(t >= s, gamma[:, None, None] ** np.maximum(t - s, 0)[None], 0.0)
    prev = gamma[:, None, None] ** (P + t - s)[None]
    c["decay"] = np.ascontiguousarray((np.concatenate([own, prev, own], 2) * P ** -0.5)
                                      .transpose(1, 0, 2)).astype(np.float32)
    c["bucket"] = bucket_table()
    dist = 255 - np.arange(384)
    c["window"] = np.tile(np.where((dist >= 0) & (dist < P), 0.0, NEG).astype(np.float32), (8, 1))
    c["upper"] = (t >= s).astype(np.float32)
    low = np.where(t <= s, 0.0, NEG).astype(np.float32)
    c["causal"] = np.concatenate([low, np.zeros((P, P), np.float32), low], 1)
    ok = tiles((cmp_end[None, :] <= pos[:, None]).astype(np.float32))
    c["cmp_ok"] = ok
    c["cmp_neg"] = np.where(ok > 0, 0.0, NEG).astype(np.float32)
    return c


class Signal:

    def __init__(self, sem, per, ahead=0):
        self.sem, self.per, self.ahead = sem, per, ahead

    def __call__(self, layer, k):
        return self.sem, layer * self.per + (k + self.ahead)


class Chain:

    def __init__(self, engine, sem):
        self.engine, self.sem, self.n = engine, sem, 0

    def link(self, ins):
        self.mark(ins)
        self.engine.wait_ge(self.sem, self.n)

    def mark(self, ins):
        self.n += 1
        ins.then_inc(self.sem, 1)
        return self.n

    def restart(self):
        self.engine.wait_ge(self.sem, self.n)
        self.engine.sem_clear(self.sem)
        self.n = 0


def build(nc, t, out):
    ctx = ExitStack()
    with ctx:
        def sb(name, shape):
            return ctx.enter_context(nc.sbuf_tensor(name, shape, F32))

        def under(name, shape):
            with nc.sbuf_tensor(name, shape, F32R) as tensor:
                return tensor

        def sem(name):
            return ctx.enter_context(nc.semaphore(name))

        def sig(name, per, ahead=0):
            return Signal(sem(name), per, ahead)

        scratch = nc.dram_tensor("bias_rows", (8, P * SKEW + TRI), F32, kind="Internal").ap()

        const = {}
        for name, shape in [("ident", [P, P]), ("rope_c", [P, NT, P]), ("rope_s", [P, NT, P]),
                            ("decay", [P, 4, TRI]), ("upper", [P, P])]:
            const[name] = sb(name, shape)
        ident, decay, upper = const["ident"], const["decay"], const["upper"]
        x = sb("x", [P, NT, D_MODEL])
        h = sb("h", [P, NT, D_MODEL])
        hT_lo = under("hT_lo", [P, KT, SEQ])
        hT = sb("hT", [P, KT, SEQ])
        w_lo = under("w_lo", [P, SLOTS, SLOT_W])
        ring = sb("ring", [P, SLOTS, SLOT_W])
        hsT_lo = under("hsT_lo", [P, KT, SEQ])
        tmp = sb("tmp", [P, NT, D_MODEL])
        hT_hi = ctx.enter_context(nc.sbuf_tensor("hT_hi", [P, KT, SEQ], F32R))
        w_hi = ctx.enter_context(nc.sbuf_tensor("w_hi", [P, HI_SLOTS, HALF_W], F32R))
        zr = sb("zr", [P, NT, 4, MIX])
        zc = sb("zc", [P, NT, 2, MIX])
        zg = sb("zg", [P, NT, 2, MIX])
        uT_hi = under("uT_hi", [P, FF_KT, SEQ])
        work = sb("work", [P, 4096 + NT * 768 + 4 * TRI])
        gates = work[:, 0:4096].rearrange("p (n t d) -> p n t d", n=2, t=NT)
        zs = work[:, 4096:5632].rearrange("p (t c) -> p t c", t=NT)
        S = work[:, 5632:5632 + 4 * TRI].rearrange("p (a c) -> p a c", a=4)
        const["bucket"] = work[0:32, 2048:2048 + TRI]
        const["window"] = work[0:8, 2432:2432 + TRI]
        vrow = work[0:8, 2816:2816 + TRI]
        uT_lo = under("uT_lo", [P, FF_KT, SEQ])
        ysT_parts = under("ysT_parts", [P, 2, 2, 4, SEQ])
        ysT_hi, ysT_lo = ysT_parts[:, 0], ysT_parts[:, 1]
        ysT = sb("ysT", [P, 4, 4, SEQ])
        hsT_hi = under("hsT_hi", [P, KT, SEQ])
        mix = sb("mix", [P, NT, D_MODEL])
        qkT = zr[:, 0, 0:2, :]
        kTt = zr[:, 1, 0:2, :]
        yr = zr[:, :, 0, :]
        zr_flat = zr[:, :, :, :].rearrange("p t a b -> p (t a b)")
        swq = zr_flat[:, 0:1024].rearrange("p (c s) -> p c s", s=SEQ)
        swk = zr_flat[:, 1024:1536].rearrange("p (c s) -> p c s", s=SEQ)
        kdup = zr_flat[:, 1536:2048].rearrange("p (t c) -> p t c", t=NT)
        pT = zr_flat[:, 2048:3072].rearrange("p (a c) -> p a c", a=2)
        cacc = zr_flat[:, 3072:4096].rearrange("p (c s) -> p c s", s=SEQ)
        bias = sb("bias", [P, 8, SEQ])
        prm_raw = sb("prm_raw", [R_END, P])
        cw_raw = sb("cw_raw", [124, P])
        ws_raw = sb("ws_raw", [P, 4, P])
        prm = sb("prm", [P, R_END])
        cw = sb("cw", [P, 124])
        wsT = sb("wsT", [P, 4, P])
        lng = sb("lng", [P, MIX])
        lnb = sb("lnb", [P, MIX])
        sinks = sb("sinks", [P, 8])
        uTp = sb("uTp", [P, 4, 30 + SEQ])
        ss = sb("ss", [P, NT])
        ms = sb("ms", [P, NT])
        rstd = sb("rstd", [P, NT])
        half = sb("half", [P, 24])
        st = sb("st", [P, 8, 6])
        mv = sb("mv", [P, 8, 2])
        var = sb("var", [P, 24])
        rs8 = sb("rs8", [P, 24])
        ssw = sb("ssw", [P, 24])
        mx = sb("mx", [P, N_MIX, 2])
        nm = sb("nm", [P, N_MIX, 2])
        rsum = sb("rsum", [P, N_MIX, 2])
        es = sb("es", [P, N_MIX, 2])
        zc_flat = zc[:, :, :, :].rearrange("p t a b -> p (t a b)")
        sg = zc_flat[:, 0:1024].rearrange("p (a t c) -> p a t c", a=2, t=NT)
        uu = zc_flat[:, 1024:2048].rearrange("p (a t c) -> p a t c", a=2, t=NT)
        rel = sb("rel", [32, 8])
        scr = S[:, 0:4, :]
        yg = zg[:, :, 1, :]

        decay_flat = decay[:, :, :].rearrange("p a b -> p (a b)")
        c2, at = {}, 0
        for name, shape in [("causal", [P, TRI]), ("rope2_c", [P, NT, HD]), ("rope2_s", [P, NT, HD]),
                            ("cmp_ok", [P, NT, N_CMP]), ("cmp_neg", [P, NT, N_CMP]),
                            ("ropec_c", [N_CMP, HD]), ("ropec_s", [N_CMP, HD])]:
            size = shape[-1] * (shape[1] if len(shape) == 3 else 1)
            c2[name] = decay_flat[0:shape[0], at:at + size]
            if len(shape) == 3:
                c2[name] = c2[name].rearrange("p (a b) -> p a b", a=shape[1])
            at += size

        def piece(flat, start, size, pattern=None, **sizes):
            part = flat[:, start:start + size]
            return part.rearrange(pattern, **sizes) if pattern else part
        w2c = piece(decay_flat, at, 256, "p (v k c) -> p v k c", v=2, k=2)
        b2c = piece(decay_flat, at + 256, 128, "p (v c) -> p v c", v=2)
        gate_b = piece(decay_flat, at + 384, 36)
        f_b = piece(decay_flat, at + 420, N_MIX)
        zg_flat = zg[:, :, :, :].rearrange("p t a b -> p (t a b)")
        mem = piece(zg_flat, 0, 2048, "p (t d) -> p t d", t=NT)
        final_g = piece(work, 5632, D_MODEL)
        tmp_flat = tmp[:, :, :].rearrange("p t d -> p (t d)")
        prm2_raw = tmp[0:N2_END, 0, 0:P]
        cv_raw = tmp[0:44, 1, :].rearrange("p (a c) -> p a c", c=P)
        prm2 = sb("prm2", [P, N2_END])
        cvp = uTp[:, :, :].rearrange("p c s -> p (c s)")[:, 0:352].rearrange(
            "p (f k r) -> p f k r", f=2, k=4)
        z2 = piece(zr_flat, 0, NT * A_IN, "p (t c) -> p t c", t=NT)
        zk = piece(zr_flat, 0, NT * SHARED, "p (t c) -> p t c", t=NT)
        zq = piece(zc_flat, 0, 2048, "p (t c) -> p t c", t=NT)
        memT = [zg[:, :, :, :].rearrange("p t a b -> p (t a b)").rearrange("p (c s) -> p c s", s=SEQ),
                mix[:, :, :].rearrange("p t d -> p (t d)").rearrange("p (c s) -> p c s", s=SEQ)]
        bias_flat = bias[:, :, :].rearrange("p a b -> p (a b)")
        mkv = [piece(bias_flat, 1024 * f, 1024, "p (t c) -> p t c", t=NT) for f in range(2)]
        mkT = [piece(zg_flat, 512 * f, 512, "p (c s) -> p c s", s=SEQ) for f in range(2)]
        ysT_flat = ysT[:, :, :, :].rearrange("p b c s -> p (b c s)")
        qT2 = piece(ysT_flat, 0, 1536, "p (c s) -> p c s", s=SEQ)
        qmT = piece(ysT_flat, 1536, 512, "p (c s) -> p c s", s=SEQ)
        kT2 = piece(ysT_flat, 2048, 1536, "p (c s) -> p c s", s=SEQ)
        u2 = piece(zc_flat, 0, 1024, "p (c s) -> p c s", s=SEQ)
        Sc = piece(zc_flat, 1024, 768, "p (t h n) -> p t h n", t=NT, n=CMP_PAD)
        kcr = piece(work, 4128, 256, "p (g c) -> p g c", g=2)
        kvd = piece(work, 0, 1024, "p (t c) -> p t c", t=NT)
        kd2 = piece(work, 1024, 1024, "p (t c) -> p t c", t=NT)
        kct = piece(zc_flat, 1920, 128, "p (g c) -> p g c", g=2)
        blocks = piece(tmp_flat, 0, 2048, "p (v m g n) -> p v m g n", v=2, m=16, g=2)
        S4 = piece(work, 0, 4 * 512, "p (a c) -> p a c", a=4)
        pT4 = piece(work, 2048, 2 * 512, "p (a c) -> p a c", a=2)
        pcT = piece(work, 3072, 768, "p (t a c) -> p t a c", t=NT, c=P)
        kvc = piece(work, 3840, 256, "p (v g c) -> p v g c", v=2, g=2)
        kcT = piece(work, 4096, 32, "p (g c) -> p g c", g=2)
        h1T = piece(work, 2048, 1024, "p (v k g n) -> p v k g n", v=2, k=2, g=2)
        gsig = piece(work, 4384, 72, "p (t h b) -> p t h b", t=NT, b=3)
        coef = piece(work, 4456, 24, "p (h t) -> p h t", t=NT)
        mxc = piece(work, 4480, 24, "p (t h) -> p t h", t=NT)
        smc = piece(work, 4504, 24, "p (t h) -> p t h", t=NT)
        xf = piece(work, 4528, 24, "p (t h) -> p t h", t=NT)
        ef = piece(work, 4552, 24, "p (t h) -> p t h", t=NT)
        nlf = piece(work, 4576, 24, "p (t h) -> p t h", t=NT)
        dcum = piece(work, 4600, 24, "p (t h) -> p t h", t=NT)
        upones = piece(work, 4624, SEQ)
        rsums = piece(work, 4896, 48, "p (a h t) -> p a h t", a=2, t=NT)
        zcv = piece(zc_flat, 0, 2048, "p (a t c) -> p a t c", a=2, t=NT)
        accv = piece(tmp_flat, 0, 2048, "p (a c s) -> p a c s", a=2, c=4)

        G = [ctx.enter_context(nc.psum_tensor(f"G{i}", [P, 512], F32)) for i in range(4)]
        T = [ctx.enter_context(nc.psum_tensor(f"T{i}", [P, 512], F32)) for i in range(4)]

        const_in = sem("const_in")
        x_in = sem("x_in")
        rel_in = sem("rel_in")
        brow_psum, brow_ready, brow_out, bias_in = sem("brow_psum"), sem("brow_ready"), sem("brow_out"), sem("bias_in")
        half_ready = sem("half_ready")
        pad_ready = sem("pad_ready")
        out_done = sem("out_done")
        w_full = [sig(f"w_full{i}", FILL * L_UNITS // SLOTS) for i in range(SLOTS)]
        unit_done = sig("unit_done", L_UNITS)
        prm_in = sig("prm_in", 16 * PRM_LOADS)
        prm_psum, prm_ready = sig("prm_psum", 1), sig("prm_ready", 1)
        x_new, sumsq, rstd_ready, h_ready = sig("x_new", 2), sig("sumsq", 2), sig("rstd_ready", 2), sig("h_ready", 2)
        hT_psum, memT_a, hT_d = sig("hT_psum", 8), sem("memT_a"), sig("hT_d", 2)
        hT_hi_ready = sig("hT_hi_ready", 2 * KT)
        ysT_hi_ready = sig("ysT_hi_ready", 3)
        cs_ready = sig("cs_ready", 1)
        z_a = sig("z_a", taken("A", 99))
        z_d = sig("z_d", taken("D", 99))
        rot_ready, rqk_psum, qT_ready, kT_ready = sig("rot_ready", 1), sig("rqk_psum", 4), sig("qT_ready", 1), sig("kT_ready", 1)
        rsc_psum, rsc_ready, ry_psum, ry_stat = sig("rsc_psum", 4), sig("rsc_ready", 4), sig("ry_psum", 1), sig("ry_stat", 1)
        ry_rstd, rya_ready, rya_psum, ysT_ret = sig("ry_rstd", 1), sig("rya_ready", 1), sig("rya_psum", 1), sig("ysT_ret", 1)
        cu_ready, cu_psum, cuT_ready = sig("cu_ready", 1), sig("cu_psum", 1), sig("cuT_ready", 1)
        cv_ready, cv_psum, cv_stat, cv_rstd = sig("cv_ready", 1), sig("cv_psum", 1), sig("cv_stat", 1), sig("cv_rstd", 1)
        cn_ready, cn_psum, ysT_conv = sig("cn_ready", 1), sig("cn_psum", 1), sig("ysT_conv", 1)
        gv_stat, gv_rstd, gv_norm, gv_ready = sig("gv_stat", 1), sig("gv_rstd", 1), sig("gv_norm", 1), sig("gv_ready", 1)
        gs_psum, gy_ready, gy_psum, ysT_gmlp = sig("gs_psum", 1), sig("gy_ready", 1), sig("gy_psum", 1), sig("ysT_gmlp", 1)
        sw_sumsq, sw_rstd, sw_norm, sw_psum = sig("sw_sumsq", 1), sig("sw_rstd", 1), sig("sw_norm", 1), sig("sw_psum", 1)
        sw_qT, sw_kT = sig("sw_qT", 1), sig("sw_kT", 1)
        sw_sc, sw_nm, sw_exp, sw_tr, sw_pT = sig("sw_sc", 8), sig("sw_nm", 8), sig("sw_exp", 8), sig("sw_tr", 8), sig("sw_pT", 8)
        sw_o, sw_sink, sw_esink, sy_ready, sy_psum, ysT_swa = (sig("sw_o", 8), sig("sw_sink", 1), sig("sw_esink", 1),
                                                               sig("sy_ready", 1), sig("sy_psum", 1), sig("ysT_swa", 1))
        mixT_psum, mixT_a, mixT_d = sig("mixT_psum", 4), sig("mixT_a", 4), sig("mixT_d", 1)
        ff_sg, ff_u, ff_tr, ff_uT = [sig(n, FF_PANELS, AHEAD) for n in ("ff_sg", "ff_u", "ff_tr", "ff_uT")]
        ff_hi = sig("ff_hi", FF_PANELS, AHEAD)
        w_hi_ready, w_lo_ready = sem("w_hi_ready"), sem("w_lo_ready")
        first_used = sem("first_used")
        d_chain, a_chain, g_chain = sem("d_chain"), sem("a_chain"), sem("g_chain")

        c2_in, mem_in, prm2_in, hold_d, hold_g = sem("c2_in"), sem("mem_in"), sem("prm2_in"), sem("hold_d"), sem("hold_g")
        prm2_psum, prm2_ready = sem("prm2_psum"), sem("prm2_ready")
        z2_a, z2_d = sem("z2_a"), sem("z2_d")
        kvd_ready = sem("kvd_ready")
        rot2, blocks_ready, up_ready = sem("rot2"), sem("blocks_ready"), sem("up_ready")
        cmpT_psum, u2_a, u2_d, hid_ready = sem("cmpT_psum"), sem("u2_a"), sem("u2_d"), sem("hid_ready")
        kvc_psum, kcr_ready, kcT_psum, kcT_ready = sem("kvc_psum"), sem("kcr_ready"), sem("kcT_psum"), sem("kcT_ready")
        turn_psum, turn_a, turn_d = sem("turn_psum"), sem("turn_a"), sem("turn_d")
        gate_in, gate_ready = sem("gate_in"), sem("gate_ready")
        csc_psum, csc_ready, cexp, cprob, cprobT, pcT_ready = (sem(n) for n in ("csc_psum", "csc_ready", "cexp", "cprob", "cprobT", "pcT_ready"))
        at_sc, at_nm, at_exp, at_tr, at_pT, at_o, at_sum = (sem(n) for n in ("at_sc", "at_nm", "at_exp", "at_tr", "at_pT", "at_o", "at_sum"))
        oT_psum, oT_a, oT_d = sem("oT_psum"), sem("oT_a"), sem("oT_d")
        fg_in, fg_exp, fg_ln, fg_ready, fg_cum = (sem(n) for n in ("fg_in", "fg_exp", "fg_ln", "fg_ready", "fg_cum"))
        cf_za, cf_zd, cf_tr, cf_tap, cf_cv, cf_silu, cf_uT = (sem(n) for n in ("cf_za", "cf_zd", "cf_tr", "cf_tap", "cf_cv", "cf_silu", "cf_uT"))

        JOBS = ([(0, "slc", i) for i in range(N_MIX)] + [(0, "win", i) for i in range(N_MIX)]
                + [(0, "mem", i) for i in range(N_MEM_H)]
                + [(1, "fgt", i) for i in range(N_MIX)] + [(1, "mem", i) for i in range(N_MEM_H)])
        LAST = [j for j, (f, kind, i) in enumerate(JOBS) if i == (N_MEM_H if kind == "mem" else N_MIX) - 1]

        def groups_before(j):
            return sum(j > e for e in LAST)

        block = ctx.enter_context(nc.Block())

        w_in2 = t["w_in"].rearrange("l k c -> (l k) c")
        w_br2 = t["w_branch"].rearrange("l n k c -> (l n k) c")
        w_out2 = t["w_out"].rearrange("l k c -> (l k) c")
        w_ffi2 = t["w_ffn_in"].rearrange("l k c -> (l k) c")
        w_ffo2 = t["w_ffn_out"].rearrange("l k c -> (l k) c")

        def rows(w, r0, k, c0, w_cols):
            return w[bass.ds(r0, k * P), :].rearrange("(k p) c -> p k c", p=P)[:, :, bass.ds(c0, w_cols)]

        def hi_half(n, b, size):
            return w_hi[:, (2 * n + b) % HI_SLOTS, 0:size]

        def half_of(buffer, n, b, size):
            return buffer[:, n % SLOTS, b * size:(b + 1) * size]

        def slot(i, k):
            return ring[:, i % SLOTS, :].rearrange("p (k c) -> p k c", k=k)

        @block.sync
        def _(sp):
            sp.dma_start(x[:, :, :], t["x"][0].rearrange("(t p) d -> p t d", p=P)).then_inc(x_in, 16)
            for name, tile in const.items():
                sp.dma_start(tile[tuple(slice(None) for _ in tile.shape)], t[name]).then_inc(const_in, 16)
            sp.dma_start(rel[:, :], t["rel_bias"]).then_inc(rel_in, 16)

            def load(layer, n, pieces):
                sp.wait_ge(*unit_done(layer, n + 1))
                for dst, src in pieces:
                    sp.dma_start(dst, src).then_inc(w_full[n % SLOTS].sem, 16)

            def split_k(n, w, r0, k, c0, w_cols):
                dst = slot(n, k) if w_cols * k == SLOT_W else ring[:, n % SLOTS, 0:k * w_cols].rearrange(
                    "p (k c) -> p k c", k=k)
                a = k // 2
                return [(dst[:, 0:a, :], rows(w, r0, a, c0, w_cols)),
                        (dst[:, a:k, :], rows(w, r0 + a * P, k - a, c0, w_cols))]

            def gate_up(n, w, r0, k0, j, half_width):
                dst = slot(n, 4).rearrange("p k (a c) -> p k a c", a=2)
                return [(dst[:, :, a, :], rows(w, r0 + k0, 4, j * 256 + a * half_width, 256)) for a in range(2)]

            with sp.Fori(0, DEPTH) as l:
                def prm_load(dst, src):
                    sp.dma_start(dst, src).then_inc(prm_in.sem, 16)

                def vec(name, r0, n):
                    prm_load(prm_raw[r0:r0 + n, :], t[name][bass.ds(l, 1), :].rearrange("a (r p) -> (a r) p", p=P))
                vec("norm1_g", R_N1, 8)
                vec("ret_gn_g", R_GN, 4)
                vec("conv_b", R_CB, 4)
                vec("conv_ln_g", R_CG, 4)
                vec("conv_ln_b", R_CLB, 4)
                vec("norm2_g", R_N2, 8)
                prm_load(prm_raw[R_BS:R_BS + 4, :], t["gmlp_bs"][bass.ds(l, 1), :, :].rearrange("a g s -> (a g) s"))
                for r, name in ((R_QG, "swa_q_g"), (R_KG, "swa_k_g")):
                    for a in range(2):
                        prm_load(prm_raw[r:r + 1, a * HD:(a + 1) * HD], t[name][bass.ds(l, 1), :])
                prm_load(cw_raw[:, :], t["conv_w"][bass.ds(l, 1), :, :, :].rearrange("a k o (c p) -> (a k o c) p", p=P))
                prm_load(ws_raw[:, :, :], t["gmlp_ws"][bass.ds(l, 1), :, :, :].rearrange("a g t s -> t (a g) s"))
                prm_load(lng[:, :], t["gmlp_ln_g"][bass.ds(l, 1), :].to_broadcast([P, MIX]))
                prm_load(lnb[:, :], t["gmlp_ln_b"][bass.ds(l, 1), :].to_broadcast([P, MIX]))
                prm_load(sinks[:, :], t["swa_sinks"][bass.ds(l, 1), :].to_broadcast([P, 8]))

                n = 0
                for c0 in [512 * p for p in range(9)] + [None]:
                    if c0 is None:
                        load(l, n, split_k(n, w_in2, l * D_MODEL, 8, SWA_C0 + 512, 256))
                        n += 1
                        continue
                    for k0 in (0, 4):
                        load(l, n, split_k(n, w_in2, l * D_MODEL + k0 * P, 4, c0, 512))
                        n += 1
                for kind, b, hf, a, _ in MIX_STEPS:
                    if kind == "gate":
                        load(l, n, split_k(n, w_in2, l * D_MODEL + a * 4 * P, 4, GATE_C0 + b * D_MODEL + hf * 512, 512))
                    else:
                        load(l, n, split_k(n, w_br2, l * 4 * MIX + b * MIX, 4, hf * 512, 512))
                    n += 1
                for hf in range(2):
                    for k0 in (0, 4):
                        load(l, n, split_k(n, w_out2, l * D_MODEL + k0 * P, 4, hf * 512, 512))
                        n += 1
                assert n == U_FF

                def ff_panel(j, n, count):
                    for k0 in (0, 4):
                        m = n + k0 // 4
                        sp.wait_ge(unit_done.sem, count + k0 // 4 + 1)
                        for dst, src in gate_up(m, w_ffi2, l * D_MODEL, k0 * P, j, D_FF):
                            sp.dma_start(dst, src).then_inc(w_full[m % SLOTS].sem, 16)
                ff_panel(0, U_FF, l * L_UNITS + U_FF)
                with sp.Fori(0, FF_PANELS // 2) as i:
                    for a in (1, 2):
                        ff_panel(i * 2 + a, U_FF + 2 * a, l * L_UNITS + i * 4 + (U_FF + 2 * a))
                n = U_DOWN
                for u in range(FF_KT // 2):
                    load(l, n, split_k(n, w_ffo2, l * D_FF + u * 2 * P, 2, 0, D_MODEL))
                    n += 1
                assert n == L_UNITS
            sp.wait_ge(*unit_done(DEPTH, 1))
            for name, tile in c2.items():
                sp.dma_start(tile, t[name]).then_inc(c2_in, 16)
            sp.dma_start(w2c, t["a_cmp_w2_2"][0].rearrange("v (k p) c -> p v k c", p=P)).then_inc(c2_in, 16)
            sp.dma_start(b2c, t["a_cmp_b2_2"].rearrange("o v c -> o (v c)").to_broadcast([P, 2 * HD])
                         .rearrange("p (v c) -> p v c", v=2)).then_inc(c2_in, 16)
            sp.dma_start(gate_b, t["a_gate_b_2"].to_broadcast([P, 36])).then_inc(c2_in, 16)
            sp.dma_start(f_b, t["b_fgate_2"].unsqueeze(0).to_broadcast([P, N_MIX])).then_inc(c2_in, 16)
            sp.dma_start(final_g, t["final_norm_2"].unsqueeze(0).to_broadcast([P, D_MODEL])).then_inc(c2_in, 16)
            sp.dma_start(mem, t["mem_2"][0].rearrange("(t p) d -> p t d", p=P)).then_inc(mem_in, 16)
            for name, r0, pattern in (("attn_norm_2", N2_ATT, "l (r p) -> (l r) p"), ("ffn_norm_2", N2_FFN, "l (r p) -> (l r) p"),
                                      ("mem_norm_2", N2_MEM, "l (r p) -> (l r) p"), ("kv_norm_2", N2_KV, "(r p) -> r p"),
                                      ("a_cmp_b1_2", N2_B1, "o v (r p) -> (o v r) p")):
                src = t[name].rearrange(pattern, p=P)
                sp.dma_start(prm2_raw[r0:r0 + src.shape[0], :], src).then_inc(prm2_in, 16)
            sp.dma_start(prm2_raw[N2_POS:N2_END, :], t["a_cmp_pos_2"].rearrange("o v (m j) d -> (o v m) (j d)", j=2)).then_inc(prm2_in, 16)
            for f in range(2):
                sp.dma_start(cv_raw[:, 4 * f:4 * f + 3, :], t["conv_w_2"][f].rearrange("k (r p) -> r k p", p=P)).then_inc(prm2_in, 16)
                sp.dma_start(cv_raw[:, 4 * f + 3, :], t["conv_b_2"][f].rearrange("(r p) -> r p", p=P)).then_inc(prm2_in, 16)

            def load_panel(n, w, c0, cols, r0=0):
                for a in range(2):
                    load(DEPTH, n + a, split_k(n + a, w, r0 + a * 4 * P, 4, c0, cols))

            def load_ffn(f):
                w_up2 = t["w_up_2"][f]
                for j in range(2):
                    for a in range(2):
                        m = U2_UP[f] + 2 * j + a
                        load(DEPTH, m, gate_up(m, w_up2, 0, 4 * P * a, j, D_FF))
                with sp.Fori(0, (FF_PANELS - 3) // 2) as i:
                    for b in (2, 3):
                        for a in range(2):
                            m = U2_UP[f] + 2 * b + a
                            sp.wait_ge(unit_done.sem, DEPTH * L_UNITS + m + 1 + i * 4)
                            for dst, src in gate_up(m, w_up2, 0, 4 * P * a, i * 2 + b, D_FF):
                                sp.dma_start(dst, src).then_inc(w_full[m % SLOTS].sem, 16)
                for a in range(2):
                    m = U2_UP[f] + 20 + a
                    load(DEPTH, m, gate_up(m, w_up2, 0, 4 * P * a, 10, D_FF))
                for u in range(FF_KT // 2):
                    load(DEPTH, U2_DOWN[f] + u, split_k(U2_DOWN[f] + u, t["w_down_2"][f], u * 2 * P, 2, 0, D_MODEL))

            for q, c0 in enumerate((0, 512, 1024, 1536)):
                load_panel(U2_PANEL[q], t["a_w_in_2"][0], c0, min(512, A_IN - c0))
            for f in range(2):
                load_panel(U2_PANEL[Q_MEM + f], t["w_mem_kv_2"][f], 0, 512)
            for kv in range(2):
                for a in range(2):
                    n = U2_CMP + 2 * kv + a
                    load(DEPTH, n, split_k(n, t["a_cmp_w1_2"][0, kv], a * 8 * P, 8, 0, CMP_HID))
            for f in range(2):
                if f:
                    for q, c0 in enumerate((0, 512, 1024, 1536)):
                        load_panel(U2_PANEL[Q_SHARED + q], t["w_kv_shared_2"], c0, min(512, SHARED - c0))
                    for q in range(2):
                        load_panel(U2_PANEL[Q_IN + q], t["b_w_in_2"][0], 512 * q, 512)
                for hf in range(2):
                    load_panel(U2_PANEL[Q_OUT[f] + hf], t["w_o_2"][f], 512 * hf, 512)
                load_ffn(f)
            sp.wait_ge(*h_ready(DEPTH, NORM_FINAL + 1))
            sp.dma_start(out[0].rearrange("(t p) d -> p t d", p=P), h[:, :, :]).then_inc(out_done, 16)
            sp.wait_ge(out_done, 16)

        @block.gpsimd
        def _(g):
            ch = Chain(g, g_chain)
            nc.gpsimd.memset(half[:, :], -0.5).then_inc(half_ready, 1)
            nc.gpsimd.memset(uTp[:, :, 0:30], 0.0).then_inc(pad_ready, 1)
            g.wait_ge(brow_ready, 1)
            g.dma_start(bass.AP(scratch.tensor, scratch.offset, [[P * SKEW + TRI, 8], [SKEW + 1, P], [1, TRI]]),
                        vrow[:, :].unsqueeze(1).to_broadcast([8, P, TRI])).then_inc(brow_out, 16)
            g.wait_ge(brow_out, 16)
            for c0, off in ((0, 127), (P, 255)):
                src = bass.AP(scratch.tensor, scratch.offset + off, [[SKEW, P], [P * SKEW + TRI, 8], [1, P]])
                g.dma_start(bias[:, :, c0:c0 + P], src).then_inc(bias_in, 16)

            def rsqrt(src, dst, n, scale, done):
                g.sem_inc(hold_g, 1)
                ch.link(nc.gpsimd.tensor_scalar(var[:, 0:n], src, scale, EPS, ALU.mult, ALU.add))
                nc.gpsimd.tensor_tensor(dst, var[:, 0:n], half[:, 0:n], ALU.pow).then_inc(done, 1)

            def norm(layer, k):
                g.wait_ge(*sumsq(layer, k + 1))
                rsqrt(ss[:, :], rstd[:, :], NT, 1.0 / D_MODEL, rstd_ready.sem)

            def split_lo(n, b, before, size):
                g.wait_ge(w_hi_ready, before * 2 + (b + 1))
                g.sem_inc(hold_g, 1)
                nc.gpsimd.tensor_tensor(half_of(w_lo, n, b, size), half_of(ring, n, b, size),
                                        hi_half(n, b, size).bitcast(F32), ALU.subtract).then_inc(w_lo_ready, 1)

            def layer_lo(first, last):
                for h_ in range(2 * first[0] + first[1], 2 * last[0] + last[1] + 1):
                    split_lo(h_ // 2, h_ % 2, l * L_UNITS + h_ // 2, HALF_W)

            def ffn_lo(n0, before, second):
                rest = 3 * FF_PANELS - 2
                with g.Fori(0, rest // 4) as i:
                    for u in range(2, 6):
                        for b in range(2):
                            split_lo(n0 + u, b, before + i * 4 + u, HALF_W)
                for u in range(2 + rest // 4 * 4, 2 + rest):
                    for b in range(2):
                        split_lo(n0 + u, b, before + u, HALF_W)

            def second_lo(first, last):
                for h_ in range(2 * first[0] + first[1], 2 * last[0] + last[1] + 1):
                    n = h_ // 2
                    if n not in U2_WHOLE:
                        split_lo(n, h_ % 2, DEPTH * L_UNITS + split_before(n), half_size(n, True))

            g.wait_ge(half_ready, 1)
            with g.Fori(0, DEPTH) as l:
                layer_lo((0, 0), (1, 0))
                norm(l, 0)
                layer_lo((1, 1), (14, 0))
                g.wait_ge(*ry_stat(l, 1))
                rsqrt(mv[:, :, 1], rs8[:, 0:8], 8, 1.0, ry_rstd.sem)
                layer_lo((14, 1), (17, 1))
                g.wait_ge(*gv_stat(l, 1))
                rsqrt(mv[:, 0:2, 1], rs8[:, 0:2], 2, 1.0, gv_rstd.sem)
                layer_lo((18, 0), (20, 1))
                g.wait_ge(*sw_sumsq(l, 1))
                rsqrt(ssw[:, 0:20], rs8[:, 0:20], 20, 1.0 / HD, sw_rstd.sem)
                layer_lo((21, 0), (37, 1))
                g.wait_ge(*cv_stat(l, 1))
                rsqrt(mv[:, 0:2, 1], rs8[:, 0:2], 2, 1.0, cv_rstd.sem)
                layer_lo((38, 0), (U_FF + 1, 0))
                norm(l, 1)
                layer_lo((U_FF + 1, 1), (U_FF + 1, 1))
                ffn_lo(U_FF, l * L_UNITS + U_FF, False)
                ch.restart()
            second_lo((0, 0), (1, 0))
            norm(DEPTH, NORM_ATT[0])
            second_lo((1, 1), (2, 1))
            norm(DEPTH, NORM_MEM)
            second_lo((3, 0), (U2_UP[0] + 1, 0))
            for f in range(2):
                up = U2_UP[f]
                norm(DEPTH, NORM_FFN[f])
                second_lo((up + 1, 1), (up + 1, 1))
                ffn_lo(up, DEPTH * L_UNITS + split_before(up), True)
                if f == 0:
                    end = up + 3 * FF_PANELS
                    second_lo((end, 0), (end + 1, 0))
                    norm(DEPTH, NORM_ATT[1])
                    second_lo((end + 1, 1), (U2_UP[1] + 1, 0))
            norm(DEPTH, NORM_FINAL)

        @block.tensor
        def _(pe):
            mm = nc.tensor.matmul
            tr = nc.tensor.transpose
            pe.wait_ge(const_in, 16 * len(const))
            pe.sem_inc(unit_done.sem, SLOTS)
            pe.sem_inc(ff_tr.sem, AHEAD)
            pe.sem_inc(first_used, USED_AHEAD)
            pe.wait_ge(rel_in, 16)
            mm(T[3][0:8, 0:TRI], rel[:, :], const["bucket"][:, :], start=True, stop=True).then_inc(brow_psum, 1)
            pe.wait_ge(brow_ready, 1)

            def turn(bank, at, src, s, c0):
                return tr(bank[:, at:at + P], src[:, s, c0:c0 + P], ident[:, :])

            def rows8(src, banks):
                for c in range(4):
                    for s in range(NT):
                        ins = turn(banks[c // 2], (c % 2) * SEQ + s * P, src, s, c * P)
                return ins

            def rows16(src, done):
                for c in range(8):
                    for s in range(NT):
                        ins = turn(T[c // 2], (c % 2) * SEQ + s * P, src, s, c * P)
                    if c % 2:
                        ins.then_inc(done, 1)

            def multiply(banks, act, k0, weights, first, last):
                for s in range(NT):
                    for kk, w in enumerate(weights):
                        ins = mm(banks[s][:, 0:w.shape[-1]], act(k0 + kk, s), w,
                                 start=first and kk == 0, stop=last and kk == len(weights) - 1)
                ins.then_inc(unit_done.sem, 1)

            def three(bank, act, k, s, hi, lo, first, last):
                a_hi, a_lo = (a[:, k, s * P:(s + 1) * P] for a in act)
                mm(bank, a_hi, hi, start=first, stop=False)
                mm(bank, a_hi, lo, start=False, stop=False)
                return mm(bank, a_lo, hi, start=False, stop=last)

            def multiply_split(banks, act, n, before, k0, width, first, last, size=HALF_W):
                tiles = size // width
                for b in range(2):
                    pe.wait_ge(w_lo_ready, before * 2 + (b + 1))
                    hi, lo = hi_half(n, b, size), half_of(w_lo, n, b, size)
                    for s in range(NT):
                        for kk in range(tiles):
                            cols = slice(kk * width, (kk + 1) * width)
                            ins = three(banks[s][:, 0:width], act, k0 + tiles * b + kk, s, hi[:, cols], lo[:, cols],
                                        first and b + kk == 0, last and b == 1 and kk == tiles - 1)
                    ins.then_inc(unit_done.sem if b else first_used, 1)

            def down_unit(n, u, before):
                for b in range(2):
                    k = 2 * u + b
                    pe.wait_ge(w_lo_ready, before * 2 + (b + 1))
                    for s in range(NT):
                        for hf in range(2):
                            cols = slice(hf * 512, (hf + 1) * 512)
                            ins = three(G[2 * s + hf][:, :], (uT_hi, uT_lo), k, s, hi_half(n, b, HALF_W)[:, cols],
                                        half_of(w_lo, n, b, HALF_W)[:, cols], k == 0, k == FF_KT - 1)
                    ins.then_inc(unit_done.sem if b else first_used, 1)

            turned = (hT_hi, hT_lo)

            with pe.Fori(0, DEPTH) as l:
                def banks_of(q):
                    if q >= 2:
                        pe.wait_ge(*z_a(l, taken("A", q - 2)))
                        pe.wait_ge(*z_d(l, taken("D", q - 2)))
                    return G[2 * (q % 2)], G[2 * (q % 2) + 1]

                def half_panel(q, a):
                    n = end_of(q) - 2 + a
                    multiply_split(banks_of(q), turned, n, l * L_UNITS + n, 4 * a, 512, a == 0, a == 1)

                def panel(q):
                    half_panel(q, 0)
                    half_panel(q, 1)

                pe.wait_ge(*prm_in(l, 16 * PRM_LOADS))
                for c in range(4):
                    tr(T[2][:, c * P:(c + 1) * P], ws_raw[:, c, :], ident[:, :])
                tr(T[1][:, 0:124], cw_raw[:, :], ident[0:124, 0:124])
                ins = tr(T[0][:, 0:R_END], prm_raw[:, :], ident[0:R_END, 0:R_END])
                ins.then_inc(prm_psum.sem, 1)
                pe.wait_ge(*prm_ready(l, 1))

                pe.wait_ge(*h_ready(l, 1))
                rows16(h, hT_psum.sem)
                pe.wait_ge(*hT_d(l, 1))
                for q in range(4):
                    panel(q)
                pe.wait_ge(*rot_ready(l, 1))
                rows16(h, rqk_psum.sem)
                panel(4)
                pe.wait_ge(*qT_ready(l, 1))
                pe.wait_ge(*kT_ready(l, 1))
                for i in range(4):
                    q_h, k_h = qkT[:, i // 2, (i % 2) * SEQ:(i % 2 + 1) * SEQ], kTt[:, i // 2, (i % 2) * SEQ:(i % 2 + 1) * SEQ]
                    mm(T[i][:, 0:SEQ], k_h[:, 0:P], q_h, start=True, stop=True)
                    mm(T[i][:, SEQ:TRI], k_h[:, P:SEQ], q_h[:, P:SEQ], start=True, stop=True).then_inc(rsc_psum.sem, 1)
                panel(5)
                pe.wait_ge(*rsc_ready(l, 4))
                pe.wait_ge(*z_a(l, taken("A", 2)))
                pe.wait_ge(*z_d(l, taken("D", 2)))
                for i in range(4):
                    v = [zr[:, s, 2, i * P:(i + 1) * P] for s in range(NT)]
                    cols = slice(i * P, (i + 1) * P)
                    mm(T[0][:, cols], scr[:, i, 0:P], v[0], start=True, stop=True)
                    mm(T[1][:, cols], scr[:, i, P:SEQ], v[0], start=True, stop=False)
                    ins = mm(T[1][:, cols], scr[:, i, SEQ:TRI], v[1], start=False, stop=True)
                ins.then_inc(ry_psum.sem, 1)
                panel(6)
                pe.wait_ge(*cu_ready(l, 1))
                rows8(mix, T[2:4]).then_inc(cu_psum.sem, 1)
                panel(7)
                pe.wait_ge(*rya_ready(l, 1))
                rows8(yr, T[0:2]).then_inc(rya_psum.sem, 1)
                panel(8)
                pe.wait_ge(*gv_ready(l, 1))
                pe.wait_ge(*cuT_ready(l, 1))
                for s in range(NT):
                    for c in range(4):
                        ins = mm(T[2 + s][:, c * P:(c + 1) * P], wsT[:, c, :], tmp[:, s, c * P:(c + 1) * P],
                                 start=True, stop=True)
                ins.then_inc(gs_psum.sem, 1)
                q, n = 9, end_of(9) - 1
                multiply_split(banks_of(q), turned, n, l * L_UNITS + n, 0, 256, True, True)
                pe.wait_ge(*gy_ready(l, 1))
                rows8(yg, T[2:4]).then_inc(gy_psum.sem, 1)

                def scores(i):
                    part = slice((i % 2) * HD, (i % 2 + 1) * HD)
                    q_h, k_h = swq[part, i // 2, :], swk[part, i // 4, :]
                    if i:
                        pe.wait_ge(*sw_nm(l, i))
                    mm(T[0][:, 0:P], q_h[:, 0:P], k_h[:, 0:P], start=True, stop=True)
                    mm(T[0][:, P:TRI], q_h[:, P:SEQ], k_h, start=True, stop=True).then_inc(sw_sc.sem, 1)

                def probs_T(i):
                    pe.wait_ge(*sw_exp(l, i + 1))
                    if i:
                        pe.wait_ge(*sw_pT(l, i))
                    for c in range(3):
                        ins = tr(T[1][:, c * P:(c + 1) * P], S[:, i % 4, c * P:(c + 1) * P], ident[:, :])
                    ins.then_inc(sw_tr.sem, 1)

                def values(i):
                    pe.wait_ge(*sw_pT(l, i + 1))
                    v = [zs[:, s, 640 + (i // 4) * HD:640 + (i // 4 + 1) * HD] for s in range(NT)]
                    cols = slice(i * HD, (i + 1) * HD)
                    p = pT[:, i % 2, :]
                    mm(T[2][:, cols], p[:, 0:P], v[0], start=True, stop=True)
                    mm(T[3][:, cols], p[:, P:SEQ], v[0], start=True, stop=False)
                    mm(T[3][:, cols], p[:, SEQ:TRI], v[1], start=False, stop=True).then_inc(sw_o.sem, 1)

                for u, (kind, b, hf, a, q) in enumerate(MIX_STEPS):
                    if kind == "gate":
                        half_panel(q, a)
                    else:
                        if hf == 0:
                            pe.wait_ge(*{0: ysT_ret, 1: ysT_conv, 2: ysT_gmlp, 3: ysT_swa}[b](l, 1))
                        act = tuple(y[:, PLACE[b]] for y in (ysT_hi, ysT_lo))
                        multiply_split(banks_of(q), act, U_MIX + u, l * L_UNITS + (U_MIX + u), 0, 512, True, True)
                    if u == 0:
                        pe.wait_ge(*sw_norm(l, 1))
                        pe.wait_ge(*ysT_ret(l, 1))
                        pe.wait_ge(*ysT_gmlp(l, 1))
                        rows8(tmp, T[0:2])
                        for kv in range(2):
                            for s in range(NT):
                                ins = tr(T[2][:, kv * SEQ + s * P:kv * SEQ + (s + 1) * P],
                                         kdup[:, s, kv * P:(kv + 1) * P], ident[:, :])
                        ins.then_inc(sw_psum.sem, 1)
                    if u == 1:
                        pe.wait_ge(*sw_qT(l, 1))
                        pe.wait_ge(*sw_kT(l, 1))
                    if 1 <= u <= 8:
                        scores(u - 1)
                    if 2 <= u <= 9:
                        probs_T(u - 2)
                    if 3 <= u <= 10:
                        values(u - 3)
                    if u == 12:
                        pe.wait_ge(*sy_ready(l, 1))
                        rows8(h, T[0:2]).then_inc(sy_psum.sem, 1)
                    if u == 16:
                        pe.wait_ge(*cv_ready(l, 1))
                        for s in range(NT):
                            for c in range(4):
                                ins = tr(T[2 + s][:, c * P:(c + 1) * P], cacc[:, c, s * P:(s + 1) * P], ident[:, :])
                        ins.then_inc(cv_psum.sem, 1)

                    if u == 19:
                        pe.wait_ge(*cn_ready(l, 1))
                        pe.wait_ge(*ysT_swa(l, 1))
                        rows8(h[:, :, MIX:2 * MIX], T[0:2]).then_inc(cn_psum.sem, 1)
                pe.wait_ge(*z_d(l, taken("D", P_OUT - 1)))
                rows16(mix, mixT_psum.sem)
                pe.wait_ge(*mixT_d(l, 1))
                panel(P_OUT)
                panel(P_OUT + 1)

                pe.wait_ge(*h_ready(l, 2))
                rows16(h, hT_psum.sem)
                pe.wait_ge(*hT_d(l, 2))

                def ff_panel(parity, n, more, j):
                    if j is not None:
                        pe.wait_ge(ff_u.sem, j)
                    for a in range(2):
                        multiply_split(G[2 * parity:2 * parity + 2], turned, n + a, l * L_UNITS + more + (n + a),
                                       4 * a, 512, a == 0, a == 1)

                def ff_turn(parity, done, free):
                    pe.wait_ge(ff_u.sem, done)
                    if free is not None:
                        pe.wait_ge(ff_uT.sem, free)
                    for c in range(2):
                        for s in range(NT):
                            ins = turn(T[parity], c * SEQ + s * P, uu[:, parity, :, :], s, c * P)
                    ins.then_inc(ff_tr.sem, 1)

                panels_before = l * FF_PANELS + AHEAD
                ff_panel(0, U_FF, 0, None)
                with pe.Fori(0, FF_PANELS // 2) as i:
                    ff_panel(1, U_FF + 2, i * 4, panels_before + i * 2)
                    ff_turn(0, panels_before + i * 2 + 1, panels_before + i * 2)
                    ff_panel(0, U_FF + 4, i * 4, panels_before + i * 2 + 1)
                    ff_turn(1, panels_before + i * 2 + 2, panels_before + i * 2)
                ff_turn(0, panels_before + FF_PANELS, panels_before + FF_PANELS - 1)
                pe.wait_ge(*ff_u(l, FF_PANELS))
                for u in range(FF_KT // 2):
                    n = U_DOWN + u
                    if u == 0:
                        pe.wait_ge(*ff_uT(l, FF_PANELS - 1))
                    if u == FF_KT // 2 - 1:
                        pe.wait_ge(*ff_uT(l, FF_PANELS))
                    down_unit(n, u, l * L_UNITS + n)

            def arrived2(n):
                pe.wait_ge(*w_full[n % SLOTS](DEPTH, FILL * (n // SLOTS + 1)))

            def unit2(n, k, cols):
                return ring[:, n % SLOTS, 0:k * cols].rearrange("p (k c) -> p k c", k=k)

            def panel2(q, src, cols=512):
                if q % 2 or q not in (Q_OUT[0], Q_SHARED, Q_OUT[1]):
                    if q >= 2:
                        pe.wait_ge(z2_a, taken2("A", q - 2))
                        pe.wait_ge(z2_d, taken2("D", q - 2))
                for a in range(2):
                    n = U2_PANEL[q] + a
                    if n not in U2_WHOLE:
                        multiply_split(G[2 * (q % 2):2 * (q % 2) + 2], src, n, DEPTH * L_UNITS + split_before(n), 4 * a, cols,
                                       a == 0, a == 1, 2 * cols)
                        continue
                    arrived2(n)
                    w = unit2(n, 4, cols)
                    multiply(G[2 * (q % 2):2 * (q % 2) + 2], lambda k, s: src[:, k, s * P:(s + 1) * P], 4 * a,
                             [w[:, k, :] for k in range(4)], a == 0, a == 1)

            def normed(k):
                pe.wait_ge(*h_ready(DEPTH, k + 1))
                rows16(h, hT_psum.sem)

            def have_hT(k):
                if k == NORM_MEM:
                    pe.wait_ge(memT_a, 1)
                pe.wait_ge(*hT_d(DEPTH, k + 1))

            def twice(cols):
                return cols.unsqueeze(1).to_broadcast([P, 2, HD])

            def turn_pair(bank, half_, src, s, c0):
                return tr(bank[:, half_ * SEQ + s * P:half_ * SEQ + (s + 1) * P], src[:, s, c0:c0 + P], ident[:, :])

            pe.wait_ge(prm2_in, 16 * 10)
            tr(T[0][:, 0:N2_END], prm2_raw, ident[0:N2_END, 0:N2_END])
            for a in range(8):
                ins = tr(T[1][:, 44 * a:44 * (a + 1)], cv_raw[:, a, :], ident[0:44, 0:44])
            ins.then_inc(prm2_psum, 1)
            pe.wait_ge(prm2_ready, 1)

            def attention(f, row_terms=None):
                jobs = [j for j, job in enumerate(JOBS) if job[0] == f]

                def scores(j):
                    _, kind, i = JOBS[j]
                    bank = T[j % 2]
                    part = slice((i % 2) * HD, (i % 2 + 1) * HD)
                    if j >= 2:
                        pe.wait_ge(at_exp if JOBS[j - 2][1] == "mem" else at_nm, j - 1)
                    if kind == "mem":
                        for s in range(NT):
                            ins = mm(bank[:, s * SEQ:(s + 1) * SEQ], qmT[part, i // 2, s * P:(s + 1) * P],
                                     mkT[f][part, i // 2, :], start=True, stop=True)
                        ins.then_inc(at_sc, 1)
                        return
                    q_h = qT2[part, i // 2, :]
                    k_h = kT2[part, {"slc": i // 6, "win": 2 + i // 6, "fgt": i // 2}[kind], :]
                    fgt = kind == "fgt"
                    mm(bank[:, 0:P], q_h[:, 0:P], k_h[:, 0:P], start=True, stop=not fgt)
                    if fgt:
                        n0, n1 = (nlf[:, s, i:i + 1].to_broadcast([P, P]) for s in range(NT))
                        mm(bank[:, 0:P], n0, upones[:, 0:P], start=False, stop=True)
                    ins = mm(bank[:, P:TRI], q_h[:, P:SEQ], k_h, start=True, stop=not fgt)
                    if fgt:
                        mm(bank[:, P:TRI], n0, upones, start=False, stop=False)
                        ins = mm(bank[:, SEQ:TRI], n1, upones[:, 0:P], start=False, stop=True)
                    ins.then_inc(at_sc, 1)

                def probs_T(j):
                    pe.wait_ge(at_exp, j + 1)
                    if j >= 2:
                        pe.wait_ge(at_pT, j - 1)
                    for c in range(4 if JOBS[j][1] == "mem" else 3):
                        ins = tr(T[2 + j % 2][:, c * P:(c + 1) * P], S4[:, j % 4, c * P:(c + 1) * P], ident[:, :])
                    ins.then_inc(at_tr, 1)

                def values(j):
                    _, kind, i = JOBS[j]
                    pe.wait_ge(at_pT, j + 1)
                    if i == 0:
                        pe.wait_ge(at_sum, groups_before(j) + 1)
                    p = pT4[:, j % 2, :]
                    if kind == "mem":
                        cols = slice(i * HD, (i + 1) * HD)
                        for s in range(NT):
                            for c in range(2):
                                ins = mm(G[2 * s][:, cols], p[:, (2 * s + c) * P:(2 * s + c + 1) * P],
                                         mkv[f][:, c, 256 + i * HD:256 + (i + 1) * HD], start=c == 0, stop=c == 1)
                        ins.then_inc(at_o, 1)
                        return
                    if kind == "fgt":
                        v_h = [zk[:, s, MIX_W + i * HD:MIX_W + (i + 1) * HD] for s in range(NT)]
                    else:
                        c0 = {"slc": 1152, "win": 1408}[kind] + (i // 6) * HD
                        v_h = [z2[:, s, c0:c0 + HD] for s in range(NT)]
                    cols = slice((i % 6) * HD, (i % 6 + 1) * HD)
                    mm(G[i // 6][:, cols], p[:, 0:P], v_h[0], start=True, stop=True)
                    mm(G[2 + i // 6][:, cols], p[:, P:SEQ], v_h[0], start=True, stop=False)
                    mm(G[2 + i // 6][:, cols], p[:, SEQ:TRI], v_h[1], start=False, stop=True).then_inc(at_o, 1)

                for step in range(len(jobs) + 2):
                    if step < len(jobs):
                        scores(jobs[step])
                    if 1 <= step <= len(jobs):
                        probs_T(jobs[step - 1])
                    if step >= 2:
                        values(jobs[step - 2])

            def out_and_ffn(f):
                pe.wait_ge(at_sum, 1 + (3 if f == 0 else 5))
                rows16(h, oT_psum)
                pe.wait_ge(oT_d, f + 1)
                panel2(Q_OUT[f], turned)
                panel2(Q_OUT[f] + 1, turned)
                normed(NORM_FFN[f])
                have_hT(NORM_FFN[f])
                done = f * FF_PANELS

                def up(j, parity, n, more):
                    pe.wait_ge(cf_za, done + j - 1)
                    pe.wait_ge(cf_zd, done + j - 1)
                    up_units(parity, n, more)

                def up_units(parity, n, more):
                    for a in range(2):
                        multiply_split(G[2 * parity:2 * parity + 2], turned, n + a,
                                       more + (DEPTH * L_UNITS + split_before(n + a)), 4 * a, 512, a == 0, a == 1)

                def channels(j, parity, first=False):
                    pe.wait_ge(cf_za, done + j + 1)
                    pe.wait_ge(cf_zd, done + j + 1)
                    if not first:
                        pe.wait_ge(cf_cv, AHEAD + done + j - 1)
                    for b in range(2):
                        for c in range(2):
                            for s in range(NT):
                                ins = turn(T[2 * parity + b], c * SEQ + s * P, zcv[:, parity, :, :], s, (2 * b + c) * P)
                        ins.then_inc(cf_tr, 1)

                n = U2_UP[f]
                up_units(0, n, 0)
                up_units(1, n + 2, 0)
                channels(0, 0, True)
                with pe.Fori(0, (FF_PANELS - 3) // 2) as i:
                    up(i * 2 + 2, 0, n + 4, i * 4)
                    channels(i * 2 + 1, 1)
                    up(i * 2 + 3, 1, n + 6, i * 4)
                    channels(i * 2 + 2, 0)
                up(10, 0, n + 20, 0)
                channels(9, 1)
                channels(10, 0)
                for u in range(FF_KT // 2):
                    if u == 0 or u >= 8:
                        pe.wait_ge(cf_uT, done + (8 if u == 0 else u + 1))
                    n = U2_DOWN[f] + u
                    down_unit(n, u, DEPTH * L_UNITS + split_before(n))

            normed(NORM_ATT[0])
            have_hT(NORM_ATT[0])
            for q in range(2):
                panel2(q, turned)
            normed(NORM_MEM)
            panel2(2, turned)
            have_hT(NORM_MEM)
            panel2(3, turned, A_IN - 1536)
            pe.wait_ge(kvd_ready, 1)
            for kv in range(2):
                for g2 in range(2):
                    for s in range(NT):
                        ins = tr(T[kv][:, g2 * SEQ + s * P:g2 * SEQ + (s + 1) * P],
                                 kvd[:, s, (2 * kv + g2) * P:(2 * kv + g2 + 1) * P], ident[:, :])
            ins.then_inc(cmpT_psum, 1)
            panel2(Q_MEM, memT[0])
            panel2(Q_MEM + 1, memT[1])
            pe.wait_ge(blocks_ready, 1)
            for kv in range(2):
                n = U2_CMP + 2 * kv
                arrived2(n)
                arrived2(n + 1)
                for ht in range(2):
                    for m in range(16):
                        w = unit2(n + m // 8, 8, CMP_HID)
                        ins = mm(T[2][:, (2 * kv + ht) * HD:(2 * kv + ht + 1) * HD], w[:, m % 8, ht * P:(ht + 1) * P],
                                 blocks[:, kv, m, :, :], start=m == 0, stop=m == 15)
                        if ht == 1 and m % 8 == 7:
                            ins.then_inc(unit_done.sem, 1)
            pe.wait_ge(rot2, 1)
            pe.wait_ge(u2_a, 1)
            pe.wait_ge(u2_d, 1)
            for c in range(4):
                for s in range(NT):
                    ins = turn_pair(T[c // 2], c % 2, h, s, c * P)
            ins.then_inc(turn_psum, 1)
            pe.wait_ge(hid_ready, 1)
            for kv in range(2):
                for g2 in range(2):
                    for ht in range(2):
                        ins = mm(T[3][:, (2 * kv + g2) * HD:(2 * kv + g2 + 1) * HD],
                                 h1T[:, kv, ht, g2, :],
                                 w2c[:, kv, ht, :], start=ht == 0, stop=ht == 1)
            ins.then_inc(kvc_psum, 1)
            pe.wait_ge(kcr_ready, 1)
            for g2 in range(2):
                ins = tr(T[3][:, g2 * 16:g2 * 16 + N_CMP], kcr[0:N_CMP, g2, :],
                         ident[0:N_CMP, 0:N_CMP])
            ins.then_inc(kcT_psum, 1)
            for c in range(4, 6):
                for s in range(NT):
                    ins = turn_pair(T[2], c % 2, h, s, c * P)
            ins.then_inc(turn_psum, 1)
            pe.wait_ge(turn_a, 1)
            for c in range(2):
                for s in range(NT):
                    ins = turn_pair(T[1], c, z2, s, 1572 + c * P)
            ins.then_inc(turn_psum, 1)
            pe.wait_ge(kcT_ready, 1)
            for br in range(2):
                for g2 in range(2):
                    for s in range(NT):
                        c0 = (2 * br + g2) * P
                        ins = tr(T[3 * br][:, g2 * SEQ + s * P:g2 * SEQ + (s + 1) * P], kd2[:, s, c0:c0 + P], ident[:, :])
            ins.then_inc(turn_psum, 1)
            pe.wait_ge(turn_d, 1)
            pe.wait_ge(turn_a, 2)
            pe.wait_ge(z2_a, taken2("A", Q_MEM + 1))
            pe.wait_ge(z2_d, taken2("D", Q_MEM + 1))
            for f in range(2):
                for c in range(2):
                    for s in range(NT):
                        ins = turn_pair(T[2 - f], c, mkv[f], s, c * P)
            ins.then_inc(turn_psum, 1)
            pe.wait_ge(turn_a, 4)
            pe.wait_ge(turn_d, 2)
            for s in range(NT):
                for i in range(N_MIX):
                    part = slice((i % 2) * HD, (i % 2 + 1) * HD)
                    at_c = (s * 6 + i // 2) * N_CMP
                    ins = mm(T[i % 2][:, at_c:at_c + N_CMP], qT2[part, i // 2, s * P:(s + 1) * P],
                       kcT[part, i // 6, 0:N_CMP], start=True, stop=True)
            ins.then_inc(csc_psum, 1)
            pe.wait_ge(cprob, 1)
            for s in range(NT):
                for c in range(3):
                    ins = tr(T[2 + s][:, c * P:(c + 1) * P], Sc[:, s, 4 * c:4 * c + 4, :].rearrange("p h n -> p (h n)"), ident[:, :])
            ins.then_inc(cprobT, 1)
            pe.wait_ge(pcT_ready, 1)
            for s in range(NT):
                for i in range(N_MIX):
                    part = slice(32 * (i % 4), 32 * (i % 4) + N_CMP)
                    at_c = (s * 3 + i // 4) * HD
                    ins = mm(G[i % 4][:, at_c:at_c + HD], pcT[part, s, i // 4, :],
                             kvc[part, 1, i // 6, :], start=True, stop=True)
            ins.then_inc(at_o, 1)
            attention(0)
            out_and_ffn(0)

            normed(NORM_ATT[1])
            have_hT(NORM_ATT[1])
            for q in range(4):
                panel2(Q_SHARED + q, (hsT_hi, hsT_lo), min(512, SHARED - 512 * q))
            for q in range(2):
                panel2(Q_IN + q, turned)
            pe.wait_ge(z2_a, taken2("A", Q_IN + 1))
            pe.wait_ge(z2_d, taken2("D", Q_IN + 1))
            for c in range(8):
                for s in range(NT):
                    ins = turn_pair(T[c // 2], c % 2, zq, s, c * P)
            ins.then_inc(turn_psum, 1)
            pe.wait_ge(turn_a, 5)
            pe.wait_ge(turn_d, 3)
            for c in range(6):
                for s in range(NT):
                    ins = turn_pair(T[c // 2], c % 2, zk, s, c * P)
            ins.then_inc(turn_psum, 1)
            pe.wait_ge(fg_ready, 1)
            mm(T[3][:, 0:N_MIX], upones[:, 0:P], nlf[:, 0, :], start=True, stop=True)
            mm(T[3][:, N_MIX:2 * N_MIX], upones[:, 0:P], nlf[:, 1, :], start=True, stop=False)
            mm(T[3][:, N_MIX:2 * N_MIX], upones[:, P:SEQ], nlf[:, 0, :], start=False, stop=True).then_inc(fg_cum, 1)
            pe.wait_ge(turn_a, 6)
            pe.wait_ge(turn_d, 4)
            attention(1)
            out_and_ffn(1)

        @block.scalar
        def _(act):
            def copy(dst, src, func=ACT.Copy, **more):
                return nc.scalar.activation(dst, src, func, **more)

            act.sem_inc(ff_sg.sem, AHEAD)
            act.sem_inc(ff_hi.sem, AHEAD)

            def split_hi(n, b, size, filled, used, done):
                if b == 0:
                    act.wait_ge(w_full[n % SLOTS].sem, filled)
                    act.wait_ge(first_used, used)
                else:
                    act.wait_ge(unit_done.sem, done)
                copy(hi_half(n, b, size), half_of(ring, n, b, size)).then_inc(w_hi_ready, 1)

            class Splits:

                def __init__(self, split):
                    self.split, self.next = split, 0

                def upto(self, n, b):
                    while self.next <= 2 * n + b:
                        self.split(self.next // 2, self.next % 2)
                        self.next += 1

                def skip_to(self, n):
                    self.next = 2 * n

            def norm_hi(layer, k, outs):
                for c in range(KT):
                    act.wait_ge(*hT_psum(layer, 4 * k + c // 2 + 1))
                    for dst, gains, row in outs:
                        ins = copy(dst[:, c, :], T[c // 2][:, (c % 2) * SEQ:(c % 2 + 1) * SEQ],
                                   scale=gains[:, row + c:row + c + 1])
                    ins.then_inc(hT_hi_ready.sem, 1)

            with act.Fori(0, DEPTH) as l:
                def split_layer(n, b, more=0):
                    split_hi(n, b, HALF_W, l * (FILL * L_UNITS // SLOTS) + more * (FILL // SLOTS) + FILL * (n // SLOTS + 1),
                             l * L_UNITS + more + (USED_AHEAD + n - 1), l * L_UNITS + more + (SLOTS + n - 1))
                splits = Splits(split_layer)

                def multiplied(n):
                    splits.upto(n + 1, 0)
                    act.wait_ge(*unit_done(l, SLOTS + n))

                def norm_sums(k):
                    act.wait_ge(*x_new(l, k + 1))
                    for s in range(NT):
                        ins = copy(h[:, s, :], x[:, s, :], ACT.Square, accum_out=ss[:, s:s + 1])
                    ins.then_inc(sumsq.sem, 1)

                def take(q, dst, func=ACT.Copy, tiles=(0,), **more):
                    multiplied(end_of(q))
                    for s in tiles:
                        b = G[2 * (q % 2) + s]
                        ins = copy(dst(s), b[:, 0:dst(s).shape[-1]], func, **more)
                    ins.then_inc(z_a.sem, 1)

                splits.upto(1, 0)
                norm_sums(0)
                splits.upto(1, 1)
                act.wait_ge(*prm_ready(l, 1))
                norm_hi(l, 0, [(hT_hi, prm, R_N1)])
                for q in range(3):
                    take(q, lambda s: zr[:, s, q, :])
                take(3, lambda s: zr[:, s, 3, :], ACT.Silu, (0, 1))
                for b in range(2):
                    splits.upto(end_of(3) + 1, 0)
                    act.wait_ge(*rqk_psum(l, b + 1))
                    if b == 0:
                        act.wait_ge(*rot_ready(l, 1))
                    ins = copy(qkT[:, b, :], T[b][:, :])
                ins.then_inc(qT_ready.sem, 1)
                take(4, lambda s: zc[:, s, 0, :])
                take(5, lambda s: zc[:, s, 1, :], ACT.Tanh, (0, 1), scale=0.5)
                take(6, lambda s: zg[:, s, 0, :], ACT.Gelu_apprx_tanh, (0, 1))
                splits.upto(end_of(6) + 1, 0)
                act.wait_ge(*cu_psum(l, 1))
                act.wait_ge(pad_ready, 1)
                for b in range(2):
                    ins = copy(uTp[:, 2 * b:2 * b + 2, 30:30 + SEQ],
                               T[2 + b][:, :].rearrange("p (c s) -> p c s", c=2), scale=0.5)
                ins.then_inc(cuT_ready.sem, 1)
                take(7, lambda s: zg[:, s, 1, :], ACT.Gelu_apprx_tanh, (0, 1))
                splits.upto(end_of(7) + 1, 0)
                act.wait_ge(*rya_psum(l, 1))
                for c in range(4):
                    ins = copy(ysT_hi[:, PLACE[0], c, :], T[c // 2][:, (c % 2) * SEQ:(c % 2 + 1) * SEQ],
                               scale=prm[:, R_GN + c:R_GN + c + 1])
                ins.then_inc(ysT_hi_ready.sem, 1)
                take(8, lambda s: zs[:, s, 0:512])
                take(9, lambda s: zs[:, s, 512:768])
                splits.upto(end_of(9) + 1, 0)
                act.wait_ge(*gy_psum(l, 1))
                for b in range(2):
                    ins = copy(ysT_hi[:, PLACE[2], 2 * b:2 * b + 2, :], T[2 + b][:, :].rearrange("p (c s) -> p c s", c=2))
                ins.then_inc(ysT_hi_ready.sem, 1)

                for u, (kind, b, hf, a, q) in enumerate(MIX_STEPS):
                    splits.upto(U_MIX + u + 2, 0)
                    if kind == "gate" and a == 1:
                        if hf == 0 and b in (3, 1):
                            act.wait_ge(*z_d(l, taken("D", P_BRANCH[{3: 0, 1: 2}[b]] + 1)))
                        take(q, lambda s: gates[:, PLACE[b], s, hf * 512:(hf + 1) * 512], ACT.Tanh, (0, 1), scale=0.5)
                    if u == 0:
                        act.wait_ge(*sw_psum(l, 1))
                        copy(swk[:, :, :], T[2][:, :].rearrange("p (c s) -> p c s", c=2),
                             scale=prm[:, R_KG:R_KG + 1]).then_inc(sw_kT.sem, 1)
                    if 1 <= u <= 8:
                        i = u - 1
                        act.wait_ge(*sw_nm(l, i + 1))
                        copy(S[:, i % 4, 0:P], S[:, i % 4, 0:P], ACT.Exp, bias=nm[:, i, 0:1], accum_out=rsum[:, i, 0:1])
                        copy(S[:, i % 4, P:TRI], S[:, i % 4, P:TRI], ACT.Exp, bias=nm[:, i, 1:2],
                             accum_out=rsum[:, i, 1:2]).then_inc(sw_exp.sem, 1)
                    if 2 <= u <= 9:
                        i = u - 2
                        act.wait_ge(*sw_tr(l, i + 1))
                        if i >= 2:
                            act.wait_ge(*sw_o(l, i - 1))
                        copy(pT[:, i % 2, 0:TRI], T[1][:, 0:TRI]).then_inc(sw_pT.sem, 1)
                    if u == 10:
                        act.wait_ge(*sw_sink(l, 1))
                        copy(es[:, 0:8, :], es[:, 0:8, :], ACT.Exp).then_inc(sw_esink.sem, 1)
                    if u == 12:
                        act.wait_ge(*sy_psum(l, 1))
                        act.wait_ge(*unit_done(l, SLOTS + end_of(P_BRANCH[0] + 1)))
                        for j in range(2):
                            ins = copy(ysT_hi[:, PLACE[3], 2 * j:2 * j + 2, :], T[j][:, :].rearrange("p (c s) -> p c s", c=2))
                        ins.then_inc(ysT_hi_ready.sem, 1)
                    if u == 19:
                        act.wait_ge(*cn_psum(l, 1))
                        for c in range(4):
                            ins = copy(cacc[:, c, :], T[c // 2][:, (c % 2) * SEQ:(c % 2 + 1) * SEQ], ACT.Silu,
                                       scale=prm[:, R_CG + c:R_CG + c + 1], bias=prm[:, R_CLB + c:R_CLB + c + 1])
                        ins.then_inc(cs_ready.sem, 1)
                for b in range(4):
                    act.wait_ge(*mixT_psum(l, b + 1))
                    copy(hT_hi[:, 2 * b:2 * b + 2, :], T[b][:, :].rearrange("p (c s) -> p c s", c=2),
                         scale=0.5).then_inc(mixT_a.sem, 1)
                splits.upto(U_FF + 1, 0)
                norm_sums(1)
                splits.upto(U_FF + 1, 1)
                norm_hi(l, 1, [(hT_hi, prm, R_N2)])

                def ff_split(u, more=0):
                    for b in range(2):
                        split_layer(U_FF + u, b, more)

                def ff_silu(parity, units, free):
                    act.wait_ge(unit_done.sem, units)
                    if free is not None:
                        act.wait_ge(ff_u.sem, free)
                    for s in range(NT):
                        ins = copy(sg[:, parity, s, :], G[2 * parity + s][:, 0:256], ACT.Silu)
                    ins.then_inc(ff_sg.sem, 1)

                def ff_take(parity, done, j):
                    act.wait_ge(ff_tr.sem, done)
                    copy(uT_hi[:, bass.ds(j * 2, 2), :], T[parity][:, :].rearrange("p (c s) -> p c s", c=2)
                         ).then_inc(ff_hi.sem, 1)

                units = l * L_UNITS + (SLOTS + U_FF)
                before = l * FF_PANELS + AHEAD
                ff_split(2)
                ff_split(3)
                ff_silu(0, units + 2, None)
                with act.Fori(0, FF_PANELS // 2) as i:
                    ff_split(4, i * 4)
                    ff_split(5, i * 4)
                    ff_silu(1, units + i * 4 + 4, before + i * 2)
                    ff_take(0, before + i * 2 + 1, i * 2)
                    ff_split(6, i * 4)
                    ff_split(7, i * 4)
                    ff_silu(0, units + i * 4 + 6, before + i * 2 + 1)
                    ff_take(1, before + i * 2 + 2, i * 2 + 1)
                ff_take(0, before + FF_PANELS, FF_PANELS - 1)
                for u in range(2 * FF_PANELS + 2, 3 * FF_PANELS):
                    ff_split(u)

            def split_second(n, b, more=0):
                if n in U2_WHOLE:
                    return
                split_hi(n, b, half_size(n, True), more * (FILL // SLOTS) + FILL * (DEPTH * L_UNITS // SLOTS + n // SLOTS + 1),
                         more + (USED_AHEAD + DEPTH * L_UNITS + split_before(n - 1)), more + (DEPTH * L_UNITS + SLOTS + n - 1))
            splits2 = Splits(split_second)

            def norm_sums2(k, src, new):
                if new:
                    act.wait_ge(*x_new(DEPTH, new))
                else:
                    act.wait_ge(mem_in, 16)
                    act.wait_ge(*h_ready(DEPTH, k))
                    act.wait_ge(*hT_psum(DEPTH, 4 * k))
                for s in range(NT):
                    ins = copy(h[:, s, :], src[:, s, :], ACT.Square, accum_out=ss[:, s:s + 1])
                ins.then_inc(sumsq.sem, 1)

            def norm_T2(k, outs):
                for c in range(4):
                    act.wait_ge(*hT_psum(DEPTH, 4 * k + c // 2 + 1))
                    for dst, row in outs:
                        ins = copy(dst[:, c, :], T[c // 2][:, (c % 2) * SEQ:(c % 2 + 1) * SEQ],
                                   scale=prm2[:, row + c:row + c + 1])
                ins.then_inc(memT_a, 1)

            def take2(q, dst):
                splits2.upto(U2_PANEL[q] + 3, 0)
                act.wait_ge(*unit_done(DEPTH, SLOTS + U2_PANEL[q] + 2))
                copy(dst, G[2 * (q % 2)][:, 0:dst.shape[-1]]).then_inc(z2_a, 1)

            def pairs(bank):
                return bank[:, :].rearrange("p (c s) -> p c s", s=SEQ)

            def attention_a(f):
                for j, (layer, kind, i) in enumerate(JOBS):
                    if layer != f:
                        continue
                    rs = rsums[:, groups_before(j) % 2]
                    act.wait_ge(at_nm, j + 1)
                    if j >= 4:
                        act.wait_ge(at_tr, j - 3)
                    if kind == "mem":
                        bank = T[j % 2]
                        copy(S4[:, j % 4, 0:SEQ], bank[:, 0:SEQ], ACT.Exp, bias=nm[:, i, 0:1], accum_out=rs[:, i, 0:1])
                        copy(S4[:, j % 4, SEQ:512], bank[:, SEQ:512], ACT.Exp, bias=nm[:, i, 1:2],
                             accum_out=rs[:, i, 1:2]).then_inc(at_exp, 1)
                        continue
                    p = S4[:, j % 4, :]
                    copy(p[:, 0:P], p[:, 0:P], ACT.Exp, bias=nm[:, i, 0:1], accum_out=rs[:, i, 0:1])
                    copy(p[:, P:TRI], p[:, P:TRI], ACT.Exp, bias=nm[:, i, 1:2],
                         accum_out=rs[:, i, 1:2]).then_inc(at_exp, 1)

            def out_and_ffn_a(f):
                for b in range(4):
                    act.wait_ge(oT_psum, 4 * f + b + 1)
                    copy(hT_hi[:, 2 * b:2 * b + 2, :], pairs(T[b])).then_inc(oT_a, 1)
                def up_split(u, more=0):
                    for b in range(2):
                        split_second(U2_UP[f] + u, b, more)
                splits2.upto(U2_UP[f] + 1, 0)
                norm_sums2(NORM_FFN[f], x, 2 + 2 * f)
                splits2.upto(U2_UP[f] + 1, 1)
                norm_hi(DEPTH, NORM_FFN[f], [(hT_hi, prm2, N2_FFN + 8 * f)])
                done = f * FF_PANELS
                units = DEPTH * L_UNITS + SLOTS + U2_UP[f]

                def take_up(j, parity, first=False):
                    act.wait_ge(unit_done.sem, units + 2 + j * 2)
                    if not first:
                        act.wait_ge(cf_tr, 2 * done + j * 2 - 2)
                    copy(zcv[:, parity, 0, :], G[2 * parity][:, :]).then_inc(cf_za, 1)

                def tap(j, parity, first=False):
                    if not first:
                        act.wait_ge(cf_uT, done + j - 1)
                    for b in range(2):
                        act.wait_ge(cf_tr, 2 * done + j * 2 + 1 + b)
                        for c in range(2):
                            tile = 22 * b + j * 2 + c
                            ins = copy(accv[:, parity, 2 * b + c, :], T[2 * parity + b][:, c * SEQ:(c + 1) * SEQ], ACT.Identity,
                                       scale=cvp[:, f, 2, bass.ds(tile, 1)], bias=cvp[:, f, 3, bass.ds(tile, 1)])
                        ins.then_inc(cf_tap, 1)

                def silu(j, parity):
                    act.wait_ge(cf_cv, AHEAD + done + j + 1)
                    copy(accv[:, parity, 0:2, :], accv[:, parity, 0:2, :], ACT.Silu).then_inc(cf_silu, 1)

                up_split(2)
                up_split(3)
                take_up(0, 0, True)
                up_split(4)
                up_split(5)
                take_up(1, 1, True)
                tap(0, 0, True)
                up_split(6)
                up_split(7)
                take_up(2, 0)
                tap(1, 1, True)
                silu(0, 0)
                with act.Fori(0, (FF_PANELS - 3) // 2) as i:
                    up_split(8, i * 4)
                    up_split(9, i * 4)
                    take_up(i * 2 + 3, 1)
                    tap(i * 2 + 2, 0)
                    silu(i * 2 + 1, 1)
                    up_split(10, i * 4)
                    up_split(11, i * 4)
                    take_up(i * 2 + 4, 0)
                    tap(i * 2 + 3, 1)
                    silu(i * 2 + 2, 0)
                tap(10, 0)
                silu(9, 1)
                silu(10, 0)
                for u in range(2 * FF_PANELS + 2, 3 * FF_PANELS):
                    up_split(u)
                splits2.skip_to(U2_UP[f] + 3 * FF_PANELS)

            splits2.upto(1, 0)
            norm_sums2(NORM_ATT[0], x, 1)
            splits2.upto(1, 1)
            act.wait_ge(prm2_ready, 1)
            norm_hi(DEPTH, NORM_ATT[0], [(hT_hi, prm2, N2_ATT)])
            norm_sums2(NORM_MEM, mem, None)
            for q in range(2):
                take2(q, z2[:, 0, 512 * q:512 * (q + 1)])
            norm_T2(NORM_MEM, [(memT[0], N2_MEM), (memT[1], N2_MEM + 8)])
            take2(2, z2[:, 0, 1024:1536])
            take2(3, z2[:, 0, 1536:A_IN])
            act.wait_ge(cmpT_psum, 1)
            copy(u2[0:HD, 0:2, :], pairs(T[0])[0:HD])
            copy(u2[HD:P, 0:2, 0:SEQ - 1], pairs(T[0])[HD:P, :, 1:SEQ]).then_inc(u2_a, 1)
            take2(Q_MEM, mkv[0][:, 0, :])
            take2(Q_MEM + 1, mkv[1][:, 0, :])
            act.wait_ge(gate_in, 1)
            copy(gsig, gsig, ACT.Sigmoid).then_inc(gate_ready, 1)
            act.wait_ge(*unit_done(DEPTH, SLOTS + U2_CMP + 4))
            for kv in range(2):
                for ht in range(2):
                    ins = copy(h1T[:, kv, ht, :, :].rearrange("p g (a n) -> p g a n", a=4),
                               T[2][:, (2 * kv + ht) * HD:(2 * kv + ht + 1) * HD].rearrange("p (g n) -> p g n", g=2)
                               .unsqueeze(2).to_broadcast([P, 2, 4, CMP_PAD]), ACT.Gelu_apprx_tanh,
                               bias=prm2[:, N2_B1 + 2 * kv + ht:N2_B1 + 2 * kv + ht + 1])
            ins.then_inc(hid_ready, 1)
            act.wait_ge(turn_psum, 1)
            copy(qT2[:, 0:2, :], pairs(T[0]), scale=HD ** -0.5)
            copy(qT2[:, 2:4, :], pairs(T[1]), scale=HD ** -0.5).then_inc(turn_a, 1)
            act.wait_ge(turn_psum, 3)
            copy(qmT[:, :, :], pairs(T[1]), scale=HD ** -0.5).then_inc(turn_a, 1)
            act.wait_ge(turn_psum, 4)
            copy(kT2[:, 0:2, :], pairs(T[0])).then_inc(turn_a, 1)
            act.wait_ge(turn_psum, 5)
            copy(mkT[1][:, :, :], pairs(T[1])).then_inc(turn_a, 1)
            act.wait_ge(csc_ready, 1)
            copy(Sc[:, :, :, 0:N_CMP], Sc[:, :, :, 0:N_CMP], ACT.Exp).then_inc(cexp, 1)
            splits2.upto(U2_PANEL[Q_OUT[0]] + 1, 1)
            attention_a(0)
            out_and_ffn_a(0)

            splits2.upto(U2_PANEL[Q_SHARED] + 1, 0)
            norm_sums2(NORM_ATT[1], x, 3)
            splits2.upto(U2_PANEL[Q_SHARED] + 1, 1)
            norm_hi(DEPTH, NORM_ATT[1], [(hT_hi, prm2, N2_ATT + 8), (hsT_hi, prm2, N2_KV)])
            for q in range(4):
                take2(Q_SHARED + q, zk[:, 0, 512 * q:min(512 * (q + 1), SHARED)])
            act.wait_ge(fg_in, 1)
            copy(ef, ef, ACT.Exp).then_inc(fg_exp, 1)
            act.wait_ge(fg_exp, 1)
            copy(ef, ef, ACT.Ln, bias=1.0).then_inc(fg_ln, 1)
            for q in range(2):
                take2(Q_IN + q, zq[:, 0, 512 * q:512 * (q + 1)])
            for b in range(2):
                if b == 0:
                    act.wait_ge(turn_psum, 6)
                ins = copy(qT2[:, 2 * b:2 * b + 2, :], pairs(T[b]), scale=HD ** -0.5)
            ins.then_inc(turn_a, 1)
            act.wait_ge(turn_psum, 7)
            for b in range(2):
                ins = copy(kT2[:, 2 * b:2 * b + 2, :], pairs(T[b]))
            ins.then_inc(turn_a, 1)
            splits2.upto(U2_PANEL[Q_OUT[1]] + 1, 1)
            attention_a(1)
            out_and_ffn_a(1)
            norm_sums2(NORM_FINAL, x, 5)

        @block.vector
        def _(dve):
            v = nc.vector
            ch = Chain(dve, d_chain)
            dve.wait_ge(x_in, 16)
            dve.sem_inc(x_new.sem, 1)
            dve.sem_inc(ff_u.sem, AHEAD)
            dve.sem_inc(ff_uT.sem, AHEAD)
            dve.sem_inc(cf_cv, AHEAD)
            dve.wait_ge(brow_psum, 1)
            v.tensor_tensor(vrow[:, :], T[3][0:8, 0:TRI], const["window"][:, :], ALU.add).then_inc(brow_ready, 1)
            dve.wait_ge(const_in, 16 * len(const))

            def norm_lo(layer, index, outs):
                for c in range(KT):
                    dve.wait_ge(*hT_hi_ready(layer, KT * index + c // 2 * 2 + 2))
                    for lo, hi, gains, row in outs:
                        ins = v.scalar_tensor_tensor(lo[:, c, :], T[c // 2][:, (c % 2) * SEQ:(c % 2 + 1) * SEQ],
                                                     gains[:, row + c:row + c + 1], hi[:, c, :].bitcast(F32),
                                                     ALU.mult, ALU.subtract)
                ins.then_inc(hT_d.sem, 1)

            def pairs(bank):
                return bank[:, :].rearrange("p (c s) -> p c s", s=SEQ)

            with dve.Fori(0, DEPTH) as l:
                def multiplied(n):
                    dve.wait_ge(*unit_done(l, SLOTS + n))

                def take(q, dst):
                    multiplied(end_of(q))
                    v.tensor_copy(dst, G[2 * (q % 2) + 1][:, 0:dst.shape[-1]]).then_inc(z_d.sem, 1)

                def norm_rows(k):
                    dve.wait_ge(*rstd_ready(l, k + 1))
                    for s in range(NT):
                        ins = v.tensor_scalar(h[:, s, :], x[:, s, :], rstd[:, s:s + 1], None, ALU.mult)
                    ins.then_inc(h_ready.sem, 1)

                dve.wait_ge(*prm_psum(l, 1))
                v.tensor_copy(prm[:, :], T[0][:, 0:R_END])
                v.tensor_copy(cw[:, :], T[1][:, 0:124])
                v.tensor_tensor(wsT[:, :, :], T[2][:, :].rearrange("p (c s) -> p c s", c=4),
                                upper[:, :].unsqueeze(1).to_broadcast([P, 4, P]), ALU.mult).then_inc(prm_ready.sem, 1)
                norm_rows(0)
                norm_lo(l, 0, [(hT_lo, hT_hi, prm, R_N1)])
                take(0, zr[:, 1, 0, :])
                take(1, zr[:, 1, 1, :])
                dve.wait_ge(*z_a(l, taken("A", 1)))
                dve.wait_ge(*z_d(l, taken("D", 1)))
                for s in range(NT):
                    z = zr[:, s, 0:2, :].rearrange("p a (b c) -> p (a b) c", c=P)
                    o = h[:, s, :].rearrange("p (b c) -> p b c", c=P)
                    w = tmp[:, s, :].rearrange("p (b c) -> p b c", c=P)
                    c_t, s_t = const["rope_c"][:, s, :], const["rope_s"][:, s, :]

                    def over_heads(a):
                        return a.unsqueeze(1).to_broadcast([P, 8, a.shape[-1]])
                    v.tensor_tensor(o, z, over_heads(c_t), ALU.mult)
                    v.tensor_tensor(w[:, :, 0:64], z[:, :, 64:P], over_heads(s_t[:, 0:64]), ALU.mult)
                    ch.link(v.tensor_tensor(w[:, :, 64:P], z[:, :, 0:64], over_heads(s_t[:, 64:P]), ALU.mult))
                    ins = v.tensor_tensor(o, o, w, ALU.add)
                ins.then_inc(rot_ready.sem, 1)
                take(2, zr[:, 1, 2, :])
                for b in range(2, 4):
                    dve.wait_ge(*rqk_psum(l, b + 1))
                    ins = v.tensor_copy(kTt[:, b - 2, :], T[b][:, :])
                ins.then_inc(kT_ready.sem, 1)
                take(4, zc[:, 1, 0, :])
                for i in range(4):
                    dve.wait_ge(*rsc_psum(l, i + 1))
                    v.tensor_tensor(scr[:, i, :], T[i][:, 0:TRI], decay[:, i, :], ALU.mult).then_inc(rsc_ready.sem, 1)
                dve.wait_ge(*z_a(l, taken("A", 5)))
                dve.wait_ge(*z_d(l, taken("D", 4)))
                v.scalar_tensor_tensor(mix[:, :, 0:MIX], zc[:, :, 1, :], 1.0, zc[:, :, 0, :],
                                       ALU.add, ALU.mult).then_inc(cu_ready.sem, 1)
                dve.wait_ge(*ry_psum(l, 1))
                for s in range(NT):
                    for i in range(4):
                        ins = v.bn_stats(st[:, 4 * s + i, :], T[s][:, i * P:(i + 1) * P])
                ch.link(ins)
                for i in range(8):
                    ins = v.bn_aggr(mv[:, i, :], st[:, i, :])
                ins.then_inc(ry_stat.sem, 1)
                dve.wait_ge(*ry_rstd(l, 1))
                for s in range(NT):
                    for i in range(4):
                        j = 4 * s + i
                        ins = v.tensor_scalar(yr[:, s, i * P:(i + 1) * P], T[s][:, i * P:(i + 1) * P],
                                              mv[:, j, 0:1], rs8[:, j:j + 1], ALU.subtract, ALU.mult)
                ch.link(ins)
                dve.wait_ge(*z_a(l, taken("A", 3)))
                v.tensor_tensor(yr, yr, zr[:, :, 3, :], ALU.mult).then_inc(rya_ready.sem, 1)
                dve.wait_ge(*z_a(l, taken("A", 7)))
                for s in range(NT):
                    ins = v.bn_stats(st[:, s, :], zg[:, s, 1, :])
                ch.link(ins)
                for s in range(NT):
                    ins = v.bn_aggr(mv[:, s, :], st[:, s, :])
                ins.then_inc(gv_stat.sem, 1)
                dve.wait_ge(*gv_rstd(l, 1))
                for s in range(NT):
                    ins = v.tensor_scalar(tmp[:, s, 0:MIX], zg[:, s, 1, :], mv[:, s, 0:1], rs8[:, s:s + 1],
                                          ALU.subtract, ALU.mult)
                ch.link(ins)
                for s in range(NT):
                    ins = v.tensor_tensor(tmp[:, s, 0:MIX], tmp[:, s, 0:MIX], lng[:, :], ALU.mult)
                ch.link(ins)
                for s in range(NT):
                    ins = v.tensor_tensor(tmp[:, s, 0:MIX], tmp[:, s, 0:MIX], lnb[:, :], ALU.add)
                ins.then_inc(gv_ready.sem, 1)
                dve.wait_ge(*ysT_hi_ready(l, 1))
                for c in range(4):
                    ins = v.scalar_tensor_tensor(ysT_lo[:, PLACE[0], c, :], T[c // 2][:, (c % 2) * SEQ:(c % 2 + 1) * SEQ],
                                                 prm[:, R_GN + c:R_GN + c + 1], ysT_hi[:, PLACE[0], c, :].bitcast(F32),
                                                 ALU.mult, ALU.subtract)
                ins.then_inc(ysT_ret.sem, 1)
                take(8, zs[:, 1, 0:512])

                def ys_lo(b, banks, turn, done):
                    dve.wait_ge(*ysT_hi_ready(l, turn))
                    for j in range(2):
                        ins = v.tensor_tensor(ysT_lo[:, PLACE[b], 2 * j:2 * j + 2, :], pairs(banks[j]),
                                              ysT_hi[:, PLACE[b], 2 * j:2 * j + 2, :].bitcast(F32), ALU.subtract)
                    ins.then_inc(done.sem, 1)
                dve.wait_ge(*gs_psum(l, 1))
                for s in range(NT):
                    for c in range(4):
                        cols = slice(c * P, (c + 1) * P)
                        ins = v.scalar_tensor_tensor(yg[:, s, cols], T[2 + s][:, cols], prm[:, R_BS + c:R_BS + c + 1],
                                                     zg[:, s, 0, cols], ALU.add, ALU.mult)
                ins.then_inc(gy_ready.sem, 1)
                take(9, zs[:, 1, 512:768])
                dve.wait_ge(*z_a(l, taken("A", 9)))
                dve.wait_ge(*z_d(l, taken("D", 9)))
                dve.wait_ge(*gs_psum(l, 1))
                ch.link(v.tensor_tensor(tmp[:, :, 0:640], zs[:, :, 0:640], zs[:, :, 0:640], ALU.mult))
                for s in range(NT):
                    ins = v.tensor_reduce(ssw[:, s * 10:s * 10 + 10],
                                          tmp[:, s, 0:640].rearrange("p (a b) -> p a b", b=HD), AX.X, ALU.add)
                ins.then_inc(sw_sumsq.sem, 1)
                dve.wait_ge(*sw_rstd(l, 1))
                for s in range(NT):
                    r = rs8[:, s * 10:s * 10 + 10]
                    v.tensor_tensor(tmp[:, s, 0:512].rearrange("p (a b) -> p a b", b=HD),
                                    zs[:, s, 0:512].rearrange("p (a b) -> p a b", b=HD),
                                    r[:, 0:8].unsqueeze(2).to_broadcast([P, 8, HD]), ALU.mult)
                    for a in range(2):
                        ins = v.tensor_tensor(kdup[:, s, :].rearrange("p (g a b) -> p g a b", a=2, b=HD)[:, :, a, :],
                                              zs[:, s, 512:640].rearrange("p (a b) -> p a b", b=HD),
                                              r[:, 8:10].unsqueeze(2).to_broadcast([P, 2, HD]), ALU.mult)
                ins.then_inc(sw_norm.sem, 1)
                ys_lo(2, T[2:4], 2, ysT_gmlp)

                dve.wait_ge(*cuT_ready(l, 1))
                tap_mark = [0] * 4

                def gated(b, hf, q):
                    cols = slice(hf * 512, (hf + 1) * 512)
                    multiplied(end_of(q))
                    dve.wait_ge(*z_a(l, taken("A", P_GATE[b] + hf)))
                    first = b == BRANCH_ORDER[0]
                    for s in range(NT):
                        dst = mix if first else tmp
                        ins = v.scalar_tensor_tensor(dst[:, s, cols], gates[:, PLACE[b], s, cols], 1.0,
                                                     G[2 * (q % 2) + s][:, :], ALU.add, ALU.mult)
                    if not first:
                        ch.link(ins)
                        ins = v.tensor_tensor(mix[:, :, cols], mix[:, :, cols], tmp[:, :, cols], ALU.add)
                    ins.then_inc(z_d.sem, 1)

                def taps(k0, k1):
                    for k in range(k0, min(k1, 31)):
                        for c in range(4):
                            wk = cw[:, 4 * k + c:4 * k + c + 1]
                            u_k = uTp[:, c, k:k + SEQ]
                            if k == 0:
                                ins = v.tensor_scalar(cacc[:, c, :], u_k, wk, prm[:, R_CB + c:R_CB + c + 1],
                                                      ALU.mult, ALU.add)
                            else:
                                dve.wait_ge(ch.sem, tap_mark[c])
                                ins = v.scalar_tensor_tensor(cacc[:, c, :], u_k, wk, cacc[:, c, :], ALU.mult, ALU.add)
                            tap_mark[c] = ch.mark(ins)

                for u, (kind, b, hf, a, q) in enumerate(MIX_STEPS):
                    if kind == "branch":
                        gated(b, hf, q)
                    if u == 0:
                        dve.wait_ge(*sw_psum(l, 1))
                        for j in range(2):
                            ins = v.tensor_scalar(swq[:, 2 * j:2 * j + 2, :],
                                                  T[j][:, :].rearrange("p (c s) -> p c s", c=2),
                                                  prm[:, R_QG:R_QG + 1], HD ** -0.5, ALU.mult, ALU.mult)
                        ins.then_inc(sw_qT.sem, 1)
                    if 1 <= u <= 8:
                        i = u - 1
                        if i == 0:
                            dve.wait_ge(bias_in, 32)
                        if i >= 4:
                            dve.wait_ge(*sw_tr(l, i - 3))
                        dve.wait_ge(*sw_sc(l, i + 1))
                        dve.sem_inc(hold_d, 1)
                        for s, cols in enumerate((slice(0, P), slice(P, TRI))):
                            near = bias[:, i, P:SEQ] if s == 0 else bias[:, i, :]
                            ins = v.tensor_tensor_reduce(out=S[:, i % 4, cols], in0=T[0][:, cols], in1=near,
                                                         scale=1.0, scalar=sinks[:, i:i + 1], op0=ALU.add, op1=ALU.max,
                                                         accum_out=mx[:, i, s:s + 1])
                        ch.link(ins)
                        v.tensor_scalar(nm[:, i, :], mx[:, i, :], -1.0, None, ALU.mult).then_inc(sw_nm.sem, 1)
                    if u == 10:
                        ch.link(v.tensor_tensor(es[:, 0:8, :], nm[:, 0:8, :],
                                                sinks[:, :].unsqueeze(2).to_broadcast([P, 8, 2]), ALU.add))
                        dve.sem_inc(sw_sink.sem, 1)
                    if u < 16:
                        taps(2 * u, 2 * u + 2)
                    if u == 11:
                        dve.wait_ge(*sw_exp(l, 8))
                        dve.wait_ge(*sw_esink(l, 1))
                        ch.link(v.tensor_tensor(rsum[:, 0:8, :], rsum[:, 0:8, :], es[:, 0:8, :], ALU.add))
                        ch.link(v.reciprocal(rsum[:, 0:8, :], rsum[:, 0:8, :]))
                        dve.wait_ge(*sw_o(l, 8))
                        for s in range(NT):
                            ins = v.tensor_tensor(h[:, s, 0:MIX].rearrange("p (a b) -> p a b", b=HD),
                                                  T[2 + s][:, :].rearrange("p (a b) -> p a b", b=HD),
                                                  rsum[:, 0:8, s:s + 1].to_broadcast([P, 8, HD]), ALU.mult)
                        ins.then_inc(sy_ready.sem, 1)
                    if u == 12:
                        ys_lo(3, T[0:2], 3, ysT_swa)
                    if u == 15:
                        dve.wait_ge(ch.sem, ch.n)
                        dve.sem_inc(cv_ready.sem, 1)
                    if u == 16:
                        dve.wait_ge(*cv_psum(l, 1))
                        for s in range(NT):
                            ins = v.bn_stats(st[:, s, :], T[2 + s][:, :])
                        ch.link(ins)
                        for s in range(NT):
                            ins = v.bn_aggr(mv[:, s, :], st[:, s, :])
                        ins.then_inc(cv_stat.sem, 1)
                        dve.wait_ge(*cv_rstd(l, 1))
                        for s in range(NT):
                            ins = v.tensor_scalar(h[:, s, MIX:2 * MIX], T[2 + s][:, :], mv[:, s, 0:1], rs8[:, s:s + 1],
                                                  ALU.subtract, ALU.mult)
                        ins.then_inc(cn_ready.sem, 1)

                    if u == 19:
                        dve.wait_ge(*cs_ready(l, 1))
                        hi = ysT_hi[:, PLACE[1], :, :]
                        ch.link(v.tensor_copy(hi, cacc))
                        v.tensor_tensor(ysT_lo[:, PLACE[1], :, :], cacc, hi.bitcast(F32), ALU.subtract
                                        ).then_inc(ysT_conv.sem, 1)
                for b in range(4):
                    dve.wait_ge(*mixT_a(l, b + 1))
                    part = slice(2 * b, 2 * b + 2)
                    ins = v.scalar_tensor_tensor(hT_lo[:, part, :], pairs(T[b]), 0.5, hT_hi[:, part, :].bitcast(F32),
                                                 ALU.mult, ALU.subtract)
                ins.then_inc(mixT_d.sem, 1)
                for hf in range(2):
                    q = P_OUT + hf
                    cols = slice(hf * 512, (hf + 1) * 512)
                    multiplied(end_of(q))
                    for s in range(NT):
                        ins = v.tensor_tensor(x[:, s, cols], x[:, s, cols], G[2 * (q % 2) + s][:, :], ALU.add)
                    ins.then_inc(z_d.sem, 1)
                dve.wait_ge(*z_d(l, taken("D", P_OUT + 1)))
                dve.sem_inc(x_new.sem, 1)
                norm_rows(1)
                norm_lo(l, 1, [(hT_lo, hT_hi, prm, R_N2)])

                def ff_hidden(parity, done, free):
                    dve.wait_ge(ff_sg.sem, done)
                    if free is not None:
                        dve.wait_ge(ff_tr.sem, free)
                    for s in range(NT):
                        ins = v.tensor_tensor(uu[:, parity, s, :], sg[:, parity, s, :],
                                              G[2 * parity + s][:, 256:512], ALU.mult)
                    ins.then_inc(ff_u.sem, 1)

                def ff_lo(parity, done, j):
                    dve.wait_ge(ff_hi.sem, done)
                    v.tensor_tensor(uT_lo[:, bass.ds(j * 2, 2), :], T[parity][:, :].rearrange("p (c s) -> p c s", c=2),
                                    uT_hi[:, bass.ds(j * 2, 2), :].bitcast(F32), ALU.subtract).then_inc(ff_uT.sem, 1)

                before = l * FF_PANELS + AHEAD
                ff_hidden(0, before + 1, None)
                with dve.Fori(0, FF_PANELS // 2) as i:
                    ff_hidden(1, before + i * 2 + 2, before + i * 2)
                    ff_lo(0, before + i * 2 + 1, i * 2)
                    ff_hidden(0, before + i * 2 + 3, before + i * 2 + 1)
                    ff_lo(1, before + i * 2 + 2, i * 2 + 1)
                ff_lo(0, before + FF_PANELS, FF_PANELS - 1)
                multiplied(L_UNITS)
                for s in range(NT):
                    for hf in range(2):
                        cols = slice(hf * 512, (hf + 1) * 512)
                        ins = v.tensor_tensor(x[:, s, cols], x[:, s, cols], G[2 * s + hf][:, :], ALU.add)
                ins.then_inc(x_new.sem, 1)
                ch.restart()

            def norm_rows2(k, src=x):
                dve.wait_ge(*rstd_ready(DEPTH, k + 1))
                for s in range(NT):
                    ins = v.tensor_scalar(h[:, s, :], src[:, s, :], rstd[:, s:s + 1], None, ALU.mult)
                ins.then_inc(h_ready.sem, 1)

            def norm_T2(k, outs):
                for c in range(4, 8):
                    dve.wait_ge(*hT_psum(DEPTH, 4 * k + c // 2 + 1))
                    for dst, row in outs:
                        ins = v.tensor_scalar(dst[:, c, :], T[c // 2][:, (c % 2) * SEQ:(c % 2 + 1) * SEQ],
                                              prm2[:, row + c:row + c + 1], None, ALU.mult)
                ins.then_inc(hT_d.sem, 1)

            def take2(q, dst):
                dve.wait_ge(*unit_done(DEPTH, SLOTS + U2_PANEL[q] + 2))
                v.tensor_copy(dst, G[2 * (q % 2) + 1][:, 0:dst.shape[-1]]).then_inc(z2_d, 1)

            def rotate(dst, src, w, c_t, s_t, heads, rows_=P):
                def over(a):
                    return a.unsqueeze(1).to_broadcast([rows_, heads, a.shape[-1]])
                v.tensor_tensor(dst, src, over(c_t), ALU.mult)
                v.tensor_tensor(w[:, :, 0:32], src[:, :, 32:HD], over(s_t[:, 0:32]), ALU.mult)
                ch.link(v.tensor_tensor(w[:, :, 32:HD], src[:, :, 0:32], over(s_t[:, 32:HD]), ALU.mult))
                return v.tensor_tensor(dst, dst, w, ALU.add)

            def combine(f, branch, at_first):
                heads = lambda a: a.rearrange("p (h c) -> p h c", c=HD)
                for s in range(NT):
                    for g2 in range(2):
                        o = heads(G[2 * s + g2][:, 0:6 * HD])
                        dst = heads(h[:, s, g2 * 384:(g2 + 1) * 384])
                        w = heads(tmp[:, s, g2 * 384:(g2 + 1) * 384])
                        cf = coef[:, 6 * g2:6 * g2 + 6, s:s + 1].to_broadcast([P, 6, HD])
                        ins = v.tensor_tensor(dst if at_first else w, o, cf, ALU.mult)
                if not at_first:
                    ch.link(ins)
                    ins = v.tensor_tensor(h[:, :, 0:MIX_W], h[:, :, 0:MIX_W], tmp[:, :, 0:MIX_W], ALU.add)
                ins.then_inc(at_sum, 1)

            def attention_d(f):
                jobs = [j for j, job in enumerate(JOBS) if job[0] == f]

                def maxima(j):
                    _, kind, i = JOBS[j]
                    bank, p = T[j % 2], S4[:, j % 4, :]
                    dve.wait_ge(at_sc, j + 1)
                    if kind == "mem":
                        ins = v.tensor_reduce(mx[:, i, :], bank[:, :].rearrange("p (t c) -> p t c", t=NT), AX.X, ALU.max)
                    elif kind == "fgt":
                        for s, cols in enumerate((slice(0, P), slice(P, TRI))):
                            ins = v.scalar_tensor_tensor(p[:, cols], bank[:, cols], dcum[:, s, i:i + 1],
                                                         c2["causal"][:, cols], ALU.add, ALU.add)
                        ch.link(ins)
                        for s, cols in enumerate((slice(0, P), slice(P, TRI))):
                            ins = v.tensor_reduce(mx[:, i, s:s + 1], p[:, cols], AX.X, ALU.max)
                    else:
                        for s, cols in enumerate((slice(0, P), slice(P, TRI))):
                            ins = v.tensor_tensor_reduce(out=p[:, cols], in0=bank[:, cols], in1=c2["causal"][:, cols],
                                                         scale=1.0, scalar=-3e38, op0=ALU.add, op1=ALU.max,
                                                         accum_out=mx[:, i, s:s + 1])
                    ch.link(ins)
                    v.tensor_scalar(nm[:, i, :], mx[:, i, :], -1.0, None, ALU.mult).then_inc(at_nm, 1)

                def probs(j):
                    dve.wait_ge(at_tr, j + 1)
                    if j >= 2:
                        dve.wait_ge(at_o, j)
                    n = 512 if JOBS[j][1] == "mem" else TRI
                    v.tensor_copy(pT4[:, j % 2, 0:n], T[2 + j % 2][:, 0:n]).then_inc(at_pT, 1)

                def finish(j):
                    _, kind, _ = JOBS[j]
                    dve.wait_ge(at_exp, j + 1)
                    n = N_MEM_H if kind == "mem" else N_MIX
                    ch.link(v.reciprocal(coef[:, 0:n, :], rsums[:, groups_before(j) % 2, 0:n, :]))
                    if kind in ("slc", "win"):
                        br = 1 if kind == "slc" else 2
                        ch.link(v.tensor_tensor(coef[:, :, :], coef[:, :, :],
                                                gsig[:, :, :, br].rearrange("p t h -> p h t"), ALU.mult))
                    dve.wait_ge(at_o, j + 2)
                    if kind != "mem":
                        combine(f, kind, kind == "fgt")
                        return
                    for s in range(NT):
                        ins = v.tensor_tensor(h[:, s, MIX_W:D_MODEL].rearrange("p (h c) -> p h c", c=HD),
                                              G[2 * s][:, 0:256].rearrange("p (h c) -> p h c", c=HD),
                                              coef[:, 0:N_MEM_H, s:s + 1].to_broadcast([P, N_MEM_H, HD]), ALU.mult)
                    ins.then_inc(at_sum, 1)

                for step in range(len(jobs) + 2):
                    if step < len(jobs):
                        maxima(jobs[step])
                    if 1 <= step <= len(jobs):
                        probs(jobs[step - 1])
                    if step >= 2 and jobs[step - 2] in LAST:
                        finish(jobs[step - 2])

            def out_and_ffn_d(f):
                for b in range(4):
                    dve.wait_ge(oT_a, 4 * f + b + 1)
                    part = slice(2 * b, 2 * b + 2)
                    ins = v.tensor_tensor(hT_lo[:, part, :], pairs(T[b]), hT_hi[:, part, :].bitcast(F32), ALU.subtract)
                ins.then_inc(oT_d, 1)
                for hf in range(2):
                    q = Q_OUT[f] + hf
                    dve.wait_ge(*unit_done(DEPTH, SLOTS + U2_PANEL[q] + 2))
                    cols = slice(hf * 512, (hf + 1) * 512)
                    for s in range(NT):
                        ins = v.tensor_tensor(x[:, s, cols], x[:, s, cols], G[2 * (q % 2) + s][:, :], ALU.add)
                    ins.then_inc(z2_d, 1)
                dve.wait_ge(z2_d, taken2("D", Q_OUT[f] + 1))
                dve.sem_inc(x_new.sem, 1)
                norm_rows2(NORM_FFN[f])
                norm_lo(DEPTH, 1 + 2 * f, [(hT_lo, hT_hi, prm2, N2_FFN + 8 * f)])
                done = f * FF_PANELS
                units = DEPTH * L_UNITS + SLOTS + U2_UP[f]

                def take_up(j, parity, first=False):
                    dve.wait_ge(unit_done.sem, units + 2 + j * 2)
                    if not first:
                        dve.wait_ge(cf_tr, 2 * done + j * 2 - 2)
                    v.tensor_copy(zcv[:, parity, 1, :], G[2 * parity + 1][:, :]).then_inc(cf_zd, 1)

                def conv(j, parity):
                    ch.restart()
                    mark = [0] * 4
                    for k in (1, 0):
                        for a in range(4):
                            b, c = a // 2, a % 2
                            if k == 1 and c == 0:
                                dve.wait_ge(cf_tap, 2 * done + j * 2 + 1 + b)
                            if k == 0:
                                dve.wait_ge(ch.sem, mark[a])
                            d = 2 - k
                            tile = 22 * b + j * 2 + c
                            acc = accv[:, parity, a, d:SEQ]
                            ins = v.scalar_tensor_tensor(acc, T[2 * parity + b][:, c * SEQ:(c + 1) * SEQ - d],
                                                         cvp[:, f, k, bass.ds(tile, 1)], acc, ALU.mult, ALU.add)
                            mark[a] = ch.mark(ins)
                    dve.wait_ge(ch.sem, ch.n)
                    dve.sem_inc(cf_cv, 1)

                def hidden(j, parity):
                    dve.wait_ge(cf_silu, done + j + 1)
                    u, hi = accv[:, parity, 0:2, :], uT_hi[:, bass.ds(j * 2, 2), :]
                    ch.link(v.tensor_tensor(u, u, accv[:, parity, 2:4, :], ALU.mult))
                    ch.link(v.tensor_copy(hi, u))
                    v.tensor_tensor(uT_lo[:, bass.ds(j * 2, 2), :], u, hi.bitcast(F32), ALU.subtract).then_inc(cf_uT, 1)

                take_up(0, 0, True)
                take_up(1, 1, True)
                conv(0, 0)
                take_up(2, 0)
                conv(1, 1)
                hidden(0, 0)
                ch.restart()
                with dve.Fori(0, (FF_PANELS - 3) // 2) as i:
                    take_up(i * 2 + 3, 1)
                    conv(i * 2 + 2, 0)
                    hidden(i * 2 + 1, 1)
                    take_up(i * 2 + 4, 0)
                    conv(i * 2 + 3, 1)
                    hidden(i * 2 + 2, 0)
                    ch.restart()
                conv(10, 0)
                hidden(9, 1)
                hidden(10, 0)
                dve.wait_ge(*unit_done(DEPTH, SLOTS + U2_DOWN[f] + FF_KT // 2))
                for s in range(NT):
                    for hf in range(2):
                        cols = slice(hf * 512, (hf + 1) * 512)
                        ins = v.tensor_tensor(x[:, s, cols], x[:, s, cols], G[2 * s + hf][:, :], ALU.add)
                ins.then_inc(x_new.sem, 1)

            dve.wait_ge(prm2_psum, 1)
            v.tensor_copy(prm2[:, :], T[0][:, 0:N2_END])
            v.tensor_copy(cvp.rearrange("p f k r -> p (f k r)"), T[1][:, 0:352]).then_inc(prm2_ready, 1)
            norm_rows2(NORM_ATT[0])
            norm_lo(DEPTH, 0, [(hT_lo, hT_hi, prm2, N2_ATT)])
            norm_rows2(NORM_MEM, mem)
            for q in range(2):
                take2(q, z2[:, 1, 512 * q:512 * (q + 1)])
            norm_T2(NORM_MEM, [(memT[0], N2_MEM), (memT[1], N2_MEM + 8)])

            def doubled(dst, src):
                return v.tensor_copy(dst.rearrange("p (g a c) -> p g a c", a=2, c=HD),
                                     src.rearrange("p (g c) -> p g c", c=HD).unsqueeze(2).to_broadcast([P, 4, 2, HD]))
            dve.wait_ge(z2_a, taken2("A", 1))
            dve.wait_ge(z2_d, taken2("D", 1))
            for s in range(NT):
                ins = doubled(kvd[:, s, :], z2[:, s, MIX_W:MIX_W + 256])
            ins.then_inc(kvd_ready, 1)
            take2(2, z2[:, 1, 1024:1536])
            take2(3, z2[:, 1, 1536:A_IN])
            dve.wait_ge(cmpT_psum, 1)
            v.tensor_copy(u2[0:HD, 2:4, :], pairs(T[1])[0:HD])
            v.tensor_copy(u2[HD:P, 2:4, 0:SEQ - 1], pairs(T[1])[HD:P, :, 1:SEQ]).then_inc(u2_d, 1)
            dve.wait_ge(c2_in, 16 * (len(c2) + 5))
            dve.wait_ge(z2_a, taken2("A", 3))
            dve.wait_ge(z2_d, taken2("D", 3))
            for s in range(NT):
                for c0, c1, heads in ((0, 0, 12), (1024, 768, 2), (1280, 896, 2)):
                    src, dst, w = (a[:, s, c:c + heads * HD].rearrange("p (h c) -> p h c", c=HD)
                                   for a, c in ((z2, c0), (h, c1), (tmp, c1)))
                    ins = rotate(dst, src, w, c2["rope2_c"][:, s, :], c2["rope2_s"][:, s, :], heads)
            ch.link(ins)
            for s in range(NT):
                ins = doubled(kd2[:, s, :], h[:, s, MIX_W:D_MODEL])
            ins.then_inc(rot2, 1)
            ch.link(v.memset(tmp_flat, 0.0))
            dve.wait_ge(rot2, 1)
            dve.wait_ge(u2_a, 1)
            dve.wait_ge(u2_d, 1)
            for kv in range(2):
                for g2 in range(2):
                    base = u2[:, 2 * kv + g2, :]
                    src = bass.AP(base.tensor, base.offset, [base.ap[0], [2, 16], [16, N_CMP]])
                    pos = prm2[:, N2_POS + 16 * kv:N2_POS + 16 * (kv + 1)].unsqueeze(2).to_broadcast([P, 16, N_CMP])
                    ins = v.tensor_tensor(blocks[:, kv, :, g2, 0:N_CMP], src, pos, ALU.add)
            ins.then_inc(blocks_ready, 1)
            take2(Q_MEM, mkv[0][:, 1, :])
            take2(Q_MEM + 1, mkv[1][:, 1, :])
            for s in range(NT):
                ins = v.tensor_tensor(gsig[:, s, :, :].rearrange("p h b -> p (h b)"), z2[:, s, 1536:1572], gate_b, ALU.add)
            ins.then_inc(gate_in, 1)
            v.tensor_copy(upones[:, 0:P], upper[:, :])
            v.memset(upones[:, P:SEQ], 1.0)
            ch.link(v.memset(Sc[:, :, :, :], 0.0))
            dve.wait_ge(kvc_psum, 1)
            ch.link(v.tensor_tensor(kvc, T[3][:, 0:256].rearrange("p (v g c) -> p v g c", v=2, g=2),
                                    b2c.unsqueeze(2).to_broadcast([P, 2, 2, HD]), ALU.add))
            ch.link(rotate(kcr[0:N_CMP, :, 0:HD], kvc[0:N_CMP, 0], kct[0:N_CMP], c2["ropec_c"], c2["ropec_s"], 2, N_CMP))
            v.tensor_copy(kcr[0:N_CMP, :, HD:P], kcr[0:N_CMP, :, 0:HD]).then_inc(kcr_ready, 1)
            dve.wait_ge(kcT_psum, 1)
            v.tensor_copy(kcT[:, :, 0:N_CMP], T[3][:, 0:32].rearrange("p (g c) -> p g c", g=2)[:, :, 0:N_CMP]).then_inc(kcT_ready, 1)
            dve.wait_ge(turn_psum, 2)
            v.tensor_scalar(qT2[:, 4:6, :], pairs(T[2]), HD ** -0.5, None, ALU.mult).then_inc(turn_d, 1)
            dve.wait_ge(turn_psum, 4)
            v.tensor_copy(kT2[:, 2:4, :], pairs(T[3]))
            dve.wait_ge(turn_psum, 5)
            v.tensor_copy(mkT[0][:, :, :], pairs(T[2])).then_inc(turn_d, 1)
            dve.wait_ge(csc_psum, 1)
            scv = Sc[:, :, :, 0:N_CMP]
            for s in range(NT):
                for b in range(2):
                    ins = v.tensor_tensor(scv[:, s, b::2], T[b][:, s * 90:(s + 1) * 90].rearrange("p (h n) -> p h n", n=N_CMP),
                                          c2["cmp_neg"][:, s, :].unsqueeze(1).to_broadcast([P, 6, N_CMP]), ALU.add)
            ch.link(ins)
            ch.link(v.tensor_reduce(mxc, scv, AX.X, ALU.max))
            for s in range(NT):
                ins = v.tensor_tensor(scv[:, s], scv[:, s], mxc[:, s, :].unsqueeze(2).to_broadcast([P, N_MIX, N_CMP]), ALU.subtract)
            ins.then_inc(csc_ready, 1)
            dve.wait_ge(cexp, 1)
            for s in range(NT):
                ins = v.tensor_tensor(scv[:, s], scv[:, s], c2["cmp_ok"][:, s, :].unsqueeze(1).to_broadcast([P, N_MIX, N_CMP]), ALU.mult)
            ins.then_inc(cprob, 1)
            dve.wait_ge(cprob, 1)
            ch.link(v.tensor_reduce(smc, scv, AX.X, ALU.add))
            ch.link(v.tensor_scalar(smc, smc, 1e-30, None, ALU.max))
            ch.link(v.reciprocal(smc, smc))
            dve.wait_ge(gate_ready, 1)
            ch.link(v.tensor_tensor(coef, smc.rearrange("p t h -> p h t"), gsig[:, :, :, 0].rearrange("p t h -> p h t"), ALU.mult))
            dve.wait_ge(cprobT, 1)
            for s in range(NT):
                ins = v.tensor_copy(pcT[:, s, :, :], T[2 + s][:, 0:TRI].rearrange("p (a c) -> p a c", c=P))
            ins.then_inc(pcT_ready, 1)
            dve.wait_ge(at_o, 1)
            for s in range(NT):
                for b in range(4):
                    ins = v.tensor_tensor(h[:, s, 0:MIX_W].rearrange("p (a b c) -> p a b c", b=4, c=HD)[:, :, b, :],
                                          G[b][:, s * 192:(s + 1) * 192].rearrange("p (a c) -> p a c", c=HD),
                                          coef[:, b::4, s:s + 1].to_broadcast([P, 3, HD]), ALU.mult)
            ins.then_inc(at_sum, 1)
            attention_d(0)
            out_and_ffn_d(0)

            norm_rows2(NORM_ATT[1])
            norm_lo(DEPTH, 2, [(hT_lo, hT_hi, prm2, N2_ATT + 8), (hsT_lo, hsT_hi, prm2, N2_KV)])
            v.tensor_copy(upones[:, 0:P], upper[:, :])
            v.memset(upones[:, P:SEQ], 1.0)
            for q in range(4):
                take2(Q_SHARED + q, zk[:, 1, 512 * q:min(512 * (q + 1), SHARED)])
            dve.wait_ge(z2_a, taken2("A", Q_SHARED + 3))
            dve.wait_ge(z2_d, taken2("D", Q_SHARED + 3))
            ch.link(v.tensor_tensor(xf, zk[:, :, 2 * MIX_W:SHARED], f_b.unsqueeze(1).to_broadcast([P, NT, N_MIX]), ALU.add))
            ch.link(v.tensor_scalar(ef, xf, -1.0, None, ALU.mult))
            v.tensor_tensor(ef, ef, xf, ALU.min).then_inc(fg_in, 1)
            ch.link(v.tensor_scalar(xf, xf, 0.0, None, ALU.min))
            dve.wait_ge(fg_ln, 1)
            v.tensor_tensor(nlf, ef, xf, ALU.subtract).then_inc(fg_ready, 1)
            for q in range(2):
                take2(Q_IN + q, zq[:, 1, 512 * q:512 * (q + 1)])
            dve.wait_ge(turn_psum, 6)
            v.tensor_scalar(qT2[:, 4:6, :], pairs(T[2]), HD ** -0.5, None, ALU.mult)
            v.tensor_scalar(qmT[:, :, :], pairs(T[3]), HD ** -0.5, None, ALU.mult).then_inc(turn_d, 1)
            dve.wait_ge(fg_cum, 1)
            v.tensor_scalar(dcum, T[3][:, 0:2 * N_MIX].rearrange("p (t h) -> p t h", t=NT), -1.0, None, ALU.mult)
            v.tensor_copy(kT2[:, 4:6, :], pairs(T[2])).then_inc(turn_d, 1)
            attention_d(1)
            out_and_ffn_d(1)
            dve.wait_ge(*rstd_ready(DEPTH, NORM_FINAL + 1))
            for s in range(NT):
                ins = v.scalar_tensor_tensor(h[:, s, :], x[:, s, :], rstd[:, s:s + 1], final_g, ALU.mult, ALU.mult)
            ins.then_inc(h_ready.sem, 1)


def kernel(**inputs):
    import numpy as _np
    import concourse.bacc as _bacc
    from concourse.bass_utils import run_bass_kernel_spmd as _run

    nc = _bacc.Bacc("TRN2", target_bir_lowering=False, num_devices=1)
    arrays, t = {}, {}
    for name, a in list(inputs.items()) + list(constants().items()):
        a = _np.ascontiguousarray(a)
        arrays[f"in_{name}"] = a
        t[name] = nc.dram_tensor(f"in_{name}", a.shape, mybir.dt.from_np(a.dtype), kind="ExternalInput").ap()
    out = nc.dram_tensor("out", (1, SEQ, D_MODEL), F32, kind="ExternalOutput").ap()
    build(nc, t, out)
    r = _run(nc, [arrays], core_ids=[0])
    return r.results[0]["out"]
```

```python
import math
from contextlib import ExitStack

import numpy as np

import concourse.bass as bass
from concourse import mybir

F32 = mybir.dt.float32
F32R = mybir.dt.float32r
ALU = mybir.AluOpType
ACT = mybir.ActivationFunctionType
AX = mybir.AxisListType

P = 128
D_MODEL = 1024
SEQ = 256
NT = SEQ // P
KT = D_MODEL // P
DEPTH = 2
EPS = 1e-6
NEG = -1e30
MIX = 512
SWA_C0 = 4096
GATE_C0 = 4864
D_FF = 2816
FF_PANELS = D_FF // 256
FF_KT = D_FF // P
TRI = 3 * P
HD = 64
N_MIX = 12
N_MEM_H = 4
MIX_W = N_MIX * HD
A_IN = 1828
N_CMP = 15
CMP_PAD = 32
CMP_HID = 256
SHARED = 2 * MIX_W + N_MIX

SLOTS = 4
D_HALVES = 12
AHEAD = 1
SKEW = 512
PRM_LOADS = 16
SLOT_W = 2048
LOADS = 2
FILL = 16 * LOADS
HALF_W = SLOT_W // 2
HI_SLOTS = 4
USED_AHEAD = 2

R_N1, R_GN, R_CB, R_CG, R_CLB, R_BS, R_N2, R_QG, R_KG, R_END = 0, 8, 12, 16, 20, 24, 28, 36, 37, 38


PANEL_EVAC = (["AD", "AD", "AD", "AA"]
              + ["AD", "AA"]
              + ["AA", "AA"]
              + ["AD", "AD"])
PANEL_UNITS = [2] * 9 + [1]
MIX_ORDER = [("gate", 0), ("branch", 0), ("gate", 2), ("branch", 2), ("gate", 3), ("gate", 1), ("branch", 3), ("branch", 1)]
BRANCH_ORDER = [b for kind, b in MIX_ORDER if kind == "branch"]
PLACE = {0: 0, 2: 1, 3: 0, 1: 1}
P_GATE, P_BRANCH, MIX_STEPS = {}, {}, []
U_MIX = sum(PANEL_UNITS)
WINDOW_AT = 2
for kind, b in MIX_ORDER:
    (P_GATE if kind == "gate" else P_BRANCH)[b] = len(PANEL_EVAC)
    for hf in range(2):
        MIX_STEPS += [(kind, b, hf, a, len(PANEL_EVAC)) for a in range(2 if kind == "gate" else 1)]
        PANEL_EVAC += ["AA" if kind == "gate" else "DD"]
        PANEL_UNITS += [2 if kind == "gate" else 1]
P_OUT = len(PANEL_EVAC)
PANEL_EVAC += ["DD"] * 2
PANEL_UNITS += [2] * 2
U_OUT = U_MIX + len(MIX_STEPS)
U_FF = U_OUT + 4
U_DOWN = U_FF + 2 * FF_PANELS
L_UNITS = U_DOWN + FF_KT // 2


def taken(engine, panel):
    return sum(engine in e for e in PANEL_EVAC[:panel + 1])


PANEL2_EVAC = ["AD"] * 6 + ["DD"] * 2 + ["AD"] * 6 + ["DD"] * 2
Q_MEM, Q_OUT, Q_SHARED, Q_IN = 4, (6, 14), 8, 12
U2_CMP = 12
U2_PANEL = [0, 2, 4, 6, 8, 10, 16, 18, 53, 55, 57, 59, 61, 63, 65, 67]
U2_UP, U2_DOWN = (20, 69), (42, 91)
U2_WHOLE = range(8, 16)
U2_SHORT = {6: 4 * 292, 7: 4 * 292, 59: 4 * 12, 60: 4 * 12}
NORMS_SPLIT = (0, 2, 3, 4)
N2_ATT, N2_FFN, N2_MEM, N2_KV, N2_B1, N2_POS, N2_END = 0, 16, 32, 48, 56, 60, 92
NORM_ATT, NORM_MEM, NORM_FFN, NORM_FINAL = (0, 3), 1, (2, 4), 5


def taken2(engine, panel):
    return sum(engine in e for e in PANEL2_EVAC[:panel + 1])


def split_before(n):
    return n - sum(u < n for u in U2_WHOLE)


def half_size(n, second=False):
    return (U2_SHORT.get(n, SLOT_W) if second else SLOT_W) // 2


def end_of(panel):
    return sum(PANEL_UNITS[:panel + 1])


def bucket_table():
    dist = np.clip(255 - np.arange(384), 0, 255)
    d = np.maximum(dist, 1).astype(np.float32)
    large = 16 + (np.log(d / np.float32(16)) / np.float32(math.log(8.0)) * np.float32(16)).astype(np.int32)
    bucket = np.where(dist < 16, dist, np.minimum(large, 31))
    return (np.arange(32)[:, None] == bucket[None, :]).astype(np.float32)


def angles(pos, half):
    inv = (np.float32(10000.0) ** (-np.arange(half, dtype=np.float32) / np.float32(half))).astype(np.float32)
    ang = pos.astype(np.float32)[:, None] * inv[None, :]
    c, s = np.cos(ang).astype(np.float32), np.sin(ang).astype(np.float32)
    return np.concatenate([c, c], 1), np.concatenate([-s, s], 1)


def constants():
    pos = np.arange(SEQ)
    tiles = lambda a: np.ascontiguousarray(a.reshape(NT, P, -1).transpose(1, 0, 2))
    c = {"ident": np.eye(P, dtype=np.float32)}
    c["rope_c"], c["rope_s"] = map(tiles, angles(pos, 64))
    c["rope2_c"], c["rope2_s"] = map(tiles, angles(pos, 32))
    cmp_end = np.arange(N_CMP) * 16 + 31
    c["ropec_c"], c["ropec_s"] = angles(cmp_end, 32)
    i = np.arange(P)
    s, t = i[:, None], i[None, :]
    gamma = 1.0 - 2.0 ** (-5.0 - np.arange(4))
    own = np.where(t >= s, gamma[:, None, None] ** np.maximum(t - s, 0)[None], 0.0)
    prev = gamma[:, None, None] ** (P + t - s)[None]
    c["decay"] = np.ascontiguousarray((np.concatenate([own, prev, own], 2) * P ** -0.5)
                                      .transpose(1, 0, 2)).astype(np.float32)
    c["bucket"] = bucket_table()
    dist = 255 - np.arange(384)
    c["window"] = np.tile(np.where((dist >= 0) & (dist < P), 0.0, NEG).astype(np.float32), (8, 1))
    c["upper"] = (t >= s).astype(np.float32)
    low = np.where(t <= s, 0.0, NEG).astype(np.float32)
    c["causal"] = np.concatenate([low, np.zeros((P, P), np.float32), low], 1)
    ok = tiles((cmp_end[None, :] <= pos[:, None]).astype(np.float32))
    c["cmp_ok"] = ok
    c["cmp_neg"] = np.where(ok > 0, 0.0, NEG).astype(np.float32)
    return c


class Signal:

    def __init__(self, sem, per, ahead=0):
        self.sem, self.per, self.ahead = sem, per, ahead

    def __call__(self, layer, k):
        return self.sem, layer * self.per + (k + self.ahead)


class Chain:

    def __init__(self, engine, sem):
        self.engine, self.sem, self.n = engine, sem, 0

    def link(self, ins):
        self.mark(ins)
        self.engine.wait_ge(self.sem, self.n)

    def mark(self, ins):
        self.n += 1
        ins.then_inc(self.sem, 1)
        return self.n

    def restart(self):
        self.engine.wait_ge(self.sem, self.n)
        self.engine.sem_clear(self.sem)
        self.n = 0


def build(nc, t, out):
    ctx = ExitStack()
    with ctx:
        def sb(name, shape):
            return ctx.enter_context(nc.sbuf_tensor(name, shape, F32))

        def under(name, shape):
            with nc.sbuf_tensor(name, shape, F32R) as tensor:
                return tensor

        def sem(name):
            return ctx.enter_context(nc.semaphore(name))

        def sig(name, per, ahead=0):
            return Signal(sem(name), per, ahead)

        scratch = nc.dram_tensor("bias_rows", (8, P * SKEW + TRI), F32, kind="Internal").ap()

        const = {}
        for name, shape in [("ident", [P, P]), ("rope_c", [P, NT, P]), ("rope_s", [P, NT, P]),
                            ("decay", [P, 4, TRI]), ("upper", [P, P])]:
            const[name] = sb(name, shape)
        ident, decay, upper = const["ident"], const["decay"], const["upper"]
        x = sb("x", [P, NT, D_MODEL])
        h = sb("h", [P, NT, D_MODEL])
        hT_lo = ctx.enter_context(nc.sbuf_tensor("hT_lo", [P, KT, SEQ], F32R))
        w_lo = under("w_lo", [P, SLOTS, SLOT_W])
        ring = sb("ring", [P, SLOTS, SLOT_W])
        hsT_lo = under("hsT_lo", [P, KT, SEQ])
        tmp = sb("tmp", [P, NT, D_MODEL])
        hT_hi = ctx.enter_context(nc.sbuf_tensor("hT_hi", [P, KT, SEQ], F32R))
        w_hi = ctx.enter_context(nc.sbuf_tensor("w_hi", [P, HI_SLOTS, HALF_W], F32R))
        zr = sb("zr", [P, NT, 4, MIX])
        zc = sb("zc", [P, NT, 2, MIX])
        zg = sb("zg", [P, NT, 2, MIX])
        uT_hi = under("uT_hi", [P, FF_KT, SEQ])
        work = sb("work", [P, 4096 + NT * 768 + 4 * TRI])
        gates = work[:, 0:4096].rearrange("p (n t d) -> p n t d", n=2, t=NT)
        zs = work[:, 4096:5632].rearrange("p (t c) -> p t c", t=NT)
        S = work[:, 5632:5632 + 4 * TRI].rearrange("p (a c) -> p a c", a=4)
        const["bucket"] = work[0:32, 2048:2048 + TRI]
        const["window"] = work[0:8, 2432:2432 + TRI]
        vrow = work[0:8, 2816:2816 + TRI]
        uT_lo = under("uT_lo", [P, FF_KT, SEQ])
        ysT_parts = under("ysT_parts", [P, 2, 2, 4, SEQ])
        ysT_hi, ysT_lo = ysT_parts[:, 0], ysT_parts[:, 1]
        ysT = sb("ysT", [P, 4, 4, SEQ])
        hsT_hi = under("hsT_hi", [P, KT, SEQ])
        mix = sb("mix", [P, NT, D_MODEL])
        qkT = zr[:, 0, 0:2, :]
        kTt = zr[:, 1, 0:2, :]
        yr = zr[:, :, 0, :]
        zr_flat = zr[:, :, :, :].rearrange("p t a b -> p (t a b)")
        swq = zr_flat[:, 0:1024].rearrange("p (c s) -> p c s", s=SEQ)
        swk = zr_flat[:, 1024:1536].rearrange("p (c s) -> p c s", s=SEQ)
        kdup = zr_flat[:, 1536:2048].rearrange("p (t c) -> p t c", t=NT)
        pT = zr_flat[:, 2048:3072].rearrange("p (a c) -> p a c", a=2)
        cacc = zr_flat[:, 3072:4096].rearrange("p (c s) -> p c s", s=SEQ)
        bias = sb("bias", [P, 8, SEQ])
        prm_raw = sb("prm_raw", [R_END, P])
        cw_raw = sb("cw_raw", [124, P])
        ws_raw = sb("ws_raw", [P, 4, P])
        prm = sb("prm", [P, R_END])
        cw = sb("cw", [P, 124])
        wsT = sb("wsT", [P, 4, P])
        lng = sb("lng", [P, MIX])
        lnb = sb("lnb", [P, MIX])
        sinks = sb("sinks", [P, 8])
        uTp = sb("uTp", [P, 4, 30 + SEQ])
        ss = sb("ss", [P, NT])
        rstd = sb("rstd", [P, NT])
        half = sb("half", [P, 24])
        st = sb("st", [P, 8, 6])
        mv = sb("mv", [P, 8, 2])
        var = sb("var", [P, 24])
        rs8 = sb("rs8", [P, 24])
        ssw = sb("ssw", [P, 24])
        mx = sb("mx", [P, N_MIX, 2])
        nm = sb("nm", [P, N_MIX, 2])
        rsum = sb("rsum", [P, N_MIX, 2])
        es = sb("es", [P, N_MIX, 2])
        zc_flat = zc[:, :, :, :].rearrange("p t a b -> p (t a b)")
        sg = zc_flat[:, 0:1024].rearrange("p (a c) -> p a c", a=2)
        uu = zc_flat[:, 1024:2048].rearrange("p (a c) -> p a c", a=2)
        rel = sb("rel", [32, 8])
        scr = S[:, 0:4, :]
        yg = zg[:, :, 1, :]

        decay_flat = decay[:, :, :].rearrange("p a b -> p (a b)")
        c2, at = {}, 0
        for name, shape in [("causal", [P, TRI]), ("rope2_c", [P, NT, HD]), ("rope2_s", [P, NT, HD]),
                            ("cmp_ok", [P, NT, N_CMP]), ("cmp_neg", [P, NT, N_CMP]),
                            ("ropec_c", [N_CMP, HD]), ("ropec_s", [N_CMP, HD])]:
            size = shape[-1] * (shape[1] if len(shape) == 3 else 1)
            c2[name] = decay_flat[0:shape[0], at:at + size]
            if len(shape) == 3:
                c2[name] = c2[name].rearrange("p (a b) -> p a b", a=shape[1])
            at += size

        def piece(flat, start, size, pattern=None, **sizes):
            part = flat[:, start:start + size]
            return part.rearrange(pattern, **sizes) if pattern else part
        w2c = piece(decay_flat, at, 256, "p (v k c) -> p v k c", v=2, k=2)
        b2c = piece(decay_flat, at + 256, 128, "p (v c) -> p v c", v=2)
        gate_b = piece(decay_flat, at + 384, 36)
        f_b = piece(decay_flat, at + 420, N_MIX)
        zg_flat = zg[:, :, :, :].rearrange("p t a b -> p (t a b)")
        mem = piece(zg_flat, 0, 2048, "p (t d) -> p t d", t=NT)
        final_g = piece(work, 5632, D_MODEL)
        tmp_flat = tmp[:, :, :].rearrange("p t d -> p (t d)")
        prm2_raw = tmp[0:N2_END, 0, 0:P]
        cv_raw = tmp[0:44, 1, :].rearrange("p (a c) -> p a c", c=P)
        prm2 = sb("prm2", [P, N2_END])
        cvp = uTp[:, :, :].rearrange("p c s -> p (c s)")[:, 0:352].rearrange(
            "p (f k r) -> p f k r", f=2, k=4)
        z2 = piece(zr_flat, 0, NT * A_IN, "p (t c) -> p t c", t=NT)
        zk = piece(zr_flat, 0, NT * SHARED, "p (t c) -> p t c", t=NT)
        zq = piece(zc_flat, 0, 2048, "p (t c) -> p t c", t=NT)
        memT = [zg[:, :, :, :].rearrange("p t a b -> p (t a b)").rearrange("p (c s) -> p c s", s=SEQ),
                mix[:, :, :].rearrange("p t d -> p (t d)").rearrange("p (c s) -> p c s", s=SEQ)]
        bias_flat = bias[:, :, :].rearrange("p a b -> p (a b)")
        mkv = [piece(bias_flat, 1024 * f, 1024, "p (t c) -> p t c", t=NT) for f in range(2)]
        mkT = [piece(zg_flat, 512 * f, 512, "p (c s) -> p c s", s=SEQ) for f in range(2)]
        ysT_flat = ysT[:, :, :, :].rearrange("p b c s -> p (b c s)")
        qT2 = piece(ysT_flat, 0, 1536, "p (c s) -> p c s", s=SEQ)
        qmT = piece(ysT_flat, 1536, 512, "p (c s) -> p c s", s=SEQ)
        kT2 = piece(ysT_flat, 2048, 1536, "p (c s) -> p c s", s=SEQ)
        u2 = piece(zc_flat, 0, 1024, "p (c s) -> p c s", s=SEQ)
        Sc = piece(zc_flat, 1024, 768, "p (t h n) -> p t h n", t=NT, n=CMP_PAD)
        kcr = piece(work, 4128, 256, "p (g c) -> p g c", g=2)
        kvd = piece(work, 0, 1024, "p (t c) -> p t c", t=NT)
        kd2 = piece(work, 1024, 1024, "p (t c) -> p t c", t=NT)
        kct = piece(zc_flat, 1920, 128, "p (g c) -> p g c", g=2)
        blocks = piece(tmp_flat, 0, 2048, "p (v m g n) -> p v m g n", v=2, m=16, g=2)
        S4 = piece(work, 0, 4 * 512, "p (a c) -> p a c", a=4)
        pT4 = piece(work, 2048, 2 * 512, "p (a c) -> p a c", a=2)
        pcT = piece(work, 3072, 768, "p (t a c) -> p t a c", t=NT, c=P)
        kvc = piece(work, 3840, 256, "p (v g c) -> p v g c", v=2, g=2)
        kcT = piece(work, 4096, 32, "p (g c) -> p g c", g=2)
        h1T = piece(work, 2048, 1024, "p (v k g n) -> p v k g n", v=2, k=2, g=2)
        gsig = piece(work, 4384, 72, "p (t h b) -> p t h b", t=NT, b=3)
        coef = piece(work, 4456, 24, "p (h t) -> p h t", t=NT)
        mxc = piece(work, 4480, 24, "p (t h) -> p t h", t=NT)
        smc = piece(work, 4504, 24, "p (t h) -> p t h", t=NT)
        xf = piece(work, 4528, 24, "p (t h) -> p t h", t=NT)
        ef = piece(work, 4552, 24, "p (t h) -> p t h", t=NT)
        nlf = piece(work, 4576, 24, "p (t h) -> p t h", t=NT)
        dcum = piece(work, 4600, 24, "p (t h) -> p t h", t=NT)
        upones = piece(work, 4624, SEQ)
        rsums = piece(work, 4896, 48, "p (a h t) -> p a h t", a=2, t=NT)
        accv = piece(tmp_flat, 0, 2048, "p (a c s) -> p a c s", a=2, c=4)

        G = [ctx.enter_context(nc.psum_tensor(f"G{i}", [P, 512], F32)) for i in range(4)]
        T = [ctx.enter_context(nc.psum_tensor(f"T{i}", [P, 512], F32)) for i in range(4)]

        const_in, early_in = sem("const_in"), sem("early_in")
        x_in = sem("x_in")
        rel_in = sem("rel_in")
        brow_psum, brow_ready, brow_out, bias_in = sem("brow_psum"), sem("brow_ready"), sem("brow_out"), sem("bias_in")
        half_ready = sem("half_ready")
        pad_ready = sem("pad_ready")
        out_done = sem("out_done")
        w_full = [sig(f"w_full{i}", FILL * L_UNITS // SLOTS) for i in range(SLOTS)]
        unit_done = sig("unit_done", L_UNITS)
        prm_in = sig("prm_in", 16 * PRM_LOADS)
        prm_psum, prm_ready = sig("prm_psum", 1), sig("prm_ready", 1)
        x_new, sumsq, rstd_ready, h_ready = (sig(n, 2 * NT) for n in ("x_new", "sumsq", "rstd_ready", "h_ready"))
        tile_done = sig("tile_done", 2)
        hT_psum, memT_a, memT_d, hT_d = sig("hT_psum", 8), sem("memT_a"), sem("memT_d"), sig("hT_d", 8)
        hT_hi_ready = sig("hT_hi_ready", 2 * KT)
        ysT_hi_ready = sig("ysT_hi_ready", 3)
        cs_ready = sig("cs_ready", 1)
        z_a = sig("z_a", taken("A", 99))
        z_d = sig("z_d", taken("D", 99))
        rot_ready, rqk_psum, qT_ready, kT_ready = sig("rot_ready", 1), sig("rqk_psum", 4), sig("qT_ready", 1), sig("kT_ready", 1)
        rsc_psum, rsc_ready, ry_psum, ry_stat = sig("rsc_psum", 4), sig("rsc_ready", 4), sig("ry_psum", 1), sig("ry_stat", 1)
        ry_rstd, rya_ready, rya_psum, ysT_ret = sig("ry_rstd", 1), sig("rya_ready", 1), sig("rya_psum", 1), sig("ysT_ret", 1)
        cu_ready, cu_psum, cuT_ready = sig("cu_ready", 1), sig("cu_psum", 1), sig("cuT_ready", 1)
        cv_ready, cv_psum, cv_stat, cv_rstd = sig("cv_ready", 1), sig("cv_psum", 1), sig("cv_stat", 1), sig("cv_rstd", 1)
        cn_ready, cn_psum, ysT_conv = sig("cn_ready", 1), sig("cn_psum", 1), sig("ysT_conv", 1)
        gv_stat, gv_rstd, gv_ready = sig("gv_stat", 1), sig("gv_rstd", 1), sig("gv_ready", 1)
        gs_psum, gy_ready, gy_psum, ysT_gmlp = sig("gs_psum", 1), sig("gy_ready", 1), sig("gy_psum", 1), sig("ysT_gmlp", 1)
        sw_sumsq, sw_rstd, sw_norm, sw_psum = sig("sw_sumsq", 1), sig("sw_rstd", 1), sig("sw_norm", 1), sig("sw_psum", 1)
        sw_qT, sw_kT = sig("sw_qT", 1), sig("sw_kT", 1)
        sw_sc, sw_nm, sw_exp, sw_tr, sw_pT = sig("sw_sc", 8), sig("sw_nm", 8), sig("sw_exp", 8), sig("sw_tr", 8), sig("sw_pT", 8)
        sw_o, sw_sink, sw_esink, sy_ready, sy_psum, ysT_swa = (sig("sw_o", 8), sig("sw_sink", 1), sig("sw_esink", 1),
                                                               sig("sy_ready", 1), sig("sy_psum", 1), sig("ysT_swa", 1))
        mixT_psum, mixT_a, mixT_d = sig("mixT_psum", 4), sig("mixT_a", 4), sig("mixT_d", 4)
        ff_sg, ff_u, ff_uT = [sig(n, FF_PANELS, AHEAD) for n in ("ff_sg", "ff_u", "ff_uT")]
        w_hi_ready, w_lo_ready = sem("w_hi_ready"), sem("w_lo_ready")
        w_lo_d = sem("w_lo_d")
        first_used = sem("first_used")
        d_chain, g_chain = sem("d_chain"), sem("g_chain")

        c2_in, mem_in, prm2_in, hold_d, hold_g = sem("c2_in"), sem("mem_in"), sem("prm2_in"), sem("hold_d"), sem("hold_g")
        prm2_psum, prm2_ready = sem("prm2_psum"), sem("prm2_ready")
        z2_a, z2_d = sem("z2_a"), sem("z2_d")
        kvd_ready = sem("kvd_ready")
        rot2, blocks_ready = sem("rot2"), sem("blocks_ready")
        cmpT_psum, u2_a, u2_d, hid_ready = sem("cmpT_psum"), sem("u2_a"), sem("u2_d"), sem("hid_ready")
        kvc_psum, kcr_ready, kcT_psum, kcT_ready = sem("kvc_psum"), sem("kcr_ready"), sem("kcT_psum"), sem("kcT_ready")
        turn_psum, turn_a, turn_d = sem("turn_psum"), sem("turn_a"), sem("turn_d")
        gate_in, gate_ready = sem("gate_in"), sem("gate_ready")
        csc_psum, csc_ready, cexp, cprob, cprobT, pcT_ready = (sem(n) for n in ("csc_psum", "csc_ready", "cexp", "cprob", "cprobT", "pcT_ready"))
        at_sc, at_nm, at_exp, at_tr, at_pT, at_o, at_sum = (sem(n) for n in ("at_sc", "at_nm", "at_exp", "at_tr", "at_pT", "at_o", "at_sum"))
        oT_psum, oT_a, oT_d = sem("oT_psum"), sem("oT_a"), sem("oT_d")
        fg_in, fg_exp, fg_ln, fg_ready, fg_cum = (sem(n) for n in ("fg_in", "fg_exp", "fg_ln", "fg_ready", "fg_cum"))
        cf_tap, cf_cv, cf_silu, cf_uT = (sem(n) for n in ("cf_tap", "cf_cv", "cf_silu", "cf_uT"))

        JOBS = ([(0, "slc", i) for i in range(N_MIX)] + [(0, "win", i) for i in range(N_MIX)]
                + [(0, "mem", i) for i in range(N_MEM_H)]
                + [(1, "fgt", i) for i in range(N_MIX)] + [(1, "mem", i) for i in range(N_MEM_H)])
        LAST = [j for j, (f, kind, i) in enumerate(JOBS) if i == (N_MEM_H if kind == "mem" else N_MIX) - 1]

        def groups_before(j):
            return sum(j > e for e in LAST)

        block = ctx.enter_context(nc.Block())

        w_in2 = t["w_in"].rearrange("l k c -> (l k) c")
        w_br2 = t["w_branch"].rearrange("l n k c -> (l n k) c")
        w_out2 = t["w_out"].rearrange("l k c -> (l k) c")
        w_ffi2 = t["w_ffn_in"].rearrange("l k c -> (l k) c")
        w_ffo2 = t["w_ffn_out"].rearrange("l k c -> (l k) c")

        def rows(w, r0, k, c0, w_cols):
            return w[bass.ds(r0, k * P), :].rearrange("(k p) c -> p k c", p=P)[:, :, bass.ds(c0, w_cols)]

        def hi_half(n, b, size):
            return w_hi[:, (2 * n + b) % HI_SLOTS, 0:size]

        def half_of(buffer, n, b, size):
            return buffer[:, n % SLOTS, b * size:(b + 1) * size]

        def slot(i, k):
            return ring[:, i % SLOTS, :].rearrange("p (k c) -> p k c", k=k)

        EARLY = ("ident", "bucket", "window")

        @block.sync
        def _(sp):
            sp.dma_start(x[:, :, :], t["x"][0].rearrange("(t p) d -> p t d", p=P)).then_inc(x_in, 16)

            def load(layer, n, pieces):
                sp.wait_ge(*unit_done(layer, n + 1))
                for dst, src in pieces:
                    sp.dma_start(dst, src).then_inc(w_full[n % SLOTS].sem, 16)

            def split_k(n, w, r0, k, c0, w_cols):
                dst = slot(n, k) if w_cols * k == SLOT_W else ring[:, n % SLOTS, 0:k * w_cols].rearrange(
                    "p (k c) -> p k c", k=k)
                a = k // 2
                return [(dst[:, 0:a, :], rows(w, r0, a, c0, w_cols)),
                        (dst[:, a:k, :], rows(w, r0 + a * P, k - a, c0, w_cols))]

            def gate_up(n, w, r0, j):
                dst = slot(n, 4).rearrange("p k (a c) -> p k a c", a=2)
                return [(dst[:, :, a, :], rows(w, r0, 4, j * 256 + a * D_FF, 256)) for a in range(2)]

            with sp.Fori(0, DEPTH) as l:
                n = 0
                for k0 in (0, 4):
                    load(l, n, split_k(n, w_in2, l * D_MODEL + k0 * P, 4, 0, 512))
                    n += 1

                def prm_load(dst, src):
                    sp.dma_start(dst, src).then_inc(prm_in.sem, 16)

                def vec(name, r0, n):
                    prm_load(prm_raw[r0:r0 + n, :], t[name][bass.ds(l, 1), :].rearrange("a (r p) -> (a r) p", p=P))
                vec("norm1_g", R_N1, 8)
                vec("ret_gn_g", R_GN, 4)
                vec("conv_b", R_CB, 4)
                vec("conv_ln_g", R_CG, 4)
                vec("conv_ln_b", R_CLB, 4)
                vec("norm2_g", R_N2, 8)
                prm_load(prm_raw[R_BS:R_BS + 4, :], t["gmlp_bs"][bass.ds(l, 1), :, :].rearrange("a g s -> (a g) s"))
                for r, name in ((R_QG, "swa_q_g"), (R_KG, "swa_k_g")):
                    for a in range(2):
                        prm_load(prm_raw[r:r + 1, a * HD:(a + 1) * HD], t[name][bass.ds(l, 1), :])
                prm_load(cw_raw[:, :], t["conv_w"][bass.ds(l, 1), :, :, :].rearrange("a k o (c p) -> (a k o c) p", p=P))
                prm_load(ws_raw[:, :, :], t["gmlp_ws"][bass.ds(l, 1), :, :, :].rearrange("a g t s -> t (a g) s"))
                prm_load(lng[:, :], t["gmlp_ln_g"][bass.ds(l, 1), :].to_broadcast([P, MIX]))
                prm_load(lnb[:, :], t["gmlp_ln_b"][bass.ds(l, 1), :].to_broadcast([P, MIX]))
                prm_load(sinks[:, :], t["swa_sinks"][bass.ds(l, 1), :].to_broadcast([P, 8]))

                for c0 in [512 * p for p in range(9)] + [None]:
                    if c0 is None:
                        load(l, n, split_k(n, w_in2, l * D_MODEL, 8, SWA_C0 + 512, 256))
                        n += 1
                        continue
                    for k0 in (0, 4):
                        if c0:
                            load(l, n, split_k(n, w_in2, l * D_MODEL + k0 * P, 4, c0, 512))
                            n += 1
                for kind, b, hf, a, _ in MIX_STEPS:
                    if kind == "gate":
                        load(l, n, split_k(n, w_in2, l * D_MODEL + a * 4 * P, 4, GATE_C0 + b * D_MODEL + hf * 512, 512))
                    else:
                        load(l, n, split_k(n, w_br2, l * 4 * MIX + b * MIX, 4, hf * 512, 512))
                    n += 1
                for hf in range(2):
                    for k0 in (0, 4):
                        load(l, n, split_k(n, w_out2, l * D_MODEL + k0 * P, 4, hf * 512, 512))
                        n += 1
                assert n == U_FF

                def ff_panel(j, n, count):
                    for k0 in (0, 4):
                        m = n + k0 // 4
                        sp.wait_ge(unit_done.sem, count + k0 // 4 + 1)
                        for dst, src in gate_up(m, w_ffi2, l * D_MODEL + k0 * P, j):
                            sp.dma_start(dst, src).then_inc(w_full[m % SLOTS].sem, 16)
                ff_panel(0, U_FF, l * L_UNITS + U_FF)
                with sp.Fori(0, FF_PANELS // 2) as i:
                    for a in (1, 2):
                        ff_panel(i * 2 + a, U_FF + 2 * a, l * L_UNITS + i * 4 + (U_FF + 2 * a))
                n = U_DOWN
                for u in range(FF_KT // 2):
                    load(l, n, split_k(n, w_ffo2, l * D_FF + u * 2 * P, 2, 0, D_MODEL))
                    n += 1
                assert n == L_UNITS
            sp.wait_ge(*unit_done(DEPTH, 1))
            for name, tile in c2.items():
                sp.dma_start(tile, t[name]).then_inc(c2_in, 16)
            sp.dma_start(w2c, t["a_cmp_w2_2"][0].rearrange("v (k p) c -> p v k c", p=P)).then_inc(c2_in, 16)
            sp.dma_start(b2c, t["a_cmp_b2_2"].rearrange("o v c -> o (v c)").to_broadcast([P, 2 * HD])
                         .rearrange("p (v c) -> p v c", v=2)).then_inc(c2_in, 16)
            sp.dma_start(gate_b, t["a_gate_b_2"].to_broadcast([P, 36])).then_inc(c2_in, 16)
            sp.dma_start(f_b, t["b_fgate_2"].unsqueeze(0).to_broadcast([P, N_MIX])).then_inc(c2_in, 16)
            sp.dma_start(final_g, t["final_norm_2"].unsqueeze(0).to_broadcast([P, D_MODEL])).then_inc(c2_in, 16)
            sp.dma_start(mem, t["mem_2"][0].rearrange("(t p) d -> p t d", p=P)).then_inc(mem_in, 16)
            for name, r0, pattern in (("attn_norm_2", N2_ATT, "l (r p) -> (l r) p"), ("ffn_norm_2", N2_FFN, "l (r p) -> (l r) p"),
                                      ("mem_norm_2", N2_MEM, "l (r p) -> (l r) p"), ("kv_norm_2", N2_KV, "(r p) -> r p"),
                                      ("a_cmp_b1_2", N2_B1, "o v (r p) -> (o v r) p")):
                src = t[name].rearrange(pattern, p=P)
                sp.dma_start(prm2_raw[r0:r0 + src.shape[0], :], src).then_inc(prm2_in, 16)
            sp.dma_start(prm2_raw[N2_POS:N2_END, :], t["a_cmp_pos_2"].rearrange("o v (m j) d -> (o v m) (j d)", j=2)).then_inc(prm2_in, 16)
            for f in range(2):
                sp.dma_start(cv_raw[:, 4 * f:4 * f + 3, :], t["conv_w_2"][f].rearrange("k (r p) -> r k p", p=P)).then_inc(prm2_in, 16)
                sp.dma_start(cv_raw[:, 4 * f + 3, :], t["conv_b_2"][f].rearrange("(r p) -> r p", p=P)).then_inc(prm2_in, 16)

            def load_panel(n, w, c0, cols, r0=0):
                for a in range(2):
                    load(DEPTH, n + a, split_k(n + a, w, r0 + a * 4 * P, 4, c0, cols))

            def load_ffn(f):
                w_up2 = t["w_up_2"][f]
                for j in range(2):
                    for a in range(2):
                        m = U2_UP[f] + 2 * j + a
                        load(DEPTH, m, gate_up(m, w_up2, 4 * P * a, j))
                with sp.Fori(0, (FF_PANELS - 3) // 2) as i:
                    for b in (2, 3):
                        for a in range(2):
                            m = U2_UP[f] + 2 * b + a
                            sp.wait_ge(unit_done.sem, DEPTH * L_UNITS + m + 1 + i * 4)
                            for dst, src in gate_up(m, w_up2, 4 * P * a, i * 2 + b):
                                sp.dma_start(dst, src).then_inc(w_full[m % SLOTS].sem, 16)
                for a in range(2):
                    m = U2_UP[f] + 20 + a
                    load(DEPTH, m, gate_up(m, w_up2, 4 * P * a, 10))
                for u in range(FF_KT // 2):
                    load(DEPTH, U2_DOWN[f] + u, split_k(U2_DOWN[f] + u, t["w_down_2"][f], u * 2 * P, 2, 0, D_MODEL))

            for q, c0 in enumerate((0, 512, 1024, 1536)):
                load_panel(U2_PANEL[q], t["a_w_in_2"][0], c0, min(512, A_IN - c0))
            for f in range(2):
                load_panel(U2_PANEL[Q_MEM + f], t["w_mem_kv_2"][f], 0, 512)
            for kv in range(2):
                for a in range(2):
                    n = U2_CMP + 2 * kv + a
                    load(DEPTH, n, split_k(n, t["a_cmp_w1_2"][0, kv], a * 8 * P, 8, 0, CMP_HID))
            for f in range(2):
                if f:
                    for q, c0 in enumerate((0, 512, 1024, 1536)):
                        load_panel(U2_PANEL[Q_SHARED + q], t["w_kv_shared_2"], c0, min(512, SHARED - c0))
                    for q in range(2):
                        load_panel(U2_PANEL[Q_IN + q], t["b_w_in_2"][0], 512 * q, 512)
                for hf in range(2):
                    load_panel(U2_PANEL[Q_OUT[f] + hf], t["w_o_2"][f], 512 * hf, 512)
                load_ffn(f)
            for s in range(NT):
                sp.wait_ge(*h_ready(DEPTH, NT * NORM_FINAL + s + 1))
                sp.dma_start(out[0, s * P:(s + 1) * P, :], h[:, s, :]).then_inc(out_done, 16)
            sp.wait_ge(out_done, 16 * NT)

        @block.gpsimd
        def _(g):
            ch = Chain(g, g_chain)
            nc.gpsimd.memset(half[:, :], -0.5).then_inc(half_ready, 1)
            nc.gpsimd.memset(uTp[:, :, 0:30], 0.0).then_inc(pad_ready, 1)
            g.wait_ge(brow_ready, 1)
            g.dma_start(bass.AP(scratch.tensor, scratch.offset, [[P * SKEW + TRI, 8], [SKEW + 1, P], [1, TRI]]),
                        vrow[:, :].unsqueeze(1).to_broadcast([8, P, TRI])).then_inc(brow_out, 16)
            g.wait_ge(brow_out, 16)
            for c0, off in ((0, 127), (P, 255)):
                src = bass.AP(scratch.tensor, scratch.offset + off, [[SKEW, P], [P * SKEW + TRI, 8], [1, P]])
                g.dma_start(bias[:, :, c0:c0 + P], src).then_inc(bias_in, 16)

            def rsqrt(src, dst, n, scale, done, at=0):
                g.sem_inc(hold_g, 1)
                ch.link(nc.gpsimd.tensor_scalar(var[:, at:at + n], src, scale, EPS, ALU.mult, ALU.add))
                nc.gpsimd.tensor_tensor(dst, var[:, at:at + n], half[:, 0:n], ALU.pow).then_inc(done, 1)

            def norm(layer, k):
                for s in range(NT):
                    g.wait_ge(*sumsq(layer, NT * k + s + 1))
                    rsqrt(ss[:, s:s + 1], rstd[:, s:s + 1], 1, 1.0 / D_MODEL, rstd_ready.sem, s)

            def split_lo(n, b, before, size, count=1):
                g.wait_ge(w_hi_ready, before * 2 + (b + 1))
                g.sem_inc(hold_g, 1)
                nc.gpsimd.tensor_tensor(half_of(w_lo, n, b, size), half_of(ring, n, b, size),
                                        hi_half(n, b, size).bitcast(F32), ALU.subtract).then_inc(w_lo_ready, count)

            def layer_lo(first, last):
                for h_ in range(2 * first[0] + first[1], 2 * last[0] + last[1] + 1):
                    split_lo(h_ // 2, h_ % 2, l * L_UNITS + h_ // 2, HALF_W)

            def ffn_lo(n0, before):
                with g.Fori(0, D_HALVES // 2) as i:
                    for u in range(2, 6):
                        if u % 2:
                            split_lo(n0 + u, 0, before + i * 4 + u, HALF_W, 2)
                            continue
                        for b in range(2):
                            split_lo(n0 + u, b, before + i * 4 + u, HALF_W)
                for u in range(2 + 2 * D_HALVES, 3 * FF_PANELS):
                    for b in range(2):
                        split_lo(n0 + u, b, before + u, HALF_W)

            def second_lo(first, last):
                for h_ in range(2 * first[0] + first[1], 2 * last[0] + last[1] + 1):
                    n = h_ // 2
                    if n not in U2_WHOLE:
                        split_lo(n, h_ % 2, DEPTH * L_UNITS + split_before(n), half_size(n, True))

            g.wait_ge(half_ready, 1)
            with g.Fori(0, DEPTH) as l:
                norm(l, 0)
                layer_lo((0, 0), (14, 0))
                g.wait_ge(*ry_stat(l, 1))
                rsqrt(mv[:, :, 1], rs8[:, 0:8], 8, 1.0, ry_rstd.sem)
                layer_lo((14, 1), (17, 1))
                g.wait_ge(*gv_stat(l, 1))
                rsqrt(mv[:, 0:2, 1], rs8[:, 0:2], 2, 1.0, gv_rstd.sem)
                layer_lo((18, 0), (20, 1))
                g.wait_ge(*sw_sumsq(l, 1))
                rsqrt(ssw[:, 0:20], rs8[:, 0:20], 20, 1.0 / HD, sw_rstd.sem)
                layer_lo((21, 0), (37, 1))
                g.wait_ge(*cv_stat(l, 1))
                rsqrt(mv[:, 0:2, 1], rs8[:, 0:2], 2, 1.0, cv_rstd.sem)
                layer_lo((38, 0), (U_FF + 1, 0))
                norm(l, 1)
                layer_lo((U_FF + 1, 1), (U_FF + 1, 1))
                ffn_lo(U_FF, l * L_UNITS + U_FF)
                ch.restart()
            norm(DEPTH, NORM_ATT[0])
            second_lo((0, 0), (2, 1))
            norm(DEPTH, NORM_MEM)
            second_lo((3, 0), (U2_UP[0] + 1, 0))
            for f in range(2):
                up = U2_UP[f]
                norm(DEPTH, NORM_FFN[f])
                second_lo((up + 1, 1), (up + 1, 1))
                ffn_lo(up, DEPTH * L_UNITS + split_before(up))
                if f == 0:
                    end = up + 3 * FF_PANELS
                    second_lo((end, 0), (end + 1, 0))
                    norm(DEPTH, NORM_ATT[1])
                    second_lo((end + 1, 1), (U2_UP[1] + 1, 0))
            norm(DEPTH, NORM_FINAL)

        @block.tensor
        def _(pe):
            mm = nc.tensor.matmul
            tr = nc.tensor.transpose
            pe.wait_ge(early_in, 16 * len(EARLY))
            pe.sem_inc(unit_done.sem, SLOTS)
            pe.sem_inc(first_used, USED_AHEAD)
            pe.wait_ge(rel_in, 16)
            mm(T[3][0:8, 0:TRI], rel[:, :], const["bucket"][:, :], start=True, stop=True).then_inc(brow_psum, 1)
            pe.wait_ge(brow_ready, 1)

            def turn(bank, at, src, s, c0):
                return tr(bank[:, at:at + P], src[:, s, c0:c0 + P], ident[:, :])

            def rows8(src, banks):
                for c in range(4):
                    for s in range(NT):
                        ins = turn(banks[c // 2], (c % 2) * SEQ + s * P, src, s, c * P)
                return ins

            def rows16(src, done):
                for c in range(8):
                    for s in range(NT):
                        ins = turn(T[c // 2], (c % 2) * SEQ + s * P, src, s, c * P)
                    if c % 2:
                        ins.then_inc(done, 1)

            def norm_turned(layer, k):
                for s in range(NT):
                    pe.wait_ge(*h_ready(layer, NT * k + s + 1))
                    for c in range(KT):
                        ins = turn(T[c // 2], (c % 2) * SEQ + s * P, h, s, c * P)
                        if s == 1 and c % 2:
                            ins.then_inc(hT_psum.sem, 1)

            def multiply(banks, act, k0, weights, first, last):
                for s in range(NT):
                    for kk, w in enumerate(weights):
                        ins = mm(banks[s][:, 0:w.shape[-1]], act(k0 + kk, s), w,
                                 start=first and kk == 0, stop=last and kk == len(weights) - 1)
                ins.then_inc(unit_done.sem, 1)

            def three(bank, act, k, s, hi, lo, first, last):
                a_hi, a_lo = (a[:, k, s * P:(s + 1) * P] for a in act)
                mm(bank, a_hi, hi, start=first, stop=False)
                mm(bank, a_hi, lo, start=False, stop=False)
                return mm(bank, a_lo, hi, start=False, stop=last)

            def multiply_split(banks, act, n, before, k0, width, first, last, size=HALF_W, ready=None):
                tiles = size // width
                for b in range(2):
                    pe.wait_ge(w_lo_ready, before * 2 + (b + 1))
                    if ready:
                        pe.wait_ge(*ready((k0 + tiles * b) // 2))
                    for s in range(NT):
                        ins = split_part(banks, act, n, b, s, k0, width, first, last, size)
                    ins.then_inc(unit_done.sem if b else first_used, 1)

            def split_part(banks, act, n, b, s, k0, width, first, last, size):
                hi, lo = hi_half(n, b, size), half_of(w_lo, n, b, size)
                tiles = size // width
                for kk in range(tiles):
                    cols = slice(kk * width, (kk + 1) * width)
                    ins = three(banks[s][:, 0:width], act, k0 + tiles * b + kk, s, hi[:, cols], lo[:, cols],
                                first and b + kk == 0, last and b == 1 and kk == tiles - 1)
                return ins

            def by_tiles(part, before):
                for s in range(NT):
                    for b in range(2):
                        if s == 0:
                            pe.wait_ge(w_lo_ready, before * 2 + (b + 1))
                        ins = part(b, s)
                        if s == 0 and b == 1:
                            ins.then_inc(tile_done.sem, 1)
                        if s == 1:
                            ins.then_inc(unit_done.sem if b else first_used, 1)

            def multiply_T(banks, act, n, before, k0, first, last, ready=None, by_vector=None):
                for b in range(2):
                    pe.wait_ge(w_lo_ready, before * 2 + (b + 1))
                    if ready:
                        pe.wait_ge(*ready(k0 // 2 + b))
                    if b and by_vector is not None:
                        pe.wait_ge(w_lo_d, by_vector)
                    hi, lo = half_of_parts(n, b)
                    for c in range(4):
                        dst = banks[c // 2][:, (c % 2) * SEQ:(c % 2 + 1) * SEQ]
                        for kk in range(2):
                            k, cols = k0 + 2 * b + kk, slice(kk * 512 + c * P, kk * 512 + (c + 1) * P)
                            mm(dst, hi[:, cols], act[0][:, k, :], start=first and b + kk + c % 2 == 0, stop=False)
                            mm(dst, hi[:, cols], act[1][:, k, :], start=False, stop=False)
                            ins = mm(dst, lo[:, cols], act[0][:, k, :], start=False, stop=last and b + kk + c % 2 == 3)
                    ins.then_inc(unit_done.sem if b else first_used, 1)

            def half_of_parts(n, b):
                return hi_half(n, b, HALF_W), half_of(w_lo, n, b, HALF_W)

            def down_unit(n, u, before, by_vector):
                def part(b, s):
                    k = 2 * u + b
                    for hf in range(2):
                        cols = slice(hf * 512, (hf + 1) * 512)
                        ins = three(T[2 * s + hf][:, :], (uT_hi, uT_lo), k, s, hi_half(n, b, HALF_W)[:, cols],
                                    half_of(w_lo, n, b, HALF_W)[:, cols], k == 0, k == FF_KT - 1)
                    return ins
                if u == FF_KT // 2 - 1:
                    by_tiles(part, before)
                    return
                for b in range(2):
                    pe.wait_ge(w_lo_ready, before * 2 + (b + 1))
                    if b and u in (1, 3):
                        pe.wait_ge(w_lo_d, by_vector + (D_HALVES - 1 + u // 2))
                    for s in range(NT):
                        ins = part(b, s)
                    ins.then_inc(unit_done.sem if b else first_used, 1)

            turned = (hT_hi, hT_lo)

            with pe.Fori(0, DEPTH) as l:
                def banks_of(q):
                    if q >= 2:
                        pe.wait_ge(*z_a(l, taken("A", q - 2)))
                        pe.wait_ge(*z_d(l, taken("D", q - 2)))
                    return G[2 * (q % 2)], G[2 * (q % 2) + 1]

                def half_panel(q, a, ready=None):
                    n = end_of(q) - 2 + a
                    multiply_split(banks_of(q), turned, n, l * L_UNITS + n, 4 * a, 512, a == 0, a == 1, ready=ready)

                def panel(q, ready=None):
                    half_panel(q, 0, ready)
                    half_panel(q, 1, ready)

                pe.wait_ge(*prm_in(l, 16 * PRM_LOADS))
                pe.wait_ge(*x_new(l, NT))
                for c in range(4):
                    tr(T[2][:, c * P:(c + 1) * P], ws_raw[:, c, :], ident[:, :])
                tr(T[1][:, 0:124], cw_raw[:, :], ident[0:124, 0:124])
                ins = tr(T[0][:, 0:R_END], prm_raw[:, :], ident[0:R_END, 0:R_END])
                ins.then_inc(prm_psum.sem, 1)
                pe.wait_ge(*prm_ready(l, 1))

                norm_turned(l, 0)
                panel(0, lambda j: hT_d(l, j + 1))
                for q in range(1, 4):
                    panel(q)
                pe.wait_ge(*rot_ready(l, 1))
                rows16(h, rqk_psum.sem)
                panel(4)
                pe.wait_ge(*qT_ready(l, 1))
                pe.wait_ge(*kT_ready(l, 1))
                for i in range(4):
                    q_h, k_h = qkT[:, i // 2, (i % 2) * SEQ:(i % 2 + 1) * SEQ], kTt[:, i // 2, (i % 2) * SEQ:(i % 2 + 1) * SEQ]
                    mm(T[i][:, 0:SEQ], k_h[:, 0:P], q_h, start=True, stop=True)
                    mm(T[i][:, SEQ:TRI], k_h[:, P:SEQ], q_h[:, P:SEQ], start=True, stop=True).then_inc(rsc_psum.sem, 1)
                panel(5)
                pe.wait_ge(*rsc_ready(l, 4))
                pe.wait_ge(*z_a(l, taken("A", 2)))
                pe.wait_ge(*z_d(l, taken("D", 2)))
                for i in range(4):
                    v = [zr[:, s, 2, i * P:(i + 1) * P] for s in range(NT)]
                    cols = slice(i * P, (i + 1) * P)
                    mm(T[0][:, cols], scr[:, i, 0:P], v[0], start=True, stop=True)
                    mm(T[1][:, cols], scr[:, i, P:SEQ], v[0], start=True, stop=False)
                    ins = mm(T[1][:, cols], scr[:, i, SEQ:TRI], v[1], start=False, stop=True)
                ins.then_inc(ry_psum.sem, 1)
                panel(6)
                pe.wait_ge(*cu_ready(l, 1))
                rows8(mix, T[2:4]).then_inc(cu_psum.sem, 1)
                panel(7)
                panel(8)
                pe.wait_ge(*rya_ready(l, 1))
                rows8(yr, T[0:2]).then_inc(rya_psum.sem, 1)
                pe.wait_ge(*gv_ready(l, 1))
                pe.wait_ge(*cuT_ready(l, 1))
                for s in range(NT):
                    for c in range(4):
                        ins = mm(T[2 + s][:, c * P:(c + 1) * P], wsT[:, c, :], tmp[:, s, c * P:(c + 1) * P],
                                 start=True, stop=True)
                ins.then_inc(gs_psum.sem, 1)
                q, n = 9, end_of(9) - 1
                multiply_split(banks_of(q), turned, n, l * L_UNITS + n, 0, 256, True, True)
                pe.wait_ge(*gy_ready(l, 1))
                rows8(yg, T[2:4]).then_inc(gy_psum.sem, 1)

                def scores(i):
                    part = slice((i % 2) * HD, (i % 2 + 1) * HD)
                    q_h, k_h = swq[part, i // 2, :], swk[part, i // 4, :]
                    if i:
                        pe.wait_ge(*sw_nm(l, i))
                    mm(T[0][:, 0:P], q_h[:, 0:P], k_h[:, 0:P], start=True, stop=True)
                    mm(T[0][:, P:TRI], q_h[:, P:SEQ], k_h, start=True, stop=True).then_inc(sw_sc.sem, 1)

                def probs_T(i):
                    pe.wait_ge(*sw_exp(l, i + 1))
                    if i:
                        pe.wait_ge(*sw_pT(l, i))
                    for c in range(3):
                        ins = tr(T[1][:, c * P:(c + 1) * P], S[:, i % 4, c * P:(c + 1) * P], ident[:, :])
                    ins.then_inc(sw_tr.sem, 1)

                def values(i):
                    pe.wait_ge(*sw_pT(l, i + 1))
                    v = [zs[:, s, 640 + (i // 4) * HD:640 + (i // 4 + 1) * HD] for s in range(NT)]
                    cols = slice(i * HD, (i + 1) * HD)
                    p = pT[:, i % 2, :]
                    mm(T[2][:, cols], p[:, 0:P], v[0], start=True, stop=True)
                    mm(T[3][:, cols], p[:, P:SEQ], v[0], start=True, stop=False)
                    mm(T[3][:, cols], p[:, SEQ:TRI], v[1], start=False, stop=True).then_inc(sw_o.sem, 1)

                for u, (kind, b, hf, a, q) in enumerate(MIX_STEPS):
                    w = u - WINDOW_AT
                    if kind == "gate":
                        half_panel(q, a)
                    else:
                        if hf == 0:
                            pe.wait_ge(*{0: ysT_ret, 1: ysT_conv, 2: ysT_gmlp, 3: ysT_swa}[b](l, 1))
                        act = tuple(y[:, PLACE[b]] for y in (ysT_hi, ysT_lo))
                        multiply_split(banks_of(q), act, U_MIX + u, l * L_UNITS + (U_MIX + u), 0, 512, True, True)
                    if w == 0:
                        pe.wait_ge(*sw_norm(l, 1))
                        pe.wait_ge(*ysT_ret(l, 1))
                        pe.wait_ge(*ysT_gmlp(l, 1))
                        rows8(tmp, T[0:2])
                        for kv in range(2):
                            for s in range(NT):
                                ins = tr(T[2][:, kv * SEQ + s * P:kv * SEQ + (s + 1) * P],
                                         kdup[:, s, kv * P:(kv + 1) * P], ident[:, :])
                        ins.then_inc(sw_psum.sem, 1)
                    if w == 1:
                        pe.wait_ge(*sw_qT(l, 1))
                        pe.wait_ge(*sw_kT(l, 1))
                    if 1 <= w <= 8:
                        scores(w - 1)
                    if 2 <= w <= 9:
                        probs_T(w - 2)
                    if 3 <= w <= 10:
                        values(w - 3)
                    if w == 12:
                        pe.wait_ge(*sy_ready(l, 1))
                        rows8(h, T[0:2]).then_inc(sy_psum.sem, 1)
                    if u == 16:
                        pe.wait_ge(*cv_ready(l, 1))
                        for s in range(NT):
                            for c in range(4):
                                ins = tr(T[2 + s][:, c * P:(c + 1) * P], cacc[:, c, s * P:(s + 1) * P], ident[:, :])
                        ins.then_inc(cv_psum.sem, 1)

                    if u == 19:
                        pe.wait_ge(*cn_ready(l, 1))
                        pe.wait_ge(*ysT_swa(l, 1))
                        rows8(h[:, :, MIX:2 * MIX], T[0:2]).then_inc(cn_psum.sem, 1)
                pe.wait_ge(*z_d(l, taken("D", P_OUT - 1)))
                rows16(mix, mixT_psum.sem)
                panel(P_OUT, lambda j: mixT_d(l, j + 1))
                half_panel(P_OUT + 1, 0)
                banks, n = banks_of(P_OUT + 1), end_of(P_OUT + 1) - 1
                by_tiles(lambda b, s: split_part(banks, turned, n, b, s, 4, 512, False, True, HALF_W), l * L_UNITS + n)
                norm_turned(l, 1)

                def ff_panel(parity, n, more, j, ready=None, by_vector=None):
                    if j is not None:
                        pe.wait_ge(ff_u.sem, j)
                    for a in range(2):
                        multiply_T(G[2 * parity:2 * parity + 2], turned, n + a, l * L_UNITS + more + (n + a),
                                   4 * a, a == 0, a == 1, ready, by_vector if a else None)

                vector_before = l * D_HALVES
                panels_before = l * FF_PANELS + AHEAD
                ff_panel(0, U_FF, 0, None, lambda j: hT_d(l, 4 + j + 1))
                with pe.Fori(0, FF_PANELS // 2) as i:
                    ff_panel(1, U_FF + 2, i * 4, panels_before + i * 2, None, vector_before + i * 2 + 1)
                    ff_panel(0, U_FF + 4, i * 4, panels_before + i * 2 + 1, None, vector_before + i * 2 + 2)
                for u in range(FF_KT // 2):
                    n = U_DOWN + u
                    if u == 0:
                        pe.wait_ge(*ff_uT(l, FF_PANELS - 1))
                    if u == FF_KT // 2 - 1:
                        pe.wait_ge(*ff_uT(l, FF_PANELS))
                    down_unit(n, u, l * L_UNITS + n, vector_before)

            def arrived2(n):
                pe.wait_ge(*w_full[n % SLOTS](DEPTH, FILL * (n // SLOTS + 1)))

            def unit2(n, k, cols):
                return ring[:, n % SLOTS, 0:k * cols].rearrange("p (k c) -> p k c", k=k)

            def panel2(q, src, cols=512, ready=None):
                if q % 2 or q not in (Q_OUT[0], Q_SHARED, Q_OUT[1]):
                    if q >= 2:
                        pe.wait_ge(z2_a, taken2("A", q - 2))
                        pe.wait_ge(z2_d, taken2("D", q - 2))
                for a in range(2):
                    n = U2_PANEL[q] + a
                    if q in (Q_OUT[0] + 1, Q_OUT[1] + 1) and a == 1:
                        banks = G[2 * (q % 2):2 * (q % 2) + 2]
                        by_tiles(lambda b, s: split_part(banks, src, n, b, s, 4, 512, False, True, HALF_W),
                                 DEPTH * L_UNITS + split_before(n))
                        continue
                    if n not in U2_WHOLE:
                        multiply_split(G[2 * (q % 2):2 * (q % 2) + 2], src, n, DEPTH * L_UNITS + split_before(n), 4 * a, cols,
                                       a == 0, a == 1, 2 * cols, ready)
                        continue
                    arrived2(n)
                    w = unit2(n, 4, cols)
                    multiply(G[2 * (q % 2):2 * (q % 2) + 2], lambda k, s: src[:, k, s * P:(s + 1) * P], 4 * a,
                             [w[:, k, :] for k in range(4)], a == 0, a == 1)

            def ready_hT(k):
                return lambda j: hT_d(DEPTH, 4 * NORMS_SPLIT.index(k) + j + 1)

            def turn_pair(bank, half_, src, s, c0):
                return tr(bank[:, half_ * SEQ + s * P:half_ * SEQ + (s + 1) * P], src[:, s, c0:c0 + P], ident[:, :])

            pe.wait_ge(prm2_in, 16 * 10)
            pe.wait_ge(*x_new(DEPTH, NT))
            tr(T[0][:, 0:N2_END], prm2_raw, ident[0:N2_END, 0:N2_END])
            for a in range(8):
                ins = tr(T[1][:, 44 * a:44 * (a + 1)], cv_raw[:, a, :], ident[0:44, 0:44])
            ins.then_inc(prm2_psum, 1)
            pe.wait_ge(prm2_ready, 1)

            def attention(f, row_terms=None):
                jobs = [j for j, job in enumerate(JOBS) if job[0] == f]

                def scores(j):
                    _, kind, i = JOBS[j]
                    bank = T[j % 2]
                    part = slice((i % 2) * HD, (i % 2 + 1) * HD)
                    if j >= 2:
                        pe.wait_ge(at_exp if JOBS[j - 2][1] == "mem" else at_nm, j - 1)
                    if kind == "mem":
                        for s in range(NT):
                            ins = mm(bank[:, s * SEQ:(s + 1) * SEQ], qmT[part, i // 2, s * P:(s + 1) * P],
                                     mkT[f][part, i // 2, :], start=True, stop=True)
                        ins.then_inc(at_sc, 1)
                        return
                    q_h = qT2[part, i // 2, :]
                    k_h = kT2[part, {"slc": i // 6, "win": 2 + i // 6, "fgt": i // 2}[kind], :]
                    fgt = kind == "fgt"
                    mm(bank[:, 0:P], q_h[:, 0:P], k_h[:, 0:P], start=True, stop=not fgt)
                    if fgt:
                        n0, n1 = (nlf[:, s, i:i + 1].to_broadcast([P, P]) for s in range(NT))
                        mm(bank[:, 0:P], n0, upones[:, 0:P], start=False, stop=True)
                    ins = mm(bank[:, P:TRI], q_h[:, P:SEQ], k_h, start=True, stop=not fgt)
                    if fgt:
                        mm(bank[:, P:TRI], n0, upones, start=False, stop=False)
                        ins = mm(bank[:, SEQ:TRI], n1, upones[:, 0:P], start=False, stop=True)
                    ins.then_inc(at_sc, 1)

                def probs_T(j):
                    pe.wait_ge(at_exp, j + 1)
                    if j >= 2:
                        pe.wait_ge(at_pT, j - 1)
                    for c in range(4 if JOBS[j][1] == "mem" else 3):
                        ins = tr(T[2 + j % 2][:, c * P:(c + 1) * P], S4[:, j % 4, c * P:(c + 1) * P], ident[:, :])
                    ins.then_inc(at_tr, 1)

                def values(j):
                    _, kind, i = JOBS[j]
                    pe.wait_ge(at_pT, j + 1)
                    if i == 0:
                        pe.wait_ge(at_sum, groups_before(j) + 1)
                    p = pT4[:, j % 2, :]
                    if kind == "mem":
                        cols = slice(i * HD, (i + 1) * HD)
                        for s in range(NT):
                            for c in range(2):
                                ins = mm(G[2 * s][:, cols], p[:, (2 * s + c) * P:(2 * s + c + 1) * P],
                                         mkv[f][:, c, 256 + i * HD:256 + (i + 1) * HD], start=c == 0, stop=c == 1)
                        ins.then_inc(at_o, 1)
                        return
                    if kind == "fgt":
                        v_h = [zk[:, s, MIX_W + i * HD:MIX_W + (i + 1) * HD] for s in range(NT)]
                    else:
                        c0 = {"slc": 1152, "win": 1408}[kind] + (i // 6) * HD
                        v_h = [z2[:, s, c0:c0 + HD] for s in range(NT)]
                    cols = slice((i % 6) * HD, (i % 6 + 1) * HD)
                    mm(G[i // 6][:, cols], p[:, 0:P], v_h[0], start=True, stop=True)
                    mm(G[2 + i // 6][:, cols], p[:, P:SEQ], v_h[0], start=True, stop=False)
                    mm(G[2 + i // 6][:, cols], p[:, SEQ:TRI], v_h[1], start=False, stop=True).then_inc(at_o, 1)

                for step in range(len(jobs) + 2):
                    if step < len(jobs):
                        scores(jobs[step])
                    if 1 <= step <= len(jobs):
                        probs_T(jobs[step - 1])
                    if step >= 2:
                        values(jobs[step - 2])

            def out_and_ffn(f):
                pe.wait_ge(at_sum, 1 + (3 if f == 0 else 5))
                rows16(h, oT_psum)
                panel2(Q_OUT[f], turned, ready=lambda j: (oT_d, 4 * f + j + 1))
                panel2(Q_OUT[f] + 1, turned)
                norm_turned(DEPTH, NORM_FFN[f])
                done = f * FF_PANELS

                def up(j, parity, n, more, by_vector):
                    pe.wait_ge(cf_cv, AHEAD + done + j - 1)
                    up_units(parity, n, more, None, by_vector)

                def up_units(parity, n, more, ready=None, by_vector=None):
                    for a in range(2):
                        multiply_T(G[2 * parity:2 * parity + 2], turned, n + a,
                                   more + (DEPTH * L_UNITS + split_before(n + a)), 4 * a, a == 0, a == 1, ready, by_vector if a else None)

                n = U2_UP[f]
                up_units(0, n, 0, ready_hT(NORM_FFN[f]))
                vector_before = (DEPTH + f) * D_HALVES
                up_units(1, n + 2, 0, None, vector_before + 1)
                with pe.Fori(0, (FF_PANELS - 3) // 2) as i:
                    up(i * 2 + 2, 0, n + 4, i * 4, vector_before + 2 + i * 2)
                    up(i * 2 + 3, 1, n + 6, i * 4, vector_before + 3 + i * 2)
                up(10, 0, n + 20, 0, vector_before + 10)
                for u in range(FF_KT // 2):
                    if u == 0 or u >= 8:
                        pe.wait_ge(cf_uT, AHEAD + done + (8 if u == 0 else u + 1))
                    n = U2_DOWN[f] + u
                    down_unit(n, u, DEPTH * L_UNITS + split_before(n), (DEPTH + f) * D_HALVES)

            norm_turned(DEPTH, NORM_ATT[0])
            for q in range(2):
                panel2(q, turned, ready=None if q else ready_hT(NORM_ATT[0]))
            norm_turned(DEPTH, NORM_MEM)
            panel2(2, turned)
            pe.wait_ge(memT_a, 1)
            pe.wait_ge(memT_d, 1)
            panel2(3, turned, A_IN - 1536)
            pe.wait_ge(kvd_ready, 1)
            for kv in range(2):
                for g2 in range(2):
                    for s in range(NT):
                        ins = tr(T[kv][:, g2 * SEQ + s * P:g2 * SEQ + (s + 1) * P],
                                 kvd[:, s, (2 * kv + g2) * P:(2 * kv + g2 + 1) * P], ident[:, :])
            ins.then_inc(cmpT_psum, 1)
            panel2(Q_MEM, memT[0])
            panel2(Q_MEM + 1, memT[1])
            pe.wait_ge(blocks_ready, 1)
            for kv in range(2):
                n = U2_CMP + 2 * kv
                arrived2(n)
                arrived2(n + 1)
                for ht in range(2):
                    for m in range(16):
                        w = unit2(n + m // 8, 8, CMP_HID)
                        ins = mm(T[2][:, (2 * kv + ht) * HD:(2 * kv + ht + 1) * HD], w[:, m % 8, ht * P:(ht + 1) * P],
                                 blocks[:, kv, m, :, :], start=m == 0, stop=m == 15)
                        if ht == 1 and m % 8 == 7:
                            ins.then_inc(unit_done.sem, 1)
            pe.wait_ge(rot2, 1)
            pe.wait_ge(u2_a, 1)
            pe.wait_ge(u2_d, 1)
            for c in range(4):
                for s in range(NT):
                    ins = turn_pair(T[c // 2], c % 2, h, s, c * P)
            ins.then_inc(turn_psum, 1)
            pe.wait_ge(hid_ready, 1)
            for kv in range(2):
                for g2 in range(2):
                    for ht in range(2):
                        ins = mm(T[3][:, (2 * kv + g2) * HD:(2 * kv + g2 + 1) * HD],
                                 h1T[:, kv, ht, g2, :],
                                 w2c[:, kv, ht, :], start=ht == 0, stop=ht == 1)
            ins.then_inc(kvc_psum, 1)
            pe.wait_ge(kcr_ready, 1)
            for g2 in range(2):
                ins = tr(T[3][:, g2 * 16:g2 * 16 + N_CMP], kcr[0:N_CMP, g2, :],
                         ident[0:N_CMP, 0:N_CMP])
            ins.then_inc(kcT_psum, 1)
            for c in range(4, 6):
                for s in range(NT):
                    ins = turn_pair(T[2], c % 2, h, s, c * P)
            ins.then_inc(turn_psum, 1)
            pe.wait_ge(turn_a, 1)
            for c in range(2):
                for s in range(NT):
                    ins = turn_pair(T[1], c, z2, s, 1572 + c * P)
            ins.then_inc(turn_psum, 1)
            pe.wait_ge(kcT_ready, 1)
            for br in range(2):
                for g2 in range(2):
                    for s in range(NT):
                        c0 = (2 * br + g2) * P
                        ins = tr(T[3 * br][:, g2 * SEQ + s * P:g2 * SEQ + (s + 1) * P], kd2[:, s, c0:c0 + P], ident[:, :])
            ins.then_inc(turn_psum, 1)
            pe.wait_ge(turn_d, 1)
            pe.wait_ge(turn_a, 2)
            pe.wait_ge(z2_a, taken2("A", Q_MEM + 1))
            pe.wait_ge(z2_d, taken2("D", Q_MEM + 1))
            for f in range(2):
                for c in range(2):
                    for s in range(NT):
                        ins = turn_pair(T[2 - f], c, mkv[f], s, c * P)
            ins.then_inc(turn_psum, 1)
            pe.wait_ge(turn_a, 4)
            pe.wait_ge(turn_d, 2)
            for s in range(NT):
                for i in range(N_MIX):
                    part = slice((i % 2) * HD, (i % 2 + 1) * HD)
                    at_c = (s * 6 + i // 2) * N_CMP
                    ins = mm(T[i % 2][:, at_c:at_c + N_CMP], qT2[part, i // 2, s * P:(s + 1) * P],
                       kcT[part, i // 6, 0:N_CMP], start=True, stop=True)
            ins.then_inc(csc_psum, 1)
            pe.wait_ge(cprob, 1)
            for s in range(NT):
                for c in range(3):
                    ins = tr(T[2 + s][:, c * P:(c + 1) * P], Sc[:, s, 4 * c:4 * c + 4, :].rearrange("p h n -> p (h n)"), ident[:, :])
            ins.then_inc(cprobT, 1)
            pe.wait_ge(pcT_ready, 1)
            for s in range(NT):
                for i in range(N_MIX):
                    part = slice(32 * (i % 4), 32 * (i % 4) + N_CMP)
                    at_c = (s * 3 + i // 4) * HD
                    ins = mm(G[i % 4][:, at_c:at_c + HD], pcT[part, s, i // 4, :],
                             kvc[part, 1, i // 6, :], start=True, stop=True)
            ins.then_inc(at_o, 1)
            attention(0)
            out_and_ffn(0)

            norm_turned(DEPTH, NORM_ATT[1])
            for q in range(4):
                panel2(Q_SHARED + q, (hsT_hi, hsT_lo), min(512, SHARED - 512 * q), None if q else ready_hT(NORM_ATT[1]))
            for q in range(2):
                panel2(Q_IN + q, turned)
            pe.wait_ge(z2_a, taken2("A", Q_IN + 1))
            pe.wait_ge(z2_d, taken2("D", Q_IN + 1))
            for c in range(8):
                for s in range(NT):
                    ins = turn_pair(T[c // 2], c % 2, zq, s, c * P)
            ins.then_inc(turn_psum, 1)
            pe.wait_ge(turn_a, 5)
            pe.wait_ge(turn_d, 3)
            for c in range(6):
                for s in range(NT):
                    ins = turn_pair(T[c // 2], c % 2, zk, s, c * P)
            ins.then_inc(turn_psum, 1)
            pe.wait_ge(fg_ready, 1)
            mm(T[3][:, 0:N_MIX], upones[:, 0:P], nlf[:, 0, :], start=True, stop=True)
            mm(T[3][:, N_MIX:2 * N_MIX], upones[:, 0:P], nlf[:, 1, :], start=True, stop=False)
            mm(T[3][:, N_MIX:2 * N_MIX], upones[:, P:SEQ], nlf[:, 0, :], start=False, stop=True).then_inc(fg_cum, 1)
            pe.wait_ge(turn_a, 6)
            pe.wait_ge(turn_d, 4)
            attention(1)
            out_and_ffn(1)

        @block.scalar
        def _(act):
            def copy(dst, src, func=ACT.Copy, **more):
                return nc.scalar.activation(dst, src, func, **more)

            for name in sorted(const, key=lambda n: n not in EARLY):
                tile = const[name]
                act.dma_start(tile[tuple(slice(None) for _ in tile.shape)], t[name]).then_inc(
                    early_in if name in EARLY else const_in, 16)
                if name == EARLY[0]:
                    act.dma_start(rel[:, :], t["rel_bias"]).then_inc(rel_in, 16)
            act.sem_inc(ff_sg.sem, AHEAD)

            def split_hi(n, b, size, filled, used, done):
                if b == 0:
                    act.wait_ge(w_full[n % SLOTS].sem, filled)
                    act.wait_ge(first_used, used)
                else:
                    act.wait_ge(unit_done.sem, done)
                copy(hi_half(n, b, size), half_of(ring, n, b, size)).then_inc(w_hi_ready, 1)

            class Splits:

                def __init__(self, split):
                    self.split, self.next = split, 0

                def upto(self, n, b):
                    while self.next <= 2 * n + b:
                        self.split(self.next // 2, self.next % 2)
                        self.next += 1

                def skip_to(self, n):
                    self.next = 2 * n

            def norm_hi(layer, k, outs):
                for c in range(KT):
                    act.wait_ge(*hT_psum(layer, 4 * k + c // 2 + 1))
                    for dst, gains, row in outs:
                        ins = copy(dst[:, c, :], T[c // 2][:, (c % 2) * SEQ:(c % 2 + 1) * SEQ],
                                   scale=gains[:, row + c:row + c + 1])
                    ins.then_inc(hT_hi_ready.sem, 1)

            with act.Fori(0, DEPTH) as l:
                def split_layer(n, b, more=0):
                    split_hi(n, b, HALF_W, l * (FILL * L_UNITS // SLOTS) + more * (FILL // SLOTS) + FILL * (n // SLOTS + 1),
                             l * L_UNITS + more + (USED_AHEAD + n - 1), l * L_UNITS + more + (SLOTS + n - 1))
                splits = Splits(split_layer)

                def multiplied(n):
                    splits.upto(n + 1, 0)
                    act.wait_ge(*unit_done(l, SLOTS + n))

                def norm_sums(k):
                    for s in range(NT):
                        act.wait_ge(*x_new(l, NT * k + s + 1))
                        copy(h[:, s, :], x[:, s, :], ACT.Square, accum_out=ss[:, s:s + 1]).then_inc(sumsq.sem, 1)

                def take(q, dst, func=ACT.Copy, tiles=(0,), **more):
                    multiplied(end_of(q))
                    for s in tiles:
                        b = G[2 * (q % 2) + s]
                        ins = copy(dst(s), b[:, 0:dst(s).shape[-1]], func, **more)
                    ins.then_inc(z_a.sem, 1)

                norm_sums(0)
                splits.upto(1, 1)
                act.wait_ge(*prm_ready(l, 1))
                norm_hi(l, 0, [(hT_hi, prm, R_N1)])
                for q in range(3):
                    take(q, lambda s: zr[:, s, q, :])
                take(3, lambda s: zr[:, s, 3, :], ACT.Silu, (0, 1))
                for b in range(2):
                    splits.upto(end_of(3) + 1, 0)
                    act.wait_ge(*rqk_psum(l, b + 1))
                    if b == 0:
                        act.wait_ge(*rot_ready(l, 1))
                    ins = copy(qkT[:, b, :], T[b][:, :])
                ins.then_inc(qT_ready.sem, 1)
                take(4, lambda s: zc[:, s, 0, :])
                take(5, lambda s: zc[:, s, 1, :], ACT.Tanh, (0, 1), scale=0.5)
                take(6, lambda s: zg[:, s, 0, :], ACT.Gelu_apprx_tanh, (0, 1))
                splits.upto(end_of(6) + 1, 0)
                act.wait_ge(*cu_psum(l, 1))
                act.wait_ge(pad_ready, 1)
                for b in range(2):
                    ins = copy(uTp[:, 2 * b:2 * b + 2, 30:30 + SEQ],
                               T[2 + b][:, :].rearrange("p (c s) -> p c s", c=2), scale=0.5)
                ins.then_inc(cuT_ready.sem, 1)
                take(7, lambda s: zg[:, s, 1, :], ACT.Gelu_apprx_tanh, (0, 1))
                take(8, lambda s: zs[:, s, 0:512])
                splits.upto(end_of(8) + 1, 0)
                act.wait_ge(*rya_psum(l, 1))
                for c in range(4):
                    ins = copy(ysT_hi[:, PLACE[0], c, :], T[c // 2][:, (c % 2) * SEQ:(c % 2 + 1) * SEQ],
                               scale=prm[:, R_GN + c:R_GN + c + 1])
                ins.then_inc(ysT_hi_ready.sem, 1)
                take(9, lambda s: zs[:, s, 512:768])
                splits.upto(end_of(9) + 1, 0)
                act.wait_ge(*gy_psum(l, 1))
                for b in range(2):
                    ins = copy(ysT_hi[:, PLACE[2], 2 * b:2 * b + 2, :], T[2 + b][:, :].rearrange("p (c s) -> p c s", c=2))
                ins.then_inc(ysT_hi_ready.sem, 1)

                for u, (kind, b, hf, a, q) in enumerate(MIX_STEPS):
                    w = u - WINDOW_AT
                    splits.upto(U_MIX + u + 2, 0)
                    if kind == "gate" and a == 1:
                        if hf == 0 and b in (3, 1):
                            act.wait_ge(*z_d(l, taken("D", P_BRANCH[{3: 0, 1: 2}[b]] + 1)))
                        take(q, lambda s: gates[:, PLACE[b], s, hf * 512:(hf + 1) * 512], ACT.Tanh, (0, 1), scale=0.5)
                    if w == 0:
                        act.wait_ge(*sw_psum(l, 1))
                        copy(swk[:, :, :], T[2][:, :].rearrange("p (c s) -> p c s", c=2),
                             scale=prm[:, R_KG:R_KG + 1]).then_inc(sw_kT.sem, 1)
                    if 1 <= w <= 8:
                        i = w - 1
                        act.wait_ge(*sw_nm(l, i + 1))
                        copy(S[:, i % 4, 0:P], S[:, i % 4, 0:P], ACT.Exp, bias=nm[:, i, 0:1], accum_out=rsum[:, i, 0:1])
                        copy(S[:, i % 4, P:TRI], S[:, i % 4, P:TRI], ACT.Exp, bias=nm[:, i, 1:2],
                             accum_out=rsum[:, i, 1:2]).then_inc(sw_exp.sem, 1)
                    if 2 <= w <= 9:
                        i = w - 2
                        act.wait_ge(*sw_tr(l, i + 1))
                        if i >= 2:
                            act.wait_ge(*sw_o(l, i - 1))
                        copy(pT[:, i % 2, 0:TRI], T[1][:, 0:TRI]).then_inc(sw_pT.sem, 1)
                    if w == 10:
                        act.wait_ge(*sw_sink(l, 1))
                        copy(es[:, 0:8, :], es[:, 0:8, :], ACT.Exp).then_inc(sw_esink.sem, 1)
                    if w == 12:
                        act.wait_ge(*sy_psum(l, 1))
                        act.wait_ge(*unit_done(l, SLOTS + end_of(P_BRANCH[0] + 1)))
                        for j in range(2):
                            ins = copy(ysT_hi[:, PLACE[3], 2 * j:2 * j + 2, :], T[j][:, :].rearrange("p (c s) -> p c s", c=2))
                        ins.then_inc(ysT_hi_ready.sem, 1)
                    if u == 19:
                        act.wait_ge(*cn_psum(l, 1))
                        for c in range(4):
                            ins = copy(cacc[:, c, :], T[c // 2][:, (c % 2) * SEQ:(c % 2 + 1) * SEQ], ACT.Silu,
                                       scale=prm[:, R_CG + c:R_CG + c + 1], bias=prm[:, R_CLB + c:R_CLB + c + 1])
                        ins.then_inc(cs_ready.sem, 1)
                for b in range(4):
                    act.wait_ge(*mixT_psum(l, b + 1))
                    copy(hT_hi[:, 2 * b:2 * b + 2, :], T[b][:, :].rearrange("p (c s) -> p c s", c=2),
                         scale=0.5).then_inc(mixT_a.sem, 1)
                splits.upto(U_FF + 1, 0)
                norm_sums(1)
                splits.upto(U_FF + 1, 1)
                norm_hi(l, 1, [(hT_hi, prm, R_N2)])

                def ff_split(u, more=0):
                    for b in range(2):
                        split_layer(U_FF + u, b, more)

                def ff_silu(parity, units, free):
                    act.wait_ge(unit_done.sem, units)
                    if free is not None:
                        act.wait_ge(ff_u.sem, free)
                    copy(sg[:, parity, :], G[2 * parity][:, :], ACT.Silu).then_inc(ff_sg.sem, 1)

                units = l * L_UNITS + (SLOTS + U_FF)
                before = l * FF_PANELS + AHEAD
                ff_split(2)
                ff_split(3)
                ff_silu(0, units + 2, None)
                with act.Fori(0, FF_PANELS // 2) as i:
                    ff_split(4, i * 4)
                    ff_split(5, i * 4)
                    ff_silu(1, units + i * 4 + 4, before + i * 2)
                    ff_split(6, i * 4)
                    ff_split(7, i * 4)
                    ff_silu(0, units + i * 4 + 6, before + i * 2 + 1)
                for u in range(2 * FF_PANELS + 2, 3 * FF_PANELS):
                    ff_split(u)

            def split_second(n, b, more=0):
                if n in U2_WHOLE:
                    return
                split_hi(n, b, half_size(n, True), more * (FILL // SLOTS) + FILL * (DEPTH * L_UNITS // SLOTS + n // SLOTS + 1),
                         more + (USED_AHEAD + DEPTH * L_UNITS + split_before(n - 1)), more + (DEPTH * L_UNITS + SLOTS + n - 1))
            splits2 = Splits(split_second)

            def norm_sums2(k, src, new):
                if not new:
                    act.wait_ge(mem_in, 16)
                    act.wait_ge(*hT_psum(DEPTH, 4 * k))
                for s in range(NT):
                    if new:
                        act.wait_ge(*x_new(DEPTH, NT * (new - 1) + s + 1))
                    copy(h[:, s, :], src[:, s, :], ACT.Square, accum_out=ss[:, s:s + 1]).then_inc(sumsq.sem, 1)

            def norm_T2(k, outs):
                for c in range(4):
                    act.wait_ge(*hT_psum(DEPTH, 4 * k + c // 2 + 1))
                    for dst, row in outs:
                        ins = copy(dst[:, c, :], T[c // 2][:, (c % 2) * SEQ:(c % 2 + 1) * SEQ],
                                   scale=prm2[:, row + c:row + c + 1])
                ins.then_inc(memT_a, 1)

            def take2(q, dst):
                splits2.upto(U2_PANEL[q] + 3, 0)
                act.wait_ge(*unit_done(DEPTH, SLOTS + U2_PANEL[q] + 2))
                copy(dst, G[2 * (q % 2)][:, 0:dst.shape[-1]]).then_inc(z2_a, 1)

            def pairs(bank):
                return bank[:, :].rearrange("p (c s) -> p c s", s=SEQ)

            def attention_a(f):
                for j, (layer, kind, i) in enumerate(JOBS):
                    if layer != f:
                        continue
                    rs = rsums[:, groups_before(j) % 2]
                    act.wait_ge(at_nm, j + 1)
                    if j >= 4:
                        act.wait_ge(at_tr, j - 3)
                    if kind == "mem":
                        bank = T[j % 2]
                        copy(S4[:, j % 4, 0:SEQ], bank[:, 0:SEQ], ACT.Exp, bias=nm[:, i, 0:1], accum_out=rs[:, i, 0:1])
                        copy(S4[:, j % 4, SEQ:512], bank[:, SEQ:512], ACT.Exp, bias=nm[:, i, 1:2],
                             accum_out=rs[:, i, 1:2]).then_inc(at_exp, 1)
                        continue
                    p = S4[:, j % 4, :]
                    copy(p[:, 0:P], p[:, 0:P], ACT.Exp, bias=nm[:, i, 0:1], accum_out=rs[:, i, 0:1])
                    copy(p[:, P:TRI], p[:, P:TRI], ACT.Exp, bias=nm[:, i, 1:2],
                         accum_out=rs[:, i, 1:2]).then_inc(at_exp, 1)

            def out_and_ffn_a(f):
                for b in range(4):
                    act.wait_ge(oT_psum, 4 * f + b + 1)
                    copy(hT_hi[:, 2 * b:2 * b + 2, :], pairs(T[b])).then_inc(oT_a, 1)
                def up_split(u, more=0):
                    for b in range(2):
                        split_second(U2_UP[f] + u, b, more)
                splits2.upto(U2_UP[f] + 1, 0)
                norm_sums2(NORM_FFN[f], x, 2 + 2 * f)
                splits2.upto(U2_UP[f] + 1, 1)
                norm_hi(DEPTH, NORM_FFN[f], [(hT_hi, prm2, N2_FFN + 8 * f)])
                done = f * FF_PANELS
                units = DEPTH * L_UNITS + SLOTS + U2_UP[f]

                def tap(j, parity, used=True):
                    act.wait_ge(unit_done.sem, units + 2 + j * 2)
                    if used:
                        act.wait_ge(cf_uT, AHEAD + done + j - 1)
                    for b in range(2):
                        for c in range(2):
                            tile = 22 * b + j * 2 + c
                            ins = copy(accv[:, parity, 2 * b + c, :], G[2 * parity + b][:, c * SEQ:(c + 1) * SEQ], ACT.Identity,
                                       scale=cvp[:, f, 2, bass.ds(tile, 1)], bias=cvp[:, f, 3, bass.ds(tile, 1)])
                        ins.then_inc(cf_tap, 1)

                def silu(j, parity):
                    act.wait_ge(cf_cv, AHEAD + done + j + 1)
                    copy(accv[:, parity, 0:2, :], accv[:, parity, 0:2, :], ACT.Silu).then_inc(cf_silu, 1)

                up_split(2)
                up_split(3)
                tap(0, 0, False)
                with act.Fori(0, FF_PANELS // 2) as i:
                    up_split(4, i * 4)
                    up_split(5, i * 4)
                    tap(i * 2 + 1, 1)
                    silu(i * 2, 0)
                    up_split(6, i * 4)
                    up_split(7, i * 4)
                    tap(i * 2 + 2, 0)
                    silu(i * 2 + 1, 1)
                silu(FF_PANELS - 1, 0)
                for u in range(2 * FF_PANELS + 2, 3 * FF_PANELS):
                    up_split(u)
                splits2.skip_to(U2_UP[f] + 3 * FF_PANELS)

            norm_sums2(NORM_ATT[0], x, 1)
            splits2.upto(1, 1)
            act.wait_ge(prm2_ready, 1)
            norm_hi(DEPTH, NORM_ATT[0], [(hT_hi, prm2, N2_ATT)])
            norm_sums2(NORM_MEM, mem, None)
            for q in range(2):
                take2(q, z2[:, 0, 512 * q:512 * (q + 1)])
            norm_T2(NORM_MEM, [(memT[0], N2_MEM), (memT[1], N2_MEM + 8)])
            take2(2, z2[:, 0, 1024:1536])
            take2(3, z2[:, 0, 1536:A_IN])
            act.wait_ge(cmpT_psum, 1)
            copy(u2[0:HD, 0:2, :], pairs(T[0])[0:HD])
            copy(u2[HD:P, 0:2, 0:SEQ - 1], pairs(T[0])[HD:P, :, 1:SEQ]).then_inc(u2_a, 1)
            take2(Q_MEM, mkv[0][:, 0, :])
            take2(Q_MEM + 1, mkv[1][:, 0, :])
            act.wait_ge(gate_in, 1)
            copy(gsig, gsig, ACT.Sigmoid).then_inc(gate_ready, 1)
            act.wait_ge(*unit_done(DEPTH, SLOTS + U2_CMP + 4))
            for kv in range(2):
                for ht in range(2):
                    ins = copy(h1T[:, kv, ht, :, :].rearrange("p g (a n) -> p g a n", a=4),
                               T[2][:, (2 * kv + ht) * HD:(2 * kv + ht + 1) * HD].rearrange("p (g n) -> p g n", g=2)
                               .unsqueeze(2).to_broadcast([P, 2, 4, CMP_PAD]), ACT.Gelu_apprx_tanh,
                               bias=prm2[:, N2_B1 + 2 * kv + ht:N2_B1 + 2 * kv + ht + 1])
            ins.then_inc(hid_ready, 1)
            act.wait_ge(turn_psum, 1)
            copy(qT2[:, 0:2, :], pairs(T[0]), scale=HD ** -0.5)
            copy(qT2[:, 2:4, :], pairs(T[1]), scale=HD ** -0.5).then_inc(turn_a, 1)
            act.wait_ge(turn_psum, 3)
            copy(qmT[:, :, :], pairs(T[1]), scale=HD ** -0.5).then_inc(turn_a, 1)
            act.wait_ge(turn_psum, 4)
            copy(kT2[:, 0:2, :], pairs(T[0])).then_inc(turn_a, 1)
            act.wait_ge(turn_psum, 5)
            copy(mkT[1][:, :, :], pairs(T[1])).then_inc(turn_a, 1)
            act.wait_ge(csc_ready, 1)
            copy(Sc[:, :, :, 0:N_CMP], Sc[:, :, :, 0:N_CMP], ACT.Exp).then_inc(cexp, 1)
            splits2.upto(U2_PANEL[Q_OUT[0]] + 1, 1)
            attention_a(0)
            out_and_ffn_a(0)

            splits2.upto(U2_PANEL[Q_SHARED] + 1, 0)
            norm_sums2(NORM_ATT[1], x, 3)
            splits2.upto(U2_PANEL[Q_SHARED] + 1, 1)
            norm_hi(DEPTH, NORM_ATT[1], [(hT_hi, prm2, N2_ATT + 8), (hsT_hi, prm2, N2_KV)])
            for q in range(4):
                take2(Q_SHARED + q, zk[:, 0, 512 * q:min(512 * (q + 1), SHARED)])
            act.wait_ge(fg_in, 1)
            copy(ef, ef, ACT.Exp).then_inc(fg_exp, 1)
            act.wait_ge(fg_exp, 1)
            copy(ef, ef, ACT.Ln, bias=1.0).then_inc(fg_ln, 1)
            for q in range(2):
                take2(Q_IN + q, zq[:, 0, 512 * q:512 * (q + 1)])
            for b in range(2):
                if b == 0:
                    act.wait_ge(turn_psum, 6)
                ins = copy(qT2[:, 2 * b:2 * b + 2, :], pairs(T[b]), scale=HD ** -0.5)
            ins.then_inc(turn_a, 1)
            act.wait_ge(turn_psum, 7)
            for b in range(2):
                ins = copy(kT2[:, 2 * b:2 * b + 2, :], pairs(T[b]))
            ins.then_inc(turn_a, 1)
            splits2.upto(U2_PANEL[Q_OUT[1]] + 1, 1)
            attention_a(1)
            out_and_ffn_a(1)
            norm_sums2(NORM_FINAL, x, 5)

        @block.vector
        def _(dve):
            v = nc.vector
            ch = Chain(dve, d_chain)
            dve.wait_ge(x_in, 16)
            dve.sem_inc(x_new.sem, NT)
            dve.sem_inc(ff_u.sem, AHEAD)
            dve.sem_inc(ff_uT.sem, AHEAD)
            dve.sem_inc(cf_cv, AHEAD)
            dve.sem_inc(cf_uT, AHEAD)
            dve.wait_ge(early_in, 16 * len(EARLY))
            dve.wait_ge(brow_psum, 1)
            v.tensor_tensor(vrow[:, :], T[3][0:8, 0:TRI], const["window"][:, :], ALU.add).then_inc(brow_ready, 1)
            dve.wait_ge(const_in, 16 * (len(const) - len(EARLY)))

            def split_lo(n, before):
                dve.wait_ge(w_hi_ready, before * 2 + 2)
                v.tensor_tensor(half_of(w_lo, n, 1, HALF_W), half_of(ring, n, 1, HALF_W), hi_half(n, 1, HALF_W).bitcast(F32),
                                ALU.subtract).then_inc(w_lo_d, 1)

            def norm_lo(layer, index, outs):
                for c in range(KT):
                    dve.wait_ge(*hT_hi_ready(layer, KT * index + c // 2 * 2 + 2))
                    for lo, hi, gains, row in outs:
                        ins = v.scalar_tensor_tensor(lo[:, c, :], T[c // 2][:, (c % 2) * SEQ:(c % 2 + 1) * SEQ],
                                                     gains[:, row + c:row + c + 1], hi[:, c, :].bitcast(F32),
                                                     ALU.mult, ALU.subtract)
                    if c % 2:
                        ins.then_inc(hT_d.sem, 1)

            def pairs(bank):
                return bank[:, :].rearrange("p (c s) -> p c s", s=SEQ)

            with dve.Fori(0, DEPTH) as l:
                def multiplied(n):
                    dve.wait_ge(*unit_done(l, SLOTS + n))

                def take(q, dst):
                    multiplied(end_of(q))
                    v.tensor_copy(dst, G[2 * (q % 2) + 1][:, 0:dst.shape[-1]]).then_inc(z_d.sem, 1)

                def norm_rows(k):
                    for s in range(NT):
                        dve.wait_ge(*rstd_ready(l, NT * k + s + 1))
                        v.tensor_scalar(h[:, s, :], x[:, s, :], rstd[:, s:s + 1], None, ALU.mult).then_inc(h_ready.sem, 1)

                dve.wait_ge(*prm_psum(l, 1))
                v.tensor_copy(prm[:, :], T[0][:, 0:R_END])
                v.tensor_copy(cw[:, :], T[1][:, 0:124])
                v.tensor_tensor(wsT[:, :, :], T[2][:, :].rearrange("p (c s) -> p c s", c=4),
                                upper[:, :].unsqueeze(1).to_broadcast([P, 4, P]), ALU.mult).then_inc(prm_ready.sem, 1)
                norm_rows(0)
                norm_lo(l, 0, [(hT_lo, hT_hi, prm, R_N1)])
                take(0, zr[:, 1, 0, :])
                take(1, zr[:, 1, 1, :])
                dve.wait_ge(*z_a(l, taken("A", 1)))
                dve.wait_ge(*z_d(l, taken("D", 1)))
                for s in range(NT):
                    z = zr[:, s, 0:2, :].rearrange("p a (b c) -> p (a b) c", c=P)
                    o = h[:, s, :].rearrange("p (b c) -> p b c", c=P)
                    w = tmp[:, s, :].rearrange("p (b c) -> p b c", c=P)
                    c_t, s_t = const["rope_c"][:, s, :], const["rope_s"][:, s, :]

                    def over_heads(a):
                        return a.unsqueeze(1).to_broadcast([P, 8, a.shape[-1]])
                    v.tensor_tensor(o, z, over_heads(c_t), ALU.mult)
                    v.tensor_tensor(w[:, :, 0:64], z[:, :, 64:P], over_heads(s_t[:, 0:64]), ALU.mult)
                    ch.link(v.tensor_tensor(w[:, :, 64:P], z[:, :, 0:64], over_heads(s_t[:, 64:P]), ALU.mult))
                    ins = v.tensor_tensor(o, o, w, ALU.add)
                ins.then_inc(rot_ready.sem, 1)
                take(2, zr[:, 1, 2, :])
                for b in range(2, 4):
                    dve.wait_ge(*rqk_psum(l, b + 1))
                    ins = v.tensor_copy(kTt[:, b - 2, :], T[b][:, :])
                ins.then_inc(kT_ready.sem, 1)
                take(4, zc[:, 1, 0, :])
                for i in range(4):
                    dve.wait_ge(*rsc_psum(l, i + 1))
                    v.tensor_tensor(scr[:, i, :], T[i][:, 0:TRI], decay[:, i, :], ALU.mult).then_inc(rsc_ready.sem, 1)
                dve.wait_ge(*z_a(l, taken("A", 5)))
                dve.wait_ge(*z_d(l, taken("D", 4)))
                v.scalar_tensor_tensor(mix[:, :, 0:MIX], zc[:, :, 1, :], 1.0, zc[:, :, 0, :],
                                       ALU.add, ALU.mult).then_inc(cu_ready.sem, 1)
                dve.wait_ge(*ry_psum(l, 1))
                for s in range(NT):
                    for i in range(4):
                        ins = v.bn_stats(st[:, 4 * s + i, :], T[s][:, i * P:(i + 1) * P])
                ch.link(ins)
                for i in range(8):
                    ins = v.bn_aggr(mv[:, i, :], st[:, i, :])
                ins.then_inc(ry_stat.sem, 1)
                dve.wait_ge(*ry_rstd(l, 1))
                for s in range(NT):
                    for i in range(4):
                        j = 4 * s + i
                        ins = v.tensor_scalar(yr[:, s, i * P:(i + 1) * P], T[s][:, i * P:(i + 1) * P],
                                              mv[:, j, 0:1], rs8[:, j:j + 1], ALU.subtract, ALU.mult)
                ch.link(ins)
                dve.wait_ge(*z_a(l, taken("A", 3)))
                v.tensor_tensor(yr, yr, zr[:, :, 3, :], ALU.mult).then_inc(rya_ready.sem, 1)
                dve.wait_ge(*z_a(l, taken("A", 7)))
                for s in range(NT):
                    ins = v.bn_stats(st[:, s, :], zg[:, s, 1, :])
                ch.link(ins)
                for s in range(NT):
                    ins = v.bn_aggr(mv[:, s, :], st[:, s, :])
                ins.then_inc(gv_stat.sem, 1)
                dve.wait_ge(*gv_rstd(l, 1))
                for s in range(NT):
                    ins = v.tensor_scalar(tmp[:, s, 0:MIX], zg[:, s, 1, :], mv[:, s, 0:1], rs8[:, s:s + 1],
                                          ALU.subtract, ALU.mult)
                ch.link(ins)
                for s in range(NT):
                    ins = v.tensor_tensor(tmp[:, s, 0:MIX], tmp[:, s, 0:MIX], lng[:, :], ALU.mult)
                ch.link(ins)
                for s in range(NT):
                    ins = v.tensor_tensor(tmp[:, s, 0:MIX], tmp[:, s, 0:MIX], lnb[:, :], ALU.add)
                ins.then_inc(gv_ready.sem, 1)
                take(8, zs[:, 1, 0:512])
                dve.wait_ge(*ysT_hi_ready(l, 1))
                for c in range(4):
                    ins = v.scalar_tensor_tensor(ysT_lo[:, PLACE[0], c, :], T[c // 2][:, (c % 2) * SEQ:(c % 2 + 1) * SEQ],
                                                 prm[:, R_GN + c:R_GN + c + 1], ysT_hi[:, PLACE[0], c, :].bitcast(F32),
                                                 ALU.mult, ALU.subtract)
                ins.then_inc(ysT_ret.sem, 1)

                def ys_lo(b, banks, turn, done):
                    dve.wait_ge(*ysT_hi_ready(l, turn))
                    for j in range(2):
                        ins = v.tensor_tensor(ysT_lo[:, PLACE[b], 2 * j:2 * j + 2, :], pairs(banks[j]),
                                              ysT_hi[:, PLACE[b], 2 * j:2 * j + 2, :].bitcast(F32), ALU.subtract)
                    ins.then_inc(done.sem, 1)
                dve.wait_ge(*gs_psum(l, 1))
                for s in range(NT):
                    for c in range(4):
                        cols = slice(c * P, (c + 1) * P)
                        ins = v.scalar_tensor_tensor(yg[:, s, cols], T[2 + s][:, cols], prm[:, R_BS + c:R_BS + c + 1],
                                                     zg[:, s, 0, cols], ALU.add, ALU.mult)
                ins.then_inc(gy_ready.sem, 1)
                take(9, zs[:, 1, 512:768])
                dve.wait_ge(*z_a(l, taken("A", 9)))
                dve.wait_ge(*z_d(l, taken("D", 9)))
                dve.wait_ge(*gs_psum(l, 1))
                ch.link(v.tensor_tensor(tmp[:, :, 0:640], zs[:, :, 0:640], zs[:, :, 0:640], ALU.mult))
                for s in range(NT):
                    ins = v.tensor_reduce(ssw[:, s * 10:s * 10 + 10],
                                          tmp[:, s, 0:640].rearrange("p (a b) -> p a b", b=HD), AX.X, ALU.add)
                ins.then_inc(sw_sumsq.sem, 1)
                dve.wait_ge(*sw_rstd(l, 1))
                for s in range(NT):
                    r = rs8[:, s * 10:s * 10 + 10]
                    v.tensor_tensor(tmp[:, s, 0:512].rearrange("p (a b) -> p a b", b=HD),
                                    zs[:, s, 0:512].rearrange("p (a b) -> p a b", b=HD),
                                    r[:, 0:8].unsqueeze(2).to_broadcast([P, 8, HD]), ALU.mult)
                    for a in range(2):
                        ins = v.tensor_tensor(kdup[:, s, :].rearrange("p (g a b) -> p g a b", a=2, b=HD)[:, :, a, :],
                                              zs[:, s, 512:640].rearrange("p (a b) -> p a b", b=HD),
                                              r[:, 8:10].unsqueeze(2).to_broadcast([P, 2, HD]), ALU.mult)
                ins.then_inc(sw_norm.sem, 1)
                ys_lo(2, T[2:4], 2, ysT_gmlp)

                dve.wait_ge(*cuT_ready(l, 1))
                tap_mark = [0] * 4

                def gated(b, hf, q):
                    cols = slice(hf * 512, (hf + 1) * 512)
                    multiplied(end_of(q))
                    dve.wait_ge(*z_a(l, taken("A", P_GATE[b] + hf)))
                    first = b == BRANCH_ORDER[0]
                    for s in range(NT):
                        dst = mix if first else tmp
                        ins = v.scalar_tensor_tensor(dst[:, s, cols], gates[:, PLACE[b], s, cols], 1.0,
                                                     G[2 * (q % 2) + s][:, :], ALU.add, ALU.mult)
                    if not first:
                        ch.link(ins)
                        ins = v.tensor_tensor(mix[:, :, cols], mix[:, :, cols], tmp[:, :, cols], ALU.add)
                    ins.then_inc(z_d.sem, 1)

                def taps(k0, k1):
                    for k in range(k0, min(k1, 31)):
                        for c in range(4):
                            wk = cw[:, 4 * k + c:4 * k + c + 1]
                            u_k = uTp[:, c, k:k + SEQ]
                            if k == 0:
                                ins = v.tensor_scalar(cacc[:, c, :], u_k, wk, prm[:, R_CB + c:R_CB + c + 1],
                                                      ALU.mult, ALU.add)
                            else:
                                dve.wait_ge(ch.sem, tap_mark[c])
                                ins = v.scalar_tensor_tensor(cacc[:, c, :], u_k, wk, cacc[:, c, :], ALU.mult, ALU.add)
                            tap_mark[c] = ch.mark(ins)

                for u, (kind, b, hf, a, q) in enumerate(MIX_STEPS):
                    w = u - WINDOW_AT
                    if kind == "branch":
                        gated(b, hf, q)
                    if w == 0:
                        dve.wait_ge(*sw_psum(l, 1))
                        for j in range(2):
                            ins = v.tensor_scalar(swq[:, 2 * j:2 * j + 2, :],
                                                  T[j][:, :].rearrange("p (c s) -> p c s", c=2),
                                                  prm[:, R_QG:R_QG + 1], HD ** -0.5, ALU.mult, ALU.mult)
                        ins.then_inc(sw_qT.sem, 1)
                    if 1 <= w <= 8:
                        i = w - 1
                        if i == 0:
                            dve.wait_ge(bias_in, 32)
                        if i >= 4:
                            dve.wait_ge(*sw_tr(l, i - 3))
                        dve.wait_ge(*sw_sc(l, i + 1))
                        dve.sem_inc(hold_d, 1)
                        for s, cols in enumerate((slice(0, P), slice(P, TRI))):
                            near = bias[:, i, P:SEQ] if s == 0 else bias[:, i, :]
                            ins = v.tensor_tensor_reduce(out=S[:, i % 4, cols], in0=T[0][:, cols], in1=near,
                                                         scale=1.0, scalar=sinks[:, i:i + 1], op0=ALU.add, op1=ALU.max,
                                                         accum_out=mx[:, i, s:s + 1])
                        ch.link(ins)
                        v.tensor_scalar(nm[:, i, :], mx[:, i, :], -1.0, None, ALU.mult).then_inc(sw_nm.sem, 1)
                    if w == 10:
                        ch.link(v.tensor_tensor(es[:, 0:8, :], nm[:, 0:8, :],
                                                sinks[:, :].unsqueeze(2).to_broadcast([P, 8, 2]), ALU.add))
                        dve.sem_inc(sw_sink.sem, 1)
                    if u < 16:
                        taps(2 * u, 2 * u + 2)
                    if w == 11:
                        dve.wait_ge(*sw_exp(l, 8))
                        dve.wait_ge(*sw_esink(l, 1))
                        ch.link(v.tensor_tensor(rsum[:, 0:8, :], rsum[:, 0:8, :], es[:, 0:8, :], ALU.add))
                        ch.link(v.reciprocal(rsum[:, 0:8, :], rsum[:, 0:8, :]))
                        dve.wait_ge(*sw_o(l, 8))
                        for s in range(NT):
                            ins = v.tensor_tensor(h[:, s, 0:MIX].rearrange("p (a b) -> p a b", b=HD),
                                                  T[2 + s][:, :].rearrange("p (a b) -> p a b", b=HD),
                                                  rsum[:, 0:8, s:s + 1].to_broadcast([P, 8, HD]), ALU.mult)
                        ins.then_inc(sy_ready.sem, 1)
                    if w == 12:
                        ys_lo(3, T[0:2], 3, ysT_swa)
                    if u == 15:
                        dve.wait_ge(ch.sem, ch.n)
                        dve.sem_inc(cv_ready.sem, 1)
                    if u == 16:
                        dve.wait_ge(*cv_psum(l, 1))
                        for s in range(NT):
                            ins = v.bn_stats(st[:, s, :], T[2 + s][:, :])
                        ch.link(ins)
                        for s in range(NT):
                            ins = v.bn_aggr(mv[:, s, :], st[:, s, :])
                        ins.then_inc(cv_stat.sem, 1)
                        dve.wait_ge(*cv_rstd(l, 1))
                        for s in range(NT):
                            ins = v.tensor_scalar(h[:, s, MIX:2 * MIX], T[2 + s][:, :], mv[:, s, 0:1], rs8[:, s:s + 1],
                                                  ALU.subtract, ALU.mult)
                        ins.then_inc(cn_ready.sem, 1)

                    if u == 19:
                        dve.wait_ge(*cs_ready(l, 1))
                        hi = ysT_hi[:, PLACE[1], :, :]
                        ch.link(v.tensor_copy(hi, cacc))
                        v.tensor_tensor(ysT_lo[:, PLACE[1], :, :], cacc, hi.bitcast(F32), ALU.subtract
                                        ).then_inc(ysT_conv.sem, 1)
                for b in range(4):
                    dve.wait_ge(*mixT_a(l, b + 1))
                    part = slice(2 * b, 2 * b + 2)
                    v.scalar_tensor_tensor(hT_lo[:, part, :], pairs(T[b]), 0.5, hT_hi[:, part, :].bitcast(F32),
                                           ALU.mult, ALU.subtract).then_inc(mixT_d.sem, 1)
                for hf in range(2):
                    q = P_OUT + hf
                    cols = slice(hf * 512, (hf + 1) * 512)
                    if hf == 0:
                        multiplied(end_of(q))
                    for s in range(NT):
                        if hf:
                            if s:
                                multiplied(end_of(q))
                            else:
                                dve.wait_ge(*tile_done(l, 1))
                        ins = v.tensor_tensor(x[:, s, cols], x[:, s, cols], G[2 * (q % 2) + s][:, :], ALU.add)
                        if hf and not s:
                            ins.then_inc(x_new.sem, 1)
                    ins.then_inc(z_d.sem, 1)
                dve.wait_ge(*z_d(l, taken("D", P_OUT + 1)))
                dve.sem_inc(x_new.sem, 1)
                norm_rows(1)
                norm_lo(l, 1, [(hT_lo, hT_hi, prm, R_N2)])

                def ff_hidden(parity, done, j):
                    dve.wait_ge(ff_sg.sem, done)
                    u, tiles = uu[:, parity, :], bass.ds(j * 2, 2)
                    ins = v.tensor_tensor(u, sg[:, parity, :], G[2 * parity + 1][:, :], ALU.mult)
                    ins.then_inc(ff_u.sem, 1)
                    dve.wait_ge(ff_u.sem, done)
                    ch.link(v.tensor_copy(uT_hi[:, tiles, :], pairs(u)))
                    v.tensor_tensor(uT_lo[:, tiles, :], pairs(u), uT_hi[:, tiles, :].bitcast(F32),
                                    ALU.subtract).then_inc(ff_uT.sem, 1)

                before = l * FF_PANELS + AHEAD
                ch.restart()
                units = l * L_UNITS
                split_lo(U_FF + 3, units + (U_FF + 3))
                ff_hidden(0, before + 1, 0)
                ch.restart()
                with dve.Fori(0, FF_PANELS // 2) as i:
                    split_lo(U_FF + 5, units + i * 4 + (U_FF + 5))
                    ff_hidden(1, before + i * 2 + 2, i * 2 + 1)
                    split_lo(U_FF + 7, units + i * 4 + (U_FF + 7))
                    ff_hidden(0, before + i * 2 + 3, i * 2 + 2)
                    ch.restart()
                split_lo(U_FF + 25, units + (U_FF + 25))
                for s in range(NT):
                    if s:
                        multiplied(L_UNITS)
                    else:
                        dve.wait_ge(*tile_done(l, 2))
                    for hf in range(2):
                        cols = slice(hf * 512, (hf + 1) * 512)
                        ins = v.tensor_tensor(x[:, s, cols], x[:, s, cols], T[2 * s + hf][:, :], ALU.add)
                    ins.then_inc(x_new.sem, 1)
                ch.restart()

            def norm_rows2(k, src=x):
                for s in range(NT):
                    dve.wait_ge(*rstd_ready(DEPTH, NT * k + s + 1))
                    v.tensor_scalar(h[:, s, :], src[:, s, :], rstd[:, s:s + 1], None, ALU.mult).then_inc(h_ready.sem, 1)

            def norm_T2(k, outs):
                for c in range(4, 8):
                    dve.wait_ge(*hT_psum(DEPTH, 4 * k + c // 2 + 1))
                    for dst, row in outs:
                        ins = v.tensor_scalar(dst[:, c, :], T[c // 2][:, (c % 2) * SEQ:(c % 2 + 1) * SEQ],
                                              prm2[:, row + c:row + c + 1], None, ALU.mult)
                ins.then_inc(memT_d, 1)

            def take2(q, dst):
                dve.wait_ge(*unit_done(DEPTH, SLOTS + U2_PANEL[q] + 2))
                v.tensor_copy(dst, G[2 * (q % 2) + 1][:, 0:dst.shape[-1]]).then_inc(z2_d, 1)

            def rotate(dst, src, w, c_t, s_t, heads, rows_=P):
                def over(a):
                    return a.unsqueeze(1).to_broadcast([rows_, heads, a.shape[-1]])
                v.tensor_tensor(dst, src, over(c_t), ALU.mult)
                v.tensor_tensor(w[:, :, 0:32], src[:, :, 32:HD], over(s_t[:, 0:32]), ALU.mult)
                ch.link(v.tensor_tensor(w[:, :, 32:HD], src[:, :, 0:32], over(s_t[:, 32:HD]), ALU.mult))
                return v.tensor_tensor(dst, dst, w, ALU.add)

            def combine(f, branch, at_first):
                heads = lambda a: a.rearrange("p (h c) -> p h c", c=HD)
                for s in range(NT):
                    for g2 in range(2):
                        o = heads(G[2 * s + g2][:, 0:6 * HD])
                        dst = heads(h[:, s, g2 * 384:(g2 + 1) * 384])
                        w = heads(tmp[:, s, g2 * 384:(g2 + 1) * 384])
                        cf = coef[:, 6 * g2:6 * g2 + 6, s:s + 1].to_broadcast([P, 6, HD])
                        ins = v.tensor_tensor(dst if at_first else w, o, cf, ALU.mult)
                if not at_first:
                    ch.link(ins)
                    ins = v.tensor_tensor(h[:, :, 0:MIX_W], h[:, :, 0:MIX_W], tmp[:, :, 0:MIX_W], ALU.add)
                ins.then_inc(at_sum, 1)

            def attention_d(f):
                jobs = [j for j, job in enumerate(JOBS) if job[0] == f]

                def maxima(j):
                    _, kind, i = JOBS[j]
                    bank, p = T[j % 2], S4[:, j % 4, :]
                    dve.wait_ge(at_sc, j + 1)
                    if kind == "mem":
                        ins = v.tensor_reduce(mx[:, i, :], bank[:, :].rearrange("p (t c) -> p t c", t=NT), AX.X, ALU.max)
                    elif kind == "fgt":
                        for s, cols in enumerate((slice(0, P), slice(P, TRI))):
                            ins = v.scalar_tensor_tensor(p[:, cols], bank[:, cols], dcum[:, s, i:i + 1],
                                                         c2["causal"][:, cols], ALU.add, ALU.add)
                        ch.link(ins)
                        for s, cols in enumerate((slice(0, P), slice(P, TRI))):
                            ins = v.tensor_reduce(mx[:, i, s:s + 1], p[:, cols], AX.X, ALU.max)
                    else:
                        for s, cols in enumerate((slice(0, P), slice(P, TRI))):
                            ins = v.tensor_tensor_reduce(out=p[:, cols], in0=bank[:, cols], in1=c2["causal"][:, cols],
                                                         scale=1.0, scalar=-3e38, op0=ALU.add, op1=ALU.max,
                                                         accum_out=mx[:, i, s:s + 1])
                    ch.link(ins)
                    v.tensor_scalar(nm[:, i, :], mx[:, i, :], -1.0, None, ALU.mult).then_inc(at_nm, 1)

                def probs(j):
                    dve.wait_ge(at_tr, j + 1)
                    if j >= 2:
                        dve.wait_ge(at_o, j)
                    n = 512 if JOBS[j][1] == "mem" else TRI
                    v.tensor_copy(pT4[:, j % 2, 0:n], T[2 + j % 2][:, 0:n]).then_inc(at_pT, 1)

                def finish(j):
                    _, kind, _ = JOBS[j]
                    dve.wait_ge(at_exp, j + 1)
                    n = N_MEM_H if kind == "mem" else N_MIX
                    ch.link(v.reciprocal(coef[:, 0:n, :], rsums[:, groups_before(j) % 2, 0:n, :]))
                    if kind in ("slc", "win"):
                        br = 1 if kind == "slc" else 2
                        ch.link(v.tensor_tensor(coef[:, :, :], coef[:, :, :],
                                                gsig[:, :, :, br].rearrange("p t h -> p h t"), ALU.mult))
                    dve.wait_ge(at_o, j + 2)
                    if kind != "mem":
                        combine(f, kind, kind == "fgt")
                        return
                    for s in range(NT):
                        ins = v.tensor_tensor(h[:, s, MIX_W:D_MODEL].rearrange("p (h c) -> p h c", c=HD),
                                              G[2 * s][:, 0:256].rearrange("p (h c) -> p h c", c=HD),
                                              coef[:, 0:N_MEM_H, s:s + 1].to_broadcast([P, N_MEM_H, HD]), ALU.mult)
                    ins.then_inc(at_sum, 1)

                for step in range(len(jobs) + 2):
                    if step < len(jobs):
                        maxima(jobs[step])
                    if 1 <= step <= len(jobs):
                        probs(jobs[step - 1])
                    if step >= 2 and jobs[step - 2] in LAST:
                        finish(jobs[step - 2])

            def out_and_ffn_d(f):
                for b in range(4):
                    dve.wait_ge(oT_a, 4 * f + b + 1)
                    part = slice(2 * b, 2 * b + 2)
                    v.tensor_tensor(hT_lo[:, part, :], pairs(T[b]), hT_hi[:, part, :].bitcast(F32),
                                    ALU.subtract).then_inc(oT_d, 1)
                for hf in range(2):
                    q = Q_OUT[f] + hf
                    cols = slice(hf * 512, (hf + 1) * 512)
                    for s in range(NT):
                        if hf and not s:
                            dve.wait_ge(*tile_done(DEPTH, 2 * f + 1))
                        else:
                            dve.wait_ge(*unit_done(DEPTH, SLOTS + U2_PANEL[q] + 2))
                        ins = v.tensor_tensor(x[:, s, cols], x[:, s, cols], G[2 * (q % 2) + s][:, :], ALU.add)
                        if hf and not s:
                            ins.then_inc(x_new.sem, 1)
                    ins.then_inc(z2_d, 1)
                dve.wait_ge(z2_d, taken2("D", Q_OUT[f] + 1))
                dve.sem_inc(x_new.sem, 1)
                norm_rows2(NORM_FFN[f])
                norm_lo(DEPTH, 1 + 2 * f, [(hT_lo, hT_hi, prm2, N2_FFN + 8 * f)])
                done = f * FF_PANELS
                units = DEPTH * L_UNITS + SLOTS + U2_UP[f]

                def conv(j, parity):
                    ch.restart()
                    mark = [0] * 4
                    for k in (1, 0):
                        for a in range(4):
                            b, c = a // 2, a % 2
                            if k == 1 and c == 0:
                                dve.wait_ge(cf_tap, 2 * done + j * 2 + 1 + b)
                            if k == 0:
                                dve.wait_ge(ch.sem, mark[a])
                            d = 2 - k
                            tile = 22 * b + j * 2 + c
                            acc = accv[:, parity, a, d:SEQ]
                            ins = v.scalar_tensor_tensor(acc, G[2 * parity + b][:, c * SEQ:(c + 1) * SEQ - d],
                                                         cvp[:, f, k, bass.ds(tile, 1)], acc, ALU.mult, ALU.add)
                            mark[a] = ch.mark(ins)
                    dve.wait_ge(ch.sem, ch.n)
                    dve.sem_inc(cf_cv, 1)

                def hidden(j, parity):
                    dve.wait_ge(cf_silu, done + j + 1)
                    u, hi = accv[:, parity, 0:2, :], uT_hi[:, bass.ds(j * 2, 2), :]
                    ch.link(v.tensor_tensor(u, u, accv[:, parity, 2:4, :], ALU.mult))
                    ch.link(v.tensor_copy(hi, u))
                    v.tensor_tensor(uT_lo[:, bass.ds(j * 2, 2), :], u, hi.bitcast(F32), ALU.subtract).then_inc(cf_uT, 1)

                n = U2_UP[f]
                before = DEPTH * L_UNITS + split_before(n)
                split_lo(n + 3, before + 3)
                conv(0, 0)
                ch.restart()
                with dve.Fori(0, FF_PANELS // 2) as i:
                    split_lo(n + 5, i * 4 + (before + 5))
                    conv(i * 2 + 1, 1)
                    hidden(i * 2, 0)
                    split_lo(n + 7, i * 4 + (before + 7))
                    conv(i * 2 + 2, 0)
                    hidden(i * 2 + 1, 1)
                    ch.restart()
                hidden(FF_PANELS - 1, 0)
                split_lo(n + 25, before + 25)
                for s in range(NT):
                    if s:
                        dve.wait_ge(*unit_done(DEPTH, SLOTS + U2_DOWN[f] + FF_KT // 2))
                    else:
                        dve.wait_ge(*tile_done(DEPTH, 2 * f + 2))
                    for hf in range(2):
                        cols = slice(hf * 512, (hf + 1) * 512)
                        ins = v.tensor_tensor(x[:, s, cols], x[:, s, cols], T[2 * s + hf][:, :], ALU.add)
                    ins.then_inc(x_new.sem, 1)

            dve.wait_ge(prm2_psum, 1)
            v.tensor_copy(prm2[:, :], T[0][:, 0:N2_END])
            v.tensor_copy(cvp.rearrange("p f k r -> p (f k r)"), T[1][:, 0:352]).then_inc(prm2_ready, 1)
            norm_rows2(NORM_ATT[0])
            norm_lo(DEPTH, 0, [(hT_lo, hT_hi, prm2, N2_ATT)])
            norm_rows2(NORM_MEM, mem)
            for q in range(2):
                take2(q, z2[:, 1, 512 * q:512 * (q + 1)])
            norm_T2(NORM_MEM, [(memT[0], N2_MEM), (memT[1], N2_MEM + 8)])

            def doubled(dst, src):
                return v.tensor_copy(dst.rearrange("p (g a c) -> p g a c", a=2, c=HD),
                                     src.rearrange("p (g c) -> p g c", c=HD).unsqueeze(2).to_broadcast([P, 4, 2, HD]))
            dve.wait_ge(z2_a, taken2("A", 1))
            dve.wait_ge(z2_d, taken2("D", 1))
            for s in range(NT):
                ins = doubled(kvd[:, s, :], z2[:, s, MIX_W:MIX_W + 256])
            ins.then_inc(kvd_ready, 1)
            take2(2, z2[:, 1, 1024:1536])
            take2(3, z2[:, 1, 1536:A_IN])
            dve.wait_ge(cmpT_psum, 1)
            v.tensor_copy(u2[0:HD, 2:4, :], pairs(T[1])[0:HD])
            v.tensor_copy(u2[HD:P, 2:4, 0:SEQ - 1], pairs(T[1])[HD:P, :, 1:SEQ]).then_inc(u2_d, 1)
            dve.wait_ge(c2_in, 16 * (len(c2) + 5))
            dve.wait_ge(z2_a, taken2("A", 3))
            dve.wait_ge(z2_d, taken2("D", 3))
            for s in range(NT):
                for c0, c1, heads in ((0, 0, 12), (1024, 768, 2), (1280, 896, 2)):
                    src, dst, w = (a[:, s, c:c + heads * HD].rearrange("p (h c) -> p h c", c=HD)
                                   for a, c in ((z2, c0), (h, c1), (tmp, c1)))
                    ins = rotate(dst, src, w, c2["rope2_c"][:, s, :], c2["rope2_s"][:, s, :], heads)
            ch.link(ins)
            for s in range(NT):
                ins = doubled(kd2[:, s, :], h[:, s, MIX_W:D_MODEL])
            ins.then_inc(rot2, 1)
            ch.link(v.memset(tmp_flat, 0.0))
            dve.wait_ge(rot2, 1)
            dve.wait_ge(u2_a, 1)
            dve.wait_ge(u2_d, 1)
            for kv in range(2):
                for g2 in range(2):
                    base = u2[:, 2 * kv + g2, :]
                    src = bass.AP(base.tensor, base.offset, [base.ap[0], [2, 16], [16, N_CMP]])
                    pos = prm2[:, N2_POS + 16 * kv:N2_POS + 16 * (kv + 1)].unsqueeze(2).to_broadcast([P, 16, N_CMP])
                    ins = v.tensor_tensor(blocks[:, kv, :, g2, 0:N_CMP], src, pos, ALU.add)
            ins.then_inc(blocks_ready, 1)
            take2(Q_MEM, mkv[0][:, 1, :])
            take2(Q_MEM + 1, mkv[1][:, 1, :])
            for s in range(NT):
                ins = v.tensor_tensor(gsig[:, s, :, :].rearrange("p h b -> p (h b)"), z2[:, s, 1536:1572], gate_b, ALU.add)
            ins.then_inc(gate_in, 1)
            v.tensor_copy(upones[:, 0:P], upper[:, :])
            v.memset(upones[:, P:SEQ], 1.0)
            ch.link(v.memset(Sc[:, :, :, :], 0.0))
            dve.wait_ge(kvc_psum, 1)
            ch.link(v.tensor_tensor(kvc, T[3][:, 0:256].rearrange("p (v g c) -> p v g c", v=2, g=2),
                                    b2c.unsqueeze(2).to_broadcast([P, 2, 2, HD]), ALU.add))
            ch.link(rotate(kcr[0:N_CMP, :, 0:HD], kvc[0:N_CMP, 0], kct[0:N_CMP], c2["ropec_c"], c2["ropec_s"], 2, N_CMP))
            v.tensor_copy(kcr[0:N_CMP, :, HD:P], kcr[0:N_CMP, :, 0:HD]).then_inc(kcr_ready, 1)
            dve.wait_ge(kcT_psum, 1)
            v.tensor_copy(kcT[:, :, 0:N_CMP], T[3][:, 0:32].rearrange("p (g c) -> p g c", g=2)[:, :, 0:N_CMP]).then_inc(kcT_ready, 1)
            dve.wait_ge(turn_psum, 2)
            v.tensor_scalar(qT2[:, 4:6, :], pairs(T[2]), HD ** -0.5, None, ALU.mult).then_inc(turn_d, 1)
            dve.wait_ge(turn_psum, 4)
            v.tensor_copy(kT2[:, 2:4, :], pairs(T[3]))
            dve.wait_ge(turn_psum, 5)
            v.tensor_copy(mkT[0][:, :, :], pairs(T[2])).then_inc(turn_d, 1)
            dve.wait_ge(csc_psum, 1)
            scv = Sc[:, :, :, 0:N_CMP]
            for s in range(NT):
                for b in range(2):
                    ins = v.tensor_tensor(scv[:, s, b::2], T[b][:, s * 90:(s + 1) * 90].rearrange("p (h n) -> p h n", n=N_CMP),
                                          c2["cmp_neg"][:, s, :].unsqueeze(1).to_broadcast([P, 6, N_CMP]), ALU.add)
            ch.link(ins)
            ch.link(v.tensor_reduce(mxc, scv, AX.X, ALU.max))
            for s in range(NT):
                ins = v.tensor_tensor(scv[:, s], scv[:, s], mxc[:, s, :].unsqueeze(2).to_broadcast([P, N_MIX, N_CMP]), ALU.subtract)
            ins.then_inc(csc_ready, 1)
            dve.wait_ge(cexp, 1)
            for s in range(NT):
                ins = v.tensor_tensor(scv[:, s], scv[:, s], c2["cmp_ok"][:, s, :].unsqueeze(1).to_broadcast([P, N_MIX, N_CMP]), ALU.mult)
            ins.then_inc(cprob, 1)
            dve.wait_ge(cprob, 1)
            ch.link(v.tensor_reduce(smc, scv, AX.X, ALU.add))
            ch.link(v.tensor_scalar(smc, smc, 1e-30, None, ALU.max))
            ch.link(v.reciprocal(smc, smc))
            dve.wait_ge(gate_ready, 1)
            ch.link(v.tensor_tensor(coef, smc.rearrange("p t h -> p h t"), gsig[:, :, :, 0].rearrange("p t h -> p h t"), ALU.mult))
            dve.wait_ge(cprobT, 1)
            for s in range(NT):
                ins = v.tensor_copy(pcT[:, s, :, :], T[2 + s][:, 0:TRI].rearrange("p (a c) -> p a c", c=P))
            ins.then_inc(pcT_ready, 1)
            dve.wait_ge(at_o, 1)
            for s in range(NT):
                for b in range(4):
                    ins = v.tensor_tensor(h[:, s, 0:MIX_W].rearrange("p (a b c) -> p a b c", b=4, c=HD)[:, :, b, :],
                                          G[b][:, s * 192:(s + 1) * 192].rearrange("p (a c) -> p a c", c=HD),
                                          coef[:, b::4, s:s + 1].to_broadcast([P, 3, HD]), ALU.mult)
            ins.then_inc(at_sum, 1)
            attention_d(0)
            out_and_ffn_d(0)

            norm_rows2(NORM_ATT[1])
            norm_lo(DEPTH, 2, [(hT_lo, hT_hi, prm2, N2_ATT + 8), (hsT_lo, hsT_hi, prm2, N2_KV)])
            v.tensor_copy(upones[:, 0:P], upper[:, :])
            v.memset(upones[:, P:SEQ], 1.0)
            for q in range(4):
                take2(Q_SHARED + q, zk[:, 1, 512 * q:min(512 * (q + 1), SHARED)])
            dve.wait_ge(z2_a, taken2("A", Q_SHARED + 3))
            dve.wait_ge(z2_d, taken2("D", Q_SHARED + 3))
            ch.link(v.tensor_tensor(xf, zk[:, :, 2 * MIX_W:SHARED], f_b.unsqueeze(1).to_broadcast([P, NT, N_MIX]), ALU.add))
            ch.link(v.tensor_scalar(ef, xf, -1.0, None, ALU.mult))
            v.tensor_tensor(ef, ef, xf, ALU.min).then_inc(fg_in, 1)
            ch.link(v.tensor_scalar(xf, xf, 0.0, None, ALU.min))
            dve.wait_ge(fg_ln, 1)
            v.tensor_tensor(nlf, ef, xf, ALU.subtract).then_inc(fg_ready, 1)
            for q in range(2):
                take2(Q_IN + q, zq[:, 1, 512 * q:512 * (q + 1)])
            dve.wait_ge(turn_psum, 6)
            v.tensor_scalar(qT2[:, 4:6, :], pairs(T[2]), HD ** -0.5, None, ALU.mult)
            v.tensor_scalar(qmT[:, :, :], pairs(T[3]), HD ** -0.5, None, ALU.mult).then_inc(turn_d, 1)
            dve.wait_ge(fg_cum, 1)
            v.tensor_scalar(dcum, T[3][:, 0:2 * N_MIX].rearrange("p (t h) -> p t h", t=NT), -1.0, None, ALU.mult)
            v.tensor_copy(kT2[:, 4:6, :], pairs(T[2])).then_inc(turn_d, 1)
            attention_d(1)
            out_and_ffn_d(1)
            for s in range(NT):
                dve.wait_ge(*rstd_ready(DEPTH, NT * NORM_FINAL + s + 1))
                v.scalar_tensor_tensor(h[:, s, :], x[:, s, :], rstd[:, s:s + 1], final_g, ALU.mult, ALU.mult
                                       ).then_inc(h_ready.sem, 1)


def kernel(**inputs):
    import numpy as _np
    import concourse.bacc as _bacc
    from concourse.bass_utils import run_bass_kernel_spmd as _run

    nc = _bacc.Bacc("TRN2", target_bir_lowering=False, num_devices=1)
    arrays, t = {}, {}
    for name, a in list(inputs.items()) + list(constants().items()):
        a = _np.ascontiguousarray(a)
        arrays[f"in_{name}"] = a
        t[name] = nc.dram_tensor(f"in_{name}", a.shape, mybir.dt.from_np(a.dtype), kind="ExternalInput").ap()
    out = nc.dram_tensor("out", (1, SEQ, D_MODEL), F32, kind="ExternalOutput").ap()
    build(nc, t, out)
    r = _run(nc, [arrays], core_ids=[0])
    return r.results[0]["out"]
```
